# Optimizing a Trainium2 kernel written in Bass

```python
import math
import jax
import jax.numpy as jnp
from jax import lax
import numpy as np
import jax, jax.numpy as jnp

D_MODEL = 2048
BATCH = 1
SEQ = 256
DEPTH = 2

CTX_LEN = 256
GRID_W = 64
D_MIX = D_MODEL
ATT_WIDTH = D_MIX // 2
POOL_WIDTH = D_MIX // 4
CONV_WIDTH = D_MIX - ATT_WIDTH - POOL_WIDTH
ATT_HEADS = 8
ATT_HD = ATT_WIDTH // (2 * ATT_HEADS)
ATT_VD = 2 * ATT_HD
POOL_WINDOWS = (2, 4, 8, 16)
POOL_GROUPS = len(POOL_WINDOWS)
POOL_GD = POOL_WIDTH // POOL_GROUPS
CONV_K = 31
Q_BLOCK = 128
ROPE_BASE = 10000.0
EPS = 1e-6
SPLITS = (ATT_WIDTH, 2 * ATT_WIDTH, 3 * ATT_WIDTH, 4 * ATT_WIDTH,
          4 * ATT_WIDTH + POOL_WIDTH, 4 * ATT_WIDTH + 2 * POOL_WIDTH,
          4 * ATT_WIDTH + 2 * POOL_WIDTH + CONV_WIDTH,
          4 * ATT_WIDTH + 2 * POOL_WIDTH + 2 * CONV_WIDTH)
N_IN = 4 * ATT_WIDTH + 2 * POOL_WIDTH + 3 * CONV_WIDTH


def _rmsnorm(x, g):
    xf = x.astype(jnp.float32)
    y = xf * lax.rsqrt(jnp.mean(xf * xf, axis=-1, keepdims=True) + EPS)
    return (y * g.astype(jnp.float32)).astype(x.dtype)

def _layernorm(x, g, b):
    xf = x.astype(jnp.float32)
    mu = jnp.mean(xf, axis=-1, keepdims=True)
    var = jnp.mean(jnp.square(xf - mu), axis=-1, keepdims=True)
    y = (xf - mu) * lax.rsqrt(var + EPS) * g.astype(jnp.float32) + b.astype(jnp.float32)
    return y.astype(x.dtype)

def _heads_qk(t):
    return t.reshape(t.shape[0], t.shape[1], ATT_HEADS, 2, ATT_HD)

def _heads_v(t):
    return t.reshape(t.shape[0], t.shape[1], ATT_HEADS, ATT_VD)

def _axial_rope(t, row, col):
    n_freq = ATT_HD // 4
    inv_freq = ROPE_BASE ** (-jnp.arange(n_freq, dtype=jnp.float32) / n_freq)

    def rot(u, pos):
        ang = pos.astype(jnp.float32)[:, None] * inv_freq[None, :]
        cos = jnp.concatenate([jnp.cos(ang)] * 2, axis=-1)[None, :, None, None, :]
        sin = jnp.concatenate([jnp.sin(ang)] * 2, axis=-1)[None, :, None, None, :]
        u1, u2 = jnp.split(u, 2, axis=-1)
        rh = jnp.concatenate([-u2, u1], axis=-1)
        return (u.astype(jnp.float32) * cos + rh.astype(jnp.float32) * sin).astype(u.dtype)

    t_row, t_col = jnp.split(t, 2, axis=-1)
    return jnp.concatenate([rot(t_row, row), rot(t_col, col)], axis=-1)

def _diff_attention(q, k, v, lam):
    B, Lq = q.shape[0], q.shape[1]
    nb = Lq // Q_BLOCK
    qb = jnp.moveaxis(q.reshape(B, nb, Q_BLOCK, ATT_HEADS, 2, ATT_HD), 1, 0)
    scale = ATT_HD ** -0.5

    def block(qq):
        s = jnp.einsum('bqhcd,bkhcd->bhcqk', qq, k).astype(jnp.float32) * scale
        p = jax.nn.softmax(s, axis=-1)
        a = p[:, :, 0] - lam * p[:, :, 1]
        return jnp.einsum('bhqk,bkhe->bqhe', a.astype(v.dtype), v)

    o = lax.map(block, qb)
    return jnp.moveaxis(o, 0, 1).reshape(B, Lq, ATT_HEADS, ATT_VD)

def _multiscale_pool(u, w_pool, pool_scale):
    B, L, _ = u.shape
    ug = u.reshape(B, L, POOL_GROUPS, POOL_GD)
    cs = jnp.concatenate([jnp.zeros((B, 1, POOL_GROUPS, POOL_GD), jnp.float32),
                          jnp.cumsum(ug.astype(jnp.float32), axis=1)], axis=1)
    t = jnp.arange(L, dtype=jnp.int32)[:, None]
    halfw = jnp.array(POOL_WINDOWS, dtype=jnp.int32)[None, :] // 2
    lo = jnp.clip(t - halfw, 0, L)
    hi = jnp.clip(t + halfw, 0, L)
    gi = jnp.arange(POOL_GROUPS, dtype=jnp.int32)[None, :]
    win_sum = cs[:, hi, gi] - cs[:, lo, gi]
    mean = win_sum / (hi - lo).astype(jnp.float32)[None, :, :, None]
    d = (mean - ug.astype(jnp.float32)).astype(u.dtype)
    y = jnp.einsum('blgc,gcd->blgd', d, w_pool) * pool_scale.reshape(POOL_GROUPS, POOL_GD)
    return y.reshape(B, L, POOL_WIDTH)

def _conformer_conv(a, b, w_dw, b_dw, ln_g, ln_b, w_pw2):
    u = a * jax.nn.sigmoid(b)
    y = lax.conv_general_dilated(u, w_dw[:, None, :].astype(u.dtype), window_strides=(1,),
                                 padding=[(CONV_K // 2, CONV_K // 2)],
                                 dimension_numbers=('NWC', 'WIO', 'NWC'),
                                 feature_group_count=CONV_WIDTH) + b_dw
    y = jax.nn.silu(_layernorm(y, ln_g, ln_b))
    return y @ w_pw2

def _mix(q, k, v, g_att, u_pool, g_pool, a_conv, b_conv, g_conv, lam, lam_init,
         subln_g, w_pool, pool_scale, w_dw, b_dw, ln_g, ln_b, w_pw2, w_out):
    B, L = q.shape[0], q.shape[1]
    o = _diff_attention(q, k, v, lam)
    y_att = (_rmsnorm(o, subln_g) * (1.0 - lam_init)).reshape(B, L, ATT_WIDTH)
    y_pool = _multiscale_pool(u_pool, w_pool, pool_scale)
    y_conv = _conformer_conv(a_conv, b_conv, w_dw, b_dw, ln_g, ln_b, w_pw2)
    y = jnp.concatenate([y_att * jax.nn.silu(g_att),
                         y_pool * jax.nn.silu(g_pool),
                         y_conv * jax.nn.silu(g_conv)], axis=-1)
    return y @ w_out

def first_inputs(seed: int = 0) -> dict:
    key = jax.random.key(seed)
    ks = jax.random.split(key, 24)
    f32 = jnp.float32
    n = lambda k, s, sc: jax.random.normal(k, s, f32) * sc
    return {
        "x": n(ks[0], (BATCH, SEQ, D_MODEL), 1.0),
        "c": n(ks[1], (BATCH, D_MODEL), 1.0),
        "ctx": n(ks[2], (BATCH, CTX_LEN, D_MODEL), 1.0),
        "c_ctx": n(ks[3], (D_MODEL,), 1.0),
        "w_mod": n(ks[4], (DEPTH, D_MODEL, 3 * D_MODEL), 0.5 * D_MODEL ** -0.5),
        "b_mod": n(ks[5], (DEPTH, 3 * D_MODEL), 0.02),
        "norm_g": 1.0 + n(ks[6], (DEPTH, D_MODEL), 0.05),
        "w_in": n(ks[7], (DEPTH, D_MODEL, N_IN), D_MODEL ** -0.5),
        "lambda_q1": n(ks[8], (DEPTH, ATT_HD), 0.1),
        "lambda_k1": n(ks[9], (DEPTH, ATT_HD), 0.1),
        "lambda_q2": n(ks[10], (DEPTH, ATT_HD), 0.1),
        "lambda_k2": n(ks[11], (DEPTH, ATT_HD), 0.1),
        "subln_g": 1.0 + n(ks[12], (DEPTH, ATT_VD), 0.05),
        "w_pool": n(ks[13], (DEPTH, POOL_GROUPS, POOL_GD, POOL_GD), POOL_GD ** -0.5),
        "pool_scale": 1.0 + n(ks[14], (DEPTH, POOL_WIDTH), 0.05),
        "w_dw": n(ks[15], (DEPTH, CONV_K, CONV_WIDTH), CONV_K ** -0.5),
        "b_dw": n(ks[16], (DEPTH, CONV_WIDTH), 0.02),
        "conv_ln_g": 1.0 + n(ks[17], (DEPTH, CONV_WIDTH), 0.05),
        "conv_ln_b": n(ks[18], (DEPTH, CONV_WIDTH), 0.02),
        "w_pw2": n(ks[19], (DEPTH, CONV_WIDTH, CONV_WIDTH), CONV_WIDTH ** -0.5),
        "w_out": n(ks[20], (DEPTH, D_MIX, D_MODEL), D_MIX ** -0.5),
        "final_g": 1.0 + n(ks[21], (D_MODEL,), 0.05),
    }

def first_block(x, c, ctx, c_ctx, w_mod, b_mod, norm_g, w_in, lambda_q1, lambda_k1, lambda_q2, lambda_k2,
              subln_g, w_pool, pool_scale, w_dw, b_dw, conv_ln_g, conv_ln_b, w_pw2, w_out, final_g):
    B, L, _ = x.shape
    rows = L // GRID_W
    row = jnp.repeat(jnp.arange(rows, dtype=jnp.int32), GRID_W)
    col = jnp.tile(jnp.arange(GRID_W, dtype=jnp.int32), rows)
    s_lat = jax.nn.silu(c)
    s_ctx = jax.nn.silu(c_ctx)
    for l in range(DEPTH):
        last = l == DEPTH - 1
        lam_init = 0.8 - 0.6 * math.exp(-0.3 * l)
        lam = (jnp.exp(jnp.sum(lambda_q1[l].astype(jnp.float32) * lambda_k1[l].astype(jnp.float32)))
               - jnp.exp(jnp.sum(lambda_q2[l].astype(jnp.float32) * lambda_k2[l].astype(jnp.float32)))
               + lam_init)
        shift, scale, gate = jnp.split((s_lat @ w_mod[l] + b_mod[l])[:, None, :], 3, axis=-1)
        shift_c, scale_c, gate_c = jnp.split(s_ctx @ w_mod[l] + b_mod[l], 3, axis=-1)
        hx = _rmsnorm(x, norm_g[l]) * (1.0 + scale) + shift
        hc = _rmsnorm(ctx, norm_g[l]) * (1.0 + scale_c) + shift_c

        q, k, v, g_att, u_pool, g_pool, a_conv, b_conv, g_conv = jnp.split(hx @ w_in[l], SPLITS, axis=-1)
        q = _axial_rope(_heads_qk(q), row, col)
        k = _axial_rope(_heads_qk(k), row, col)
        v = _heads_v(v)
        if last:
            k_c, v_c = jnp.split(hc @ w_in[l][:, ATT_WIDTH:3 * ATT_WIDTH], 2, axis=-1)
        else:
            (q_c, k_c, v_c, g_att_c, u_pool_c, g_pool_c,
             a_conv_c, b_conv_c, g_conv_c) = jnp.split(hc @ w_in[l], SPLITS, axis=-1)
        k_c = _heads_qk(k_c)
        v_c = _heads_v(v_c)

        lw = (subln_g[l], w_pool[l], pool_scale[l], w_dw[l], b_dw[l],
              conv_ln_g[l], conv_ln_b[l], w_pw2[l], w_out[l])
        y = _mix(q, jnp.concatenate([k_c, k], axis=1), jnp.concatenate([v_c, v], axis=1),
                 g_att, u_pool, g_pool, a_conv, b_conv, g_conv, lam, lam_init, *lw)
        if not last:
            y_c = _mix(_heads_qk(q_c), k_c, v_c, g_att_c, u_pool_c, g_pool_c,
                       a_conv_c, b_conv_c, g_conv_c, lam, lam_init, *lw)
            ctx = ctx + gate_c * y_c
        x = x + gate * y
    return _rmsnorm(x, final_g)


DEPTH_2 = 1

HEAD_DIM = 128
N_ATTN_HEADS = 8
ATTN_WIDTH = N_ATTN_HEADS * HEAD_DIM
MOBA_BLOCK = 256
MOBA_TOPK = 3
Q_CHUNK = 32
ROPE_THETA = 10000.0
SSM_WIDTH = D_MODEL // 2
SSM_GROUP = 16
SSM_GROUPS = SSM_WIDTH // SSM_GROUP
SSM_STATE = 64
FFN_HIDDEN = 5632
CONV_WIDTH_2 = 3
N_BRANCHES = 2
N_MOD = 6
IN_WIDTH = 3 * ATTN_WIDTH + SSM_WIDTH + N_BRANCHES * D_MODEL
NEG_INF = -1e30


def rms_norm(x, g):
    xf = x.astype(jnp.float32)
    y = xf * lax.rsqrt(jnp.mean(xf * xf, axis=-1, keepdims=True) + EPS)
    return y.astype(x.dtype) * g

def rotary(x, positions):
    half = HEAD_DIM // 2
    inv_freq = ROPE_THETA ** (-jnp.arange(half, dtype=jnp.float32) / half)
    ang = positions.astype(jnp.float32)[..., None] * inv_freq
    cos = jnp.cos(ang)[:, :, None, :].astype(x.dtype)
    sin = jnp.sin(ang)[:, :, None, :].astype(x.dtype)
    x1, x2 = x[..., :half], x[..., half:]
    return jnp.concatenate([x1 * cos - x2 * sin, x1 * sin + x2 * cos], axis=-1)

def moba_attention(q, k, v):
    b, h, s, dh = q.shape
    n_blocks = -(-s // MOBA_BLOCK)
    s_pad = n_blocks * MOBA_BLOCK
    topk = min(MOBA_TOPK, n_blocks)
    pad = ((0, 0), (0, 0), (0, s_pad - s), (0, 0))
    k_p = jnp.pad(k, pad)
    v_p = jnp.pad(v, pad)
    k_blocks = k_p.reshape(b, h, n_blocks, MOBA_BLOCK, dh)
    v_blocks = v_p.reshape(b, h, n_blocks, MOBA_BLOCK, dh)
    k_mean = jnp.mean(k_blocks.astype(jnp.float32), axis=3).astype(k.dtype)
    scale = HEAD_DIM ** -0.5
    gather = jax.vmap(jax.vmap(lambda blocks, idx: blocks[idx]))

    def chunk(ci):
        start = ci * Q_CHUNK
        q_c = lax.dynamic_slice_in_dim(q, start, Q_CHUNK, axis=2)
        t = start + jnp.arange(Q_CHUNK)
        cur = start // MOBA_BLOCK
        blk_scores = jnp.einsum('bhqd,bhnd->bhqn', q_c, k_mean).astype(jnp.float32)
        past = jnp.arange(n_blocks) < cur
        blk_scores = jnp.where(past, blk_scores, NEG_INF)
        _, idx = lax.top_k(blk_scores, topk)
        slot_ok = jnp.arange(topk) < cur
        k_sel = gather(k_blocks, idx)
        v_sel = gather(v_blocks, idx)
        s_sel = jnp.einsum('bhqd,bhqnjd->bhqnj', q_c, k_sel).astype(jnp.float32) * scale
        s_sel = jnp.where(slot_ok[:, None], s_sel, NEG_INF).reshape(b, h, Q_CHUNK, topk * MOBA_BLOCK)
        k_own = lax.dynamic_slice_in_dim(k_p, cur * MOBA_BLOCK, MOBA_BLOCK, axis=2)
        v_own = lax.dynamic_slice_in_dim(v_p, cur * MOBA_BLOCK, MOBA_BLOCK, axis=2)
        s_own = jnp.einsum('bhqd,bhjd->bhqj', q_c, k_own).astype(jnp.float32) * scale
        key_pos = cur * MOBA_BLOCK + jnp.arange(MOBA_BLOCK)
        s_own = jnp.where(key_pos[None, :] <= t[:, None], s_own, NEG_INF)
        p = jax.nn.softmax(jnp.concatenate([s_sel, s_own], axis=-1), axis=-1).astype(v.dtype)
        p_sel = p[..., :topk * MOBA_BLOCK].reshape(b, h, Q_CHUNK, topk, MOBA_BLOCK)
        p_own = p[..., topk * MOBA_BLOCK:]
        return (jnp.einsum('bhqnj,bhqnjd->bhqd', p_sel, v_sel)
                + jnp.einsum('bhqj,bhjd->bhqd', p_own, v_own))

    out = lax.map(chunk, jnp.arange(s // Q_CHUNK))
    return out.transpose(1, 2, 0, 3, 4).reshape(b, h, s, dh)

def s5_branch(u, lam_re, lam_im, log_dt, b_re, b_im, c_re, c_im, d_skip, w_glu, b_glu):
    bsz, s, _ = u.shape
    f32 = jnp.float32
    ug = u.reshape(bsz, s, SSM_GROUPS, SSM_GROUP).astype(f32)
    dt = jnp.exp(log_dt.astype(f32))[:, None]
    lr = lam_re.astype(f32)
    li = lam_im.astype(f32)
    mag = jnp.exp(lr * dt)
    ab_re = mag * jnp.cos(li * dt)
    ab_im = mag * jnp.sin(li * dt)
    den = lr * lr + li * li
    nr = ab_re - 1.0
    ni = ab_im
    coef_re = (nr * lr + ni * li) / den
    coef_im = (ni * lr - nr * li) / den
    bu_re = jnp.einsum('bsgh,gph->bsgp', ug, b_re.astype(f32))
    bu_im = jnp.einsum('bsgh,gph->bsgp', ug, b_im.astype(f32))
    x_re0 = coef_re * bu_re - coef_im * bu_im
    x_im0 = coef_re * bu_im + coef_im * bu_re
    a_re = jnp.broadcast_to(ab_re, x_re0.shape)
    a_im = jnp.broadcast_to(ab_im, x_re0.shape)

    def combine(e1, e2):
        a1r, a1i, b1r, b1i = e1
        a2r, a2i, b2r, b2i = e2
        return (a2r * a1r - a2i * a1i, a2r * a1i + a2i * a1r,
                a2r * b1r - a2i * b1i + b2r, a2r * b1i + a2i * b1r + b2i)

    _, _, xr, xi = lax.associative_scan(combine, (a_re, a_im, x_re0, x_im0), axis=1)
    y = (jnp.einsum('bsgp,ghp->bsgh', xr, c_re.astype(f32))
         - jnp.einsum('bsgp,ghp->bsgh', xi, c_im.astype(f32))
         + d_skip.astype(f32).reshape(SSM_GROUPS, SSM_GROUP) * ug)
    y = jax.nn.gelu(y.reshape(bsz, s, SSM_WIDTH)).astype(u.dtype)
    return y * jax.nn.sigmoid(y @ w_glu + b_glu)

def causal_dwconv(u, w, bias):
    ch = u.shape[-1]
    y = lax.conv_general_dilated(u, w[:, None, :].astype(u.dtype), window_strides=(1,),
                                 padding=[(CONV_WIDTH_2 - 1, 0)],
                                 dimension_numbers=('NWC', 'WIO', 'NWC'),
                                 feature_group_count=ch)
    return y + bias

def second_inputs(seed: int = 0) -> dict:
    key = jax.random.key(seed)
    ks = jax.random.split(key, 32)
    nrm = jax.random.normal
    L = DEPTH_2
    x = nrm(ks[0], (BATCH, SEQ, D_MODEL), jnp.float32)
    c = nrm(ks[1], (BATCH, D_MODEL), jnp.float32)
    offsets = jax.random.randint(ks[2], (BATCH, 1), 0, 1024, dtype=jnp.int32)
    positions = offsets + jnp.arange(SEQ, dtype=jnp.int32)[None, :]
    w_mod = nrm(ks[3], (L, D_MODEL, N_MOD * D_MODEL), jnp.float32) * (0.5 * D_MODEL ** -0.5)
    b_mod = nrm(ks[4], (L, N_MOD * D_MODEL), jnp.float32) * 0.01
    norm1_g = 1.0 + 0.02 * nrm(ks[5], (L, D_MODEL), jnp.float32)
    w_in = nrm(ks[6], (L, D_MODEL, IN_WIDTH), jnp.float32) * D_MODEL ** -0.5
    q_norm_g = 1.0 + 0.02 * nrm(ks[7], (L, HEAD_DIM), jnp.float32)
    k_norm_g = 1.0 + 0.02 * nrm(ks[8], (L, HEAD_DIM), jnp.float32)
    n_idx = jnp.arange(SSM_STATE, dtype=jnp.float32)
    ssm_lambda_re = -0.5 + 0.01 * nrm(ks[9], (L, SSM_GROUPS, SSM_STATE), jnp.float32)
    ssm_lambda_im = math.pi * n_idx + 0.01 * nrm(ks[10], (L, SSM_GROUPS, SSM_STATE), jnp.float32)
    ssm_log_dt = jax.random.uniform(ks[11], (L, SSM_GROUPS), jnp.float32, math.log(1e-3), math.log(1e-1))
    b_scale = (2.0 * SSM_GROUP) ** -0.5
    ssm_b_re = nrm(ks[12], (L, SSM_GROUPS, SSM_STATE, SSM_GROUP), jnp.float32) * b_scale
    ssm_b_im = nrm(ks[13], (L, SSM_GROUPS, SSM_STATE, SSM_GROUP), jnp.float32) * b_scale
    c_scale = (2.0 * SSM_STATE) ** -0.5
    ssm_c_re = nrm(ks[14], (L, SSM_GROUPS, SSM_GROUP, SSM_STATE), jnp.float32) * c_scale
    ssm_c_im = nrm(ks[15], (L, SSM_GROUPS, SSM_GROUP, SSM_STATE), jnp.float32) * c_scale
    ssm_d = nrm(ks[16], (L, SSM_WIDTH), jnp.float32)
    w_glu = nrm(ks[17], (L, SSM_WIDTH, SSM_WIDTH), jnp.float32) * SSM_WIDTH ** -0.5
    b_glu = nrm(ks[18], (L, SSM_WIDTH), jnp.float32) * 0.01
    w_attn_br = nrm(ks[19], (L, ATTN_WIDTH, D_MODEL), jnp.float32) * ATTN_WIDTH ** -0.5
    w_ssm_br = nrm(ks[20], (L, SSM_WIDTH, D_MODEL), jnp.float32) * SSM_WIDTH ** -0.5
    w_out = nrm(ks[21], (L, D_MODEL, D_MODEL), jnp.float32) * D_MODEL ** -0.5
    norm2_g = 1.0 + 0.02 * nrm(ks[22], (L, D_MODEL), jnp.float32)
    w_up = nrm(ks[23], (L, D_MODEL, 2 * FFN_HIDDEN), jnp.float32) * D_MODEL ** -0.5
    conv_w = nrm(ks[24], (L, CONV_WIDTH_2, 2 * FFN_HIDDEN), jnp.float32) * CONV_WIDTH_2 ** -0.5
    conv_b = nrm(ks[25], (L, 2 * FFN_HIDDEN), jnp.float32) * 0.01
    w_down = nrm(ks[26], (L, FFN_HIDDEN, D_MODEL), jnp.float32) * FFN_HIDDEN ** -0.5
    return {'x': x, 'c': c, 'positions': positions, 'w_mod': w_mod, 'b_mod': b_mod,
            'norm1_g': norm1_g, 'w_in': w_in, 'q_norm_g': q_norm_g, 'k_norm_g': k_norm_g,
            'ssm_lambda_re': ssm_lambda_re, 'ssm_lambda_im': ssm_lambda_im, 'ssm_log_dt': ssm_log_dt,
            'ssm_b_re': ssm_b_re, 'ssm_b_im': ssm_b_im, 'ssm_c_re': ssm_c_re, 'ssm_c_im': ssm_c_im,
            'ssm_d': ssm_d, 'w_glu': w_glu, 'b_glu': b_glu, 'w_attn_br': w_attn_br,
            'w_ssm_br': w_ssm_br, 'w_out': w_out, 'norm2_g': norm2_g, 'w_up': w_up,
            'conv_w': conv_w, 'conv_b': conv_b, 'w_down': w_down}

def second_block(x, c, positions, w_mod, b_mod, norm1_g, w_in, q_norm_g, k_norm_g,
              ssm_lambda_re, ssm_lambda_im, ssm_log_dt, ssm_b_re, ssm_b_im, ssm_c_re, ssm_c_im,
              ssm_d, w_glu, b_glu, w_attn_br, w_ssm_br, w_out, norm2_g, w_up, conv_w, conv_b,
              w_down):
    bsz, s, _ = x.shape
    split_pts = [ATTN_WIDTH, 2 * ATTN_WIDTH, 3 * ATTN_WIDTH, 3 * ATTN_WIDTH + SSM_WIDTH]
    for l in range(DEPTH_2):
        mod = jax.nn.silu(c) @ w_mod[l] + b_mod[l]
        sh1, sc1, g1, sh2, sc2, g2 = jnp.split(mod, N_MOD, axis=-1)

        h = rms_norm(x, norm1_g[l]) * (1.0 + sc1[:, None]) + sh1[:, None]
        proj = h @ w_in[l]
        q, k, v, u, gates = jnp.split(proj, split_pts, axis=-1)
        q = rotary(rms_norm(q.reshape(bsz, s, N_ATTN_HEADS, HEAD_DIM), q_norm_g[l]), positions)
        k = rotary(rms_norm(k.reshape(bsz, s, N_ATTN_HEADS, HEAD_DIM), k_norm_g[l]), positions)
        v = v.reshape(bsz, s, N_ATTN_HEADS, HEAD_DIM)
        attn = moba_attention(q.transpose(0, 2, 1, 3), k.transpose(0, 2, 1, 3), v.transpose(0, 2, 1, 3))
        y_attn = attn.transpose(0, 2, 1, 3).reshape(bsz, s, ATTN_WIDTH)
        y_ssm = s5_branch(u, ssm_lambda_re[l], ssm_lambda_im[l], ssm_log_dt[l], ssm_b_re[l], ssm_b_im[l],
                          ssm_c_re[l], ssm_c_im[l], ssm_d[l], w_glu[l], b_glu[l])
        gate_a, gate_s = jnp.split(gates, N_BRANCHES, axis=-1)
        merged = (jax.nn.sigmoid(gate_a) * (y_attn @ w_attn_br[l])
                  + jax.nn.sigmoid(gate_s) * (y_ssm @ w_ssm_br[l]))
        x = x + g1[:, None] * (merged @ w_out[l])

        h2 = rms_norm(x, norm2_g[l]) * (1.0 + sc2[:, None]) + sh2[:, None]
        up = causal_dwconv(h2 @ w_up[l], conv_w[l], conv_b[l])
        val, gt = jnp.split(up, 2, axis=-1)
        x = x + g2[:, None] * ((jax.nn.silu(gt) * val) @ w_down[l])
    return x


def setup_inputs(seed=0):
    out = dict(first_inputs(seed))
    for name, value in second_inputs(seed + 1).items():
        if name != "x":
            out[name + "_2"] = value
    return out


def reference(
    x, c, ctx, c_ctx, w_mod, b_mod, norm_g, w_in, lambda_q1, lambda_k1, lambda_q2, lambda_k2,
    subln_g, w_pool, pool_scale, w_dw, b_dw, conv_ln_g, conv_ln_b, w_pw2, w_out, final_g, c_2,
    positions_2, w_mod_2, b_mod_2, norm1_g_2, w_in_2, q_norm_g_2, k_norm_g_2, ssm_lambda_re_2,
    ssm_lambda_im_2, ssm_log_dt_2, ssm_b_re_2, ssm_b_im_2, ssm_c_re_2, ssm_c_im_2, ssm_d_2,
    w_glu_2, b_glu_2, w_attn_br_2, w_ssm_br_2, w_out_2, norm2_g_2, w_up_2, conv_w_2, conv_b_2,
    w_down_2,
):
    x = first_block(
        x, c, ctx, c_ctx, w_mod, b_mod, norm_g, w_in, lambda_q1, lambda_k1, lambda_q2,
        lambda_k2, subln_g, w_pool, pool_scale, w_dw, b_dw, conv_ln_g, conv_ln_b, w_pw2, w_out,
        final_g,
    )
    return second_block(
        x, c_2, positions_2, w_mod_2, b_mod_2, norm1_g_2, w_in_2, q_norm_g_2, k_norm_g_2,
        ssm_lambda_re_2, ssm_lambda_im_2, ssm_log_dt_2, ssm_b_re_2, ssm_b_im_2, ssm_c_re_2,
        ssm_c_im_2, ssm_d_2, w_glu_2, b_glu_2, w_attn_br_2, w_ssm_br_2, w_out_2, norm2_g_2,
        w_up_2, conv_w_2, conv_b_2, w_down_2,
    )


_drawn_inputs = setup_inputs


def setup_inputs(seed=0):
    import zlib

    import numpy as np

    out = dict(_drawn_inputs(seed))
    spreads = {}
    factors = {'b_mod': 2.831,
     'norm_g': 3.64,
     'lambda_q1': 8.0,
     'lambda_k1': 8.0,
     'lambda_q2': 8.0,
     'lambda_k2': 8.0,
     'subln_g': 8.0,
     'pool_scale': 8.0,
     'b_dw': 8.0,
     'conv_ln_g': 8.0,
     'conv_ln_b': 8.0,
     'b_mod_2': 6.239,
     'norm1_g_2': 8.0,
     'q_norm_g_2': 8.0,
     'k_norm_g_2': 8.0,
     'ssm_lambda_re_2': 64.0,
     'ssm_lambda_im_2': 64.0,
     'ssm_log_dt_2': 64.0,
     'ssm_b_re_2': 64.0,
     'ssm_b_im_2': 64.0,
     'ssm_c_re_2': 64.0,
     'ssm_c_im_2': 64.0,
     'b_glu_2': 64.0,
     'norm2_g_2': 8.0,
     'conv_b_2': 33.16}
    for name, (base, spread) in spreads.items():
        noise = np.random.default_rng([zlib.crc32(name.encode()), seed]).standard_normal(out[name].shape)
        drawn = base * np.exp(spread * noise) if base else spread * noise
        out[name] = jnp.asarray(drawn.astype(out[name].dtype))
    for name, factor in factors.items():
        out[name] = (out[name] * factor).astype(out[name].dtype)
    return out
```

```python
import math
from contextlib import ExitStack

import numpy as np
import concourse.bass as bass
from concourse import mybir

P = 128
D = 2048
KT = D // P
T = 256
T2 = 2 * T
EPS = 1e-6
KB = 256
UNIT = 16 * P

A0_, B0_, UP_, GP_, GC_, Q_, K_, V_, GA_ = 0, 4, 8, 12, 16, 20, 28, 36, 44
IN_TILES = 52
SPECIAL = 2
FFN = 44

VEC = {}
_at = 0
for _name, _cols in [
    ("cvec", 48), ("b_mod", 192), ("norm_g", 32), ("subln_g", 2), ("pool_scale", 8), ("b_dw", 8), ("ln_g", 8),
    ("ln_b", 8), ("w_dw", 2 * 4 * 31), ("lam", 8), ("final_g", 16), ("norm1_g", 16), ("q_g", 1), ("k_g", 1),
    ("b_glu", 8), ("norm2_g", 16), ("d_skip", 8), ("conv_b", 88), ("conv_w", 88 * 3),
    ("lam_re", 64), ("lam_im", 64), ("log_dt", 64), ("inv_freq", 1), ("half0", 1), ("half1", 1), ("sign2pi", 1),
    ("eps", 1), ("half_pi", 1),
]:
    VEC[_name] = (_at, _cols)
    _at += _cols
NVEC = _at


def feature_columns(v):
    return v.reshape(-1, P).T


def tiles_of(w):
    kt, nt = w.shape[0] // P, w.shape[1] // P
    return w.reshape(kt, P, nt, P).transpose(2, 1, 0, 3).reshape(nt, P, kt * P)


def pairs_of(w):
    kt, nt = w.shape[0] // P, w.shape[1] // P
    return w.reshape(kt, P, nt // 2, 2, P).transpose(2, 1, 3, 0, 4).reshape(nt // 2, P, 2 * kt * P)


def lay_out(a):
    out = {}
    f = np.float32
    out["xin"] = np.stack([a["ctx"][0].T.reshape(KT, P, T), a["x"][0].T.reshape(KT, P, T)], 2) \
        .transpose(1, 0, 2, 3).reshape(P, KT * T2)
    order = [range(40, 44), range(44, 48), range(32, 36), range(36, 40), range(48, 52),
             range(0, 8), range(8, 16), range(16, 24), range(24, 32)]
    order = [n for r in order for n in r]
    for l in range(2):
        out[f"w_in{l}"] = tiles_of(a["w_in"][l])[order]
        out[f"w_out{l}"] = tiles_of(a["w_out"][l])
        small = np.zeros((SPECIAL, P, UNIT), f)
        small[0, :, :4 * P] = a["w_pool"][l].transpose(1, 0, 2).reshape(P, 4 * P)
        small[1] = a["w_pw2"][l].reshape(4, P, 4, P).transpose(1, 2, 0, 3).reshape(P, UNIT)
        out[f"w_small{l}"] = small
    out["w_mods"] = np.concatenate([tiles_of(a["w_mod"][0]), tiles_of(a["w_mod"][1]), tiles_of(a["w_mod_2"][0])])
    order2 = list(range(24, 32)) + list(range(24)) + list(range(32, 64))
    out["w_in2"] = tiles_of(a["w_in_2"][0])[order2]
    out["w_glu"] = pairs_of(a["w_glu_2"][0])
    out["w_abr"] = pairs_of(a["w_attn_br_2"][0])
    out["w_sbr"] = pairs_of(a["w_ssm_br_2"][0])
    out["w_out2"] = tiles_of(a["w_out_2"][0])
    up = tiles_of(a["w_up_2"][0])
    out["w_up"] = np.stack([up[:FFN], up[FFN:]], 1).reshape(2 * FFN, P, UNIT)
    down = a["w_down_2"][0].reshape(FFN, P, KT, P).transpose(2, 1, 0, 3)
    down = np.concatenate([down, np.zeros((KT, P, 48 - FFN, P), f)], 2)
    out["w_down"] = down.reshape(KT, P, 3, UNIT).transpose(0, 2, 1, 3).reshape(3 * KT, P, UNIT)

    vec = np.zeros((P, NVEC), f)

    def put(name, v):
        at, n = VEC[name]
        vec[:v.shape[0], at:at + n] = v

    put("cvec", np.stack([feature_columns(v) for v in (a["c"][0], a["c_ctx"], a["c_2"][0])], 2).reshape(P, 48))
    put("b_mod", np.concatenate([feature_columns(v) for v in (a["b_mod"][0], a["b_mod"][1], a["b_mod_2"][0])], 1))
    for name, key in [("norm_g", "norm_g"), ("subln_g", "subln_g"), ("pool_scale", "pool_scale"), ("b_dw", "b_dw"),
                      ("ln_g", "conv_ln_g"), ("ln_b", "conv_ln_b"), ("final_g", "final_g"), ("norm1_g", "norm1_g_2"),
                      ("q_g", "q_norm_g_2"), ("k_g", "k_norm_g_2"), ("b_glu", "b_glu_2"), ("norm2_g", "norm2_g_2"),
                      ("d_skip", "ssm_d_2")]:
        put(name, feature_columns(a[key]))
    put("w_dw", a["w_dw"].reshape(2, 31, 4, P).transpose(3, 0, 2, 1).reshape(P, -1))
    put("lam", np.stack([a["lambda_q1"], a["lambda_k1"], a["lambda_q2"], a["lambda_k2"]], 1).reshape(8, 64).T)
    pair = lambda v: feature_columns(v).reshape(P, 2, FFN).transpose(0, 2, 1)
    put("conv_b", pair(a["conv_b_2"][0]).reshape(P, -1))
    put("conv_w", np.stack([pair(a["conv_w_2"][0][i]) for i in range(3)], 3).reshape(P, -1))
    twice = lambda v: np.concatenate([v, v], 0)
    put("lam_re", twice(a["ssm_lambda_re_2"][0].T))
    put("lam_im", twice(a["ssm_lambda_im_2"][0].T))
    put("log_dt", np.broadcast_to(a["ssm_log_dt_2"], (P, 64)))
    half = np.arange(64, dtype=f)
    put("inv_freq", twice((f(10000.0) ** (-half / f(64))).astype(f)[:, None]))
    low = (np.arange(P) < 64)[:, None]
    put("half0", low.astype(f))
    put("half1", (~low).astype(f))
    put("sign2pi", np.where(low, 2 * math.pi, -2 * math.pi).astype(f))
    put("eps", np.full((P, 1), EPS, f))
    put("half_pi", np.full((P, 1), math.pi / 2, f))
    out["vec"] = vec
    out["positions"] = a["positions_2"]
    bre, bim = (a[k][0].transpose(0, 2, 1) for k in ("ssm_b_re_2", "ssm_b_im_2"))
    b = np.stack([np.concatenate([bre, bim], 2), np.concatenate([bim, bre], 2)], 2)
    bp = np.zeros((8, 4, 2, 16, 2, 2, P), f)
    b = b.reshape(8, 4, 2, 16, 2, P)
    for par in range(2):
        bp[:, :, par, :, par] = b[:, :, par]
    out["ssm_b"] = bp.reshape(8, P, 4 * P)
    c = np.stack([twice(a[k][0].transpose(2, 0, 1)) for k in ("ssm_c_re_2", "ssm_c_im_2")], 1)
    out["ssm_c"] = c.reshape(P, 2, 8, 8, 16).transpose(2, 0, 1, 3, 4).reshape(8, P, 256)

    eye = np.eye(P, dtype=f)
    rot1 = np.zeros((P, P), f)
    rot2 = np.zeros((P, P), f)
    for m in range(P):
        if m % 32 < 16:
            rot1[m + 16, m] = -1
        else:
            rot1[m - 16, m] = 1
        if m < 64:
            rot2[m + 64, m] = -1
        else:
            rot2[m - 64, m] = 1
    mask = np.where(np.arange(P)[None, :] <= np.arange(P)[:, None], 0.0, -1e30).astype(f)
    t = np.arange(T)
    freq = (f(10000.0) ** (-np.arange(16, dtype=f) / f(16))).astype(f)
    m = np.arange(P)
    pos = np.where(((m % 64) < 32)[:, None], (t // 64)[None, :], (t % 64)[None, :]).astype(f)
    ang = (pos * freq[m % 16][:, None]).astype(f)
    out["const"] = np.concatenate([eye, np.ones((P, P), f), rot1, rot2, mask, np.cos(ang), np.sin(ang)], 1).astype(f)
    cnt = np.stack([np.minimum(t + h, T) - np.maximum(t - h, 0) for h in (1, 2, 4, 8)])
    out["rcount"] = (f(1) / cnt.astype(f)).reshape(1, 4 * T)
    out["steps"] = t.astype(f).reshape(1, T)
    return out


ARRAYS = ["xin", "w_mods", "vec", "const", "rcount", "steps", "positions", "ssm_b", "ssm_c",
          "w_in0", "w_small0", "w_out0", "w_in1", "w_small1", "w_out1", "w_in2", "w_glu", "w_abr", "w_sbr",
          "w_out2", "w_up", "w_down"]
LAM_INIT = [0.8 - 0.6 * math.exp(-0.3 * l) for l in range(2)]


class Steps:

    def __init__(self, eng, sem):
        self.eng, self.sem, self.at, self.turn = eng, sem, 0, 0

    def mark(self, ins):
        ins.then_inc(self.sem, 1)
        self.at += 1

    def wait(self, back=0):
        self.eng.wait_ge(self.sem, self.at - back + self.turn)

    def loop(self, i, per_turn, start=0):
        self.turn, self.first, self.per_turn = (i - start) * per_turn, self.at, per_turn

    def end(self, turns):
        assert self.at - self.first == self.per_turn, (self.at - self.first, self.per_turn)
        self.at, self.turn = self.first + turns * self.per_turn, 0


def build(nc, dram, out):
    f32, f32r, i32 = mybir.dt.float32, mybir.dt.float32r, mybir.dt.int32
    ACT, ALU = mybir.ActivationFunctionType, mybir.AluOpType
    AX = mybir.AxisListType.X
    ctx = ExitStack()
    ds = bass.ds

    def at(kib, name, shape, dt=f32):
        if kib:
            with nc.sbuf_tensor(f"skip_{name}", [P, int(kib * KB)], f32):
                with nc.sbuf_tensor(name, shape, dt) as t:
                    return t
        with nc.sbuf_tensor(name, shape, dt) as t:
            return t

    MODW = at(0, "mod_weights", [P, 8, UNIT])
    HH = at(0, "h_high", [P, KT, T2], f32r)
    HL = at(32, "h_low", [P, KT, T2], f32r)
    WS = at(0, "attention_space", [P, 16384])
    H2H = at(0, "h2_high", [P, KT, T], f32r)
    H2L = at(16, "h2_low", [P, KT, T], f32r)
    WS2 = at(32, "second_space", [P, 8192])
    YAH = at(0, "y_attn_high", [P, 8, T], f32r)
    YAL = at(8, "y_attn_low", [P, 8, T], f32r)
    YSH = at(16, "y_ssm_high", [P, 8, T], f32r)
    YSL = at(24, "y_ssm_low", [P, 8, T], f32r)
    MH = at(32, "merged_high", [P, KT, T], f32r)
    ML = at(48, "merged_low", [P, KT, T], f32r)
    FH = at(32, "ffn_high", [P, FFN, T], f32r)
    FL = at(76, "ffn_low", [P, FFN, T], f32r)
    FT = at(120, "ffn_space", [P, 8, T])
    R2 = at(64, "region2", [P, 12288])
    GSH = at(72, "gelu_high", [P, 8, T], f32r)
    GSL = at(80, "gelu_low", [P, 8, T], f32r)
    R3 = at(112, "region3", [P, 8192])
    RAW = [at(144 + 8 * s, f"raw{s}", [P, UNIT]) for s in range(2)]
    WH = [at(160 + 8 * s, f"w_high{s}", [P, UNIT], f32r) for s in range(2)]
    WL = [at(176 + 8 * s, f"w_low{s}", [P, UNIT], f32r) for s in range(2)]
    o = 192 * KB
    small = {}
    for name, n in [("vec", NVEC), ("const", 9 * P), ("mod", 576), ("rcount", 4 * T), ("gain", 32), ("lam", 8),
                    ("mx", 4), ("nb", 4), ("sums", 4), ("rc", 4), ("ss", 8), ("rr", 8), ("sg", 2)]:
        small[name] = at(o / KB, name + "_sb", [P, n])
        o += -(-n // 8) * 8
    VE, CO, MODF, RCNT, GAIN, LAM = (small[n] for n in ("vec", "const", "mod", "rcount", "gain", "lam"))
    MX, NB, SM, RC, SS, RR, SG = (small[n] for n in ("mx", "nb", "sums", "rc", "ss", "rr", "sg"))
    MOD = MODF[:].rearrange("p (n c) -> p n c", c=3)
    IDENT, ONES, ROT1, ROT2, MASK = (CO[:, P * i:P * (i + 1)] for i in range(5))
    COS, SIN = CO[:, 5 * P:7 * P], CO[:, 7 * P:9 * P]
    XIN = R2[:, 0:8192].rearrange("p (k t) -> p k t", t=T2)
    NT_ = R2[:, 8192:12288].rearrange("p (n t) -> p n t", t=T2)
    CT0 = R3[:, 0:4096].rearrange("p (k t) -> p k t", t=T)
    RES = R3[:, 4096:8192].rearrange("p (k t) -> p k t", t=T)

    def vec(name, n=0, cols=1):
        return VE[:, VEC[name][0] + n:VEC[name][0] + n + cols]

    def vec_at(name, n):
        return VE[:, ds(VEC[name][0] + n, 1)]

    def tile(view, n):
        return view[:, ds(n, 1), :].rearrange("p a t -> p (a t)")

    BANK = [ctx.enter_context(nc.psum_tensor(f"bank{i}", [P, T2], f32)) for i in range(8)]
    L, AUX = BANK[:4], BANK[4:]

    _w, _at = {}, 0
    for _n, _c in [("BST", 512), ("CST", 256), ("WPAD", 2176), ("COEF", 384), ("STEPS", 256), ("PH", 512),
                   ("RN", 512), ("CT", 1024), ("ST", 1024), ("W", 512), ("TM", 512), ("US", 256), ("T12", 256)]:
        _w[_n] = WS2[:, _at:_at + _c]
        _at += _c
    assert _at <= 8192
    BST, CST, WPAD, COEF, STEPS, PH, RN, CTAB, STAB, SW, STM, US, T12 = _w.values()
    POSI = R3[:, 0:T].bitcast(i32)
    bst = BST.rearrange("p (r s n) -> p r s n", r=2, s=2)
    GATE_A = R2[:, 8192:12288].rearrange("p (n t) -> p n t", t=T)
    GATE_S = R3[:, 0:4096].rearrange("p (n t) -> p n t", t=T)
    U2, Q2, K2, V2 = (R2[:, 2048 * i:2048 * (i + 1)].rearrange("p (n t) -> p n t", t=T) for i in range(4))
    JOBS = [[(0, T), (1, T), (2, T2), (3, T2)], [(0, T2), (1, T2)]]
    JOBS2 = [(0, P), (1, T)]

    def att_views(l):
        f = lambda a, n: WS[:, a:a + n]
        two = lambda a: [f(a, T2), f(a + T2, T2)]
        QS, KS, VS, VT = two(0), two(1024), two(2048), two(3072)
        PP = [[f(4096 + 512 * (2 * b + c), T2) for c in range(2)] for b in range(2)]
        AA, AT = two(6144), two(7168)
        return QS, KS, VS, VT, PP, AA, AT, f(8192, T2), f(8704, T2), f(9216, T2)

    QKV2 = R2[:, 2048:8192].rearrange("p (n t) -> p n t", t=T)
    US8 = WS2[:, 3584:5632]

    def src_in0(k):
        return tile(XIN, k)

    def src_in1(k):
        v4 = R3[:].rearrange("p (s k t) -> p s k t", s=2, k=KT)
        return v4[:, :, ds(k, 1), :].rearrange("p s a t -> p s (a t)")

    def src_res(k):
        return tile(RES, k)

    def as_src(ap, src):
        return ap.rearrange("p (s t) -> p s t", s=2) if src is src_in1 else ap

    def att2_views():
        f = lambda a, n: WS2[:, a:a + n]
        two = lambda a, n: [f(a, n), f(a + n, n)]
        return dict(QS=two(0, T), KS=two(512, T), VS=two(1024, T), VT=two(1536, T), PP=two(2048, T), AT=two(2560, T),
                    SQ=f(3072, T2), VV=f(3584, T2), R0=f(4096, T2), TT=f(4608, T2), QN=f(5120, T2), SS_=two(5632, T),
                    SQ2=f(6144, T2))

    sems = {}

    def sem(name):
        if name not in sems:
            sems[name] = ctx.enter_context(nc.semaphore(name))
        return sems[name]

    raw_in = [sem("raw_in0"), sem("raw_in1")]
    high_ready = sem("high_ready")
    split_ready = sem("split_ready")
    units_done = sem("units_done")
    bank_free = [sem(f"bank_free{b}") for b in range(4)]

    STREAM = [("w_in0", 0, 36), ("w_small0", 0, 2), ("w_in0", 36, 16), ("w_out0", 0, 16),
              ("w_in1", 0, 36), ("w_small1", 0, 2), ("w_in1", 36, 16), ("w_out1", 0, 16),
              ("w_in2", 0, 64), ("w_glu", 0, 4), ("w_abr", 0, 8), ("w_sbr", 0, 8), ("w_out2", 0, 16),
              ("w_up", 0, 88), ("w_down", 0, 48)]
    UNITS = sum(n for _, _, n in STREAM)
    U_IN, U_SMALL, U_INB, U_OUT = [0, 70], [36, 106], [38, 108], [54, 124]
    U_IN2, U_GLU, U_ABR, U_SBR, U_OUT2, U_UP, U_DOWN = 140, 204, 208, 216, 224, 240, 328
    T_IN, T_OUT, T_IN2, T_GLU, T_ABR, T_SBR, T_OUT2, T_UP, T_DOWN = \
        [0, 68], [52, 120], 136, 200, 208, 224, 240, 256, 344
    assert UNITS == U_DOWN + 48

    def evacuated(eng, tiles):
        for b in range(4):
            eng.wait_ge(bank_free[b], 1 + tiles // 4)

    N_AT = {"in0": 0, "in1": 1, "fin": 2, "b1": 3, "b2": 4}
    S_AT = {"in0": 0, "in1": 1, "b1": 2, "b2": 3}

    def views(l):
        w = T2 if l == 0 else T
        split = lambda r, a, n, t: r[:, a:a + n * t].rearrange("p (n t) -> p n t", t=t)
        if l == 0:
            q, k, v = split(R2, 0, 8, T2), split(R2, 4096, 8, T2), split(R2, 8192, 8, T2)
            up, uc = split(R2, 8192, 4, T2), split(R2, 8192 + 4 * T2, 4, T2)
        else:
            k, v, q = split(R2, 0, 8, T2), split(R2, 4096, 8, T2), split(R2, 8192, 8, T)
            up, uc = split(R2, 4096, 4, T), split(R2, 4096 + 4 * T, 4, T)
        y = split(R3, 0, 16, w)
        return w, q, k, v, up, uc, y

    block = ctx.enter_context(nc.Block())

    @block.sync
    def _(sp):
        sp.dma_start(VE[:], dram["vec"]).then_inc(sem("vec_in"), 16)
        sp.dma_start(CO[:], dram["const"]).then_inc(sem("const_in"), 16)
        sp.dma_start(R2[:, 0:8192], dram["xin"]).then_inc(sem("x_in"), 16)
        sp.dma_start(RCNT[:], dram["rcount"].broadcast_to([P, 4 * T])).then_inc(sem("rcount_in"), 16)

        mods = dram["w_mods"].rearrange("(i s) p n -> i s p n", s=8)
        for s in range(8):
            sp.dma_start(MODW[:, s, :], mods[0, s]).then_inc(sem(f"mod_in{s}"), 16)
        with sp.Fori(1, 24) as i:
            for s in range(8):
                sp.wait_ge(sem("mod_used"), 8 * i + s - 7)
                sp.dma_start(MODW[:, s, :], mods[ds(i, 1), s].rearrange("a p n -> (a p) n")) \
                    .then_inc(sem(f"mod_in{s}"), 16)

        def stream(name, first, n, u0):
            w = dram[name].rearrange("(i s) p n -> i s p n", s=2)
            start = 0
            if u0 == 0:
                for s in range(2):
                    sp.dma_start(RAW[s][:], w[0, s]).then_inc(raw_in[s], 16)
                start = 1

            def two(i):
                for s in range(2):
                    sp.wait_ge(split_ready, u0 - 1 + 2 * i + s)
                    sp.dma_start(RAW[s][:], w[ds(first // 2 + i, 1), s].rearrange("a p n -> (a p) n")) \
                        .then_inc(raw_in[s], 16)
            with sp.Fori(start, n // 2) as i:
                two(i)

        u = 0
        for name, first, n in STREAM:
            if name == "w_in2":
                stream(name, 0, 8, u)
                w = dram["w_in2"].rearrange("(i s) p n -> i s p n", s=2)
                with sp.Fori(0, 7) as j:
                    for k in range(8):
                        s = k % 2
                        sp.wait_ge(split_ready, u + 7 + 8 * j + k)
                        sp.dma_start(RAW[s][:], w[ds(4 * j + 4 + k // 2, 1), s].rearrange("a p n -> (a p) n")) \
                            .then_inc(raw_in[s], 16)
                    sp.wait_ge(sem("ssm_b"), 1 + 4 * j + 4)
                    sp.dma_start(BST, dram["ssm_b"][ds(j + 1, 1)].rearrange("a p n -> (a p) n")).then_inc(sem("b_in"), 16)
                    sp.wait_ge(sem("ssm_w"), j + 1)
                    sp.dma_start(CST, dram["ssm_c"][ds(j + 1, 1)].rearrange("a p n -> (a p) n")).then_inc(sem("c_in"), 16)
            else:
                stream(name, first, n, u)
            u += n
        for c in range(4):
            for s in range(2):
                sp.wait_ge(bank_free[s], 1 + T_DOWN // 4 + 2 * (c + 1))
            sp.dma_start(out[:, 4 * c:4 * c + 4, :], RES[:, 4 * c:4 * c + 4, :]).then_inc(sem("stored"), 16)
        sp.wait_ge(sem("stored"), 64)

    @block.gpsimd
    def _(pool):
        with pool.Fori(0, UNITS // 2) as i:
            for s in range(2):
                pool.wait_ge(high_ready, 2 * i + s + 1)
                nc.gpsimd.tensor_tensor(WL[s][:], RAW[s][:], WH[s][:], ALU.subtract).then_inc(split_ready, 1)

    @block.tensor
    def _(pe):
        for n in [f"at{l}_{m}" for l in range(2) for m in ("pv", "ot")] + ["ssm_b", "ssm_c", "a2_ssum", "a2_pv"]:
            pe.sem_inc(sem(n), 1)
        pe.sem_inc(sem("n_squsd"), 2)
        pe.wait_ge(sem("s_ready"), 1)
        scol = vec("cvec", 0, 48)
        with pe.Fori(0, 24) as i:
            for s in range(8):
                pe.wait_ge(sem(f"mod_in{s}"), 16 * i + 16)
                pe.wait_ge(sem("mod_out"), 8 * i + s + 1)
                for k in range(KT):
                    last = nc.tensor.matmul(BANK[s][:, 0:3], MODW[:, s, P * k:P * (k + 1)],
                                            scol[:, 3 * k:3 * k + 3], start=k == 0, stop=k == KT - 1)
                last.then_inc(sem("mod_used"), 1)

        def norm(name, n):
            if name == "in0":
                pe.wait_ge(sem("mod_out"), 8 + 192)
            for k in range(KT):
                pe.wait_ge(sem("n_sq"), 16 * N_AT[name] + k + 1)
                nc.tensor.matmul(AUX[0][:, 0:n], ONES, NT_[:, k % 2, 0:n], start=k == 0, stop=k == KT - 1) \
                    .then_inc(sem("n_squsd"), 1)

        def product(bank, slot, blocks, k0, hi, lo, t0, n, first, last):
            for j, b in enumerate(blocks):
                h, l = (r[:, k0 + j, t0:t0 + n] for r in (hi, lo))
                w = slice(P * b, P * (b + 1))
                nc.tensor.matmul(bank[:, 0:n], WH[slot][:, w], h, start=first and j == 0, stop=False)
                nc.tensor.matmul(bank[:, 0:n], WH[slot][:, w], l, start=False, stop=False)
                end = nc.tensor.matmul(bank[:, 0:n], WL[slot][:, w], h, start=False,
                                       stop=last and j == len(blocks) - 1)
            return end

        def tiles(u0, t0_, n_tiles, hi, lo, t0, n):
            with pe.Fori(0, n_tiles // 4) as i:
                for s in range(4):
                    pe.wait_ge(split_ready, u0 + 4 * i + s + 1)
                    pe.wait_ge(bank_free[s], 1 + t0_ // 4 + i)
                    product(L[s], s % 2, range(16), 0, hi, lo, t0, n, True, True).then_inc(units_done, 1)

        def small(l):
            w, q, k, v, up, uc, y = views(l)
            name = f"cv{l}"
            pe.wait_ge(sem("cv_conv"), l + 1)
            for c in range(4):
                last = nc.tensor.matmul(AUX[0][:, 0:w], ONES, y[:, 4 + c, :], start=c == 0, stop=c == 3)
            last.then_inc(sem("cv_sum"), 1)
            u = U_SMALL[l]
            pe.wait_ge(split_ready, u + 1)
            pe.wait_ge(sem("cv_pool"), l + 1)
            for g in range(4):
                if g >= 2:
                    pe.wait_ge(sem("cv_pooled"), 4 * l + g - 1)
                for half, wt in enumerate((WH[0], WL[0])):
                    last = nc.tensor.matmul(AUX[2 + g % 2][:, 0:w], wt[:, P * g:P * (g + 1)].bitcast(f32),
                                            y[:, g, :], start=half == 0, stop=half == 1)
                last.then_inc(sem("cv_poolmm") if g < 3 else units_done, 1)
            pe.wait_ge(sem("cv_sq"), l + 1)
            for c in range(4):
                last = nc.tensor.matmul(AUX[1][:, 0:w], ONES, uc[:, c, :], start=c == 0, stop=c == 3)
            last.then_inc(sem("cv_var"), 1)
            pe.wait_ge(split_ready, u + 2)
            pe.wait_ge(sem("cv_z"), l + 1)
            for n in range(4):
                if n >= 2:
                    pe.wait_ge(sem("cv_pw"), 4 * l + n - 1)
                for c in range(4):
                    for half, wt in enumerate((WH[1], WL[1])):
                        b = 4 * n + c
                        last = nc.tensor.matmul(AUX[n % 2][:, 0:w], wt[:, P * b:P * (b + 1)].bitcast(f32),
                                                uc[:, c, :], start=c == 0 and half == 0, stop=c == 3 and half == 1)
                last.then_inc(sem("cv_pwmm") if n < 3 else units_done, 1)

        def attention(l):
            w, q, k, v, up, uc, y = views(l)
            nm = f"at{l}"
            jobs = JOBS[l]
            J = len(jobs)
            QS, KS, VS, VT, PP, AA, AT, OC, TR, SD = att_views(l)
            with pe.Fori(0, 4) as i:
                for e in range(2):
                    h = 2 * i + e
                    if e == 0:
                        pe.wait_ge(sem(nm + "_oc"), 1 + 2 * i)
                    else:
                        pe.wait_ge(sem(nm + "_qk"), h)
                    nc.tensor.matmul(BANK[4][:, 0:T], ROT1, tile(q, h)[:, w - T:w], start=True, stop=True)
                    nc.tensor.matmul(BANK[4][:, T:T2], ROT1, tile(k, h)[:, T:T2], start=True, stop=True) \
                        .then_inc(sem(nm + "_rot"), 1)
                    pe.wait_ge(sem(nm + "_vs"), h + 1)
                    if e == 0:
                        pe.wait_ge(sem(nm + "_y"), 1 + 2 * i)
                    else:
                        pe.wait_ge(sem(nm + "_vt"), h)
                    for c in range(4):
                        last = nc.tensor.transpose(BANK[5][:, P * c:P * (c + 1)], VS[e][:, P * c:P * (c + 1)], IDENT)
                    last.then_inc(sem(nm + "_vtr"), 1)

                def scores(g):
                    e, (qt, nk) = g // J, jobs[g % J]
                    if g == 0:
                        pe.wait_ge(sem(nm + "_qk"), 2 * i + 1)
                    if g == J:
                        pe.wait_ge(sem(nm + "_qk"), 2 * i + 2)
                    if g >= 2:
                        pe.wait_ge(sem(nm + "_exp"), 2 * J * i + g - 1)
                    for c in range(2):
                        r = slice(64 * c, 64 * c + 64)
                        last = nc.tensor.matmul(BANK[2 * (g % 2) + c][:, 0:nk], QS[e][r, P * qt:P * (qt + 1)],
                                                KS[e][r, 0:nk], start=True, stop=True)
                    last.then_inc(sem(nm + "_sc"), 1)

                def out_back(e):
                    pe.wait_ge(sem(nm + "_on"), 1 + 2 * i + e + 1)
                    if e == 1:
                        pe.wait_ge(sem(nm + "_y"), 1 + 2 * i + 1)
                    for jj in range(J):
                        last = nc.tensor.transpose(BANK[5][:, P * jj:P * (jj + 1)], OC[:, P * jj:P * (jj + 1)], IDENT)
                    last.then_inc(sem(nm + "_ot"), 1)

                scores(0)
                scores(1)
                for g in range(2 * J):
                    e, (qt, nk) = g // J, jobs[g % J]
                    pe.wait_ge(sem(nm + "_comb"), 2 * J * i + g + 1)
                    pe.wait_ge(sem(nm + "_at"), 1 + 2 * J * i + g)
                    for c in range(nk // P):
                        last = nc.tensor.transpose(BANK[6][:, P * c:P * (c + 1)], AA[g % 2][:, P * c:P * (c + 1)], IDENT)
                    last.then_inc(sem(nm + "_tr"), 1)
                    if g + 2 < 2 * J:
                        scores(g + 2)
                    pe.wait_ge(sem(nm + "_at"), 1 + 2 * J * i + g + 1)
                    if g % J == 0:
                        pe.wait_ge(sem(nm + "_vt"), 2 * i + e + 1)
                    if g == 0:
                        pe.wait_ge(sem(nm + "_oc"), 1 + 2 * i)
                    ob = BANK[7] if e == 0 else BANK[4]
                    for c in range(nk // P):
                        last = nc.tensor.matmul(ob[:, P * (g % J):P * (g % J + 1)], AT[g % 2][:, P * c:P * (c + 1)],
                                                VT[e][:, P * c:P * (c + 1)], start=c == 0, stop=c == nk // P - 1)
                    last.then_inc(sem(nm + "_pv"), 1)
                    if g == J + 1:
                        out_back(0)
                out_back(1)

        norm("in0", T2)
        pe.wait_ge(sem("lam_prod"), 1)
        nc.tensor.matmul(AUX[1][:, 0:4], ONES[0:64, :], LAM[0:64, 0:4], start=True, stop=True) \
            .then_inc(sem("lam_sum"), 1)
        for l in range(2):
            w = T2 if l == 0 else T
            t0 = T2 - w
            if l == 1:
                norm("in1", T2)
            pe.wait_ge(sem("n_hl"), 16 * S_AT[f"in{l}"] + 2 + KT)
            n_in = T_IN[l]
            if l == 0:
                tiles(0, 0, 36, HH, HL, 0, T2)
            else:
                tiles(U_IN[1], n_in, 28, HH, HL, T, T)
                tiles(U_IN[1] + 28, n_in + 28, 8, HH, HL, 0, T2)
            small(l)
            tiles(U_INB[l], n_in + 36, 8, HH, HL, 0, T2)
            tiles(U_INB[l] + 8, n_in + 44, 8, HH, HL, t0, w)
            evacuated(pe, n_in + 52)
            pe.wait_ge(sem("cv_pw"), 4 * l + 4)
            pe.wait_ge(sem("cv_pooled"), 4 * l + 4)
            attention(l)
            pe.wait_ge(sem(f"ys{l}_lo"), 16 // 4)
            pe.wait_ge(sem(f"at{l}_exp"), 8 * len(JOBS[l]))
            tiles(U_OUT[l], T_OUT[l], 16, HH, HL, t0, w)

        norm("fin", T)
        norm("b1", T)
        pe.wait_ge(sem("n_hl"), 16 * S_AT["b1"] + 2 + KT)
        tiles(U_IN2, T_IN2, 8, H2H, H2L, 0, T)

        def inputs(j, a):
            pe.wait_ge(sem("ssm_read"), 1 + 4 * j + a)
            for s in range(2):
                for r in range(2):
                    last = nc.tensor.matmul(AUX[s][:, T * r:T * (r + 1)], bst[32 * a:32 * a + 32, r, s, :],
                                            US[32 * a:32 * a + 32, :], start=True, stop=True)
            last.then_inc(sem("ssm_b"), 1)

        def outputs(j, a):
            pe.wait_ge(sem("ssm_x"), 4 * j + a + 1)
            for ver, x in enumerate((STM, SW)):
                for r in range(2):
                    g = 2 * a + r
                    last = nc.tensor.matmul(AUX[2][:, 0:T], WPAD[:, 1024 * ver + P * g:1024 * ver + P * (g + 1)],
                                            x[:, T * r:T * (r + 1)], start=a == 0 and ver == 0 and r == 0,
                                            stop=a == 3 and ver == 1 and r == 1)
            last.then_inc(sem("ssm_c"), 1)

        def step_start(j):
            pe.wait_ge(sem("b_in"), 16 * j + 16)
            pe.wait_ge(sem("us_ready"), j + 1)
            pe.wait_ge(sem("ssm_y"), 1 + j)
            pe.wait_ge(sem("ssm_w"), j + 1)

        with pe.Fori(0, 7) as j:
            step_start(j)
            for a in range(4):
                inputs(j, a)
                for r in range(2):
                    s = (2 * a + r) % 4
                    pe.wait_ge(split_ready, U_IN2 + 9 + 8 * j + 2 * a + r)
                    pe.wait_ge(bank_free[s], 1 + (T_IN2 + 8) // 4 + 2 * j + a // 2)
                    product(L[s], r, range(16), 0, H2H, H2L, 0, T, True, True).then_inc(units_done, 1)
                outputs(j, a)
        step_start(7)
        for a in range(4):
            inputs(7, a)
            outputs(7, a)

        v = att2_views()
        evacuated(pe, T_IN2 + 64)
        pe.wait_ge(sem("ssm_y"), 1 + 8)
        with pe.Fori(0, 4) as i:
            for e in range(2):
                h = 2 * i + e
                pe.wait_ge(sem("a2_sq"), h + 1)
                pe.wait_ge(sem("a2_vv"), 1 + h)
                nc.tensor.matmul(BANK[5][:, 0:T2], ONES, v["SQ"], start=True, stop=True).then_inc(sem("a2_ssum"), 1)
                pe.wait_ge(sem("a2_vs"), h + 1)
                for c in range(2):
                    last = nc.tensor.transpose(BANK[6][:, P * c:P * (c + 1)], v["VS"][e][:, P * c:P * (c + 1)], IDENT)
                last.then_inc(sem("a2_vtr"), 1)
                pe.wait_ge(sem("a2_qn"), h + 1)
                pe.wait_ge(sem("a2_qk"), 1 + h)
                nc.tensor.matmul(BANK[4][:, 0:T2], ROT2, v["QN"], start=True, stop=True).then_inc(sem("a2_rot"), 1)
                pe.wait_ge(sem("a2_vt"), h + 1)

            def scores2(g):
                e, (qt, nk) = g // 2, JOBS2[g % 2]
                pe.wait_ge(sem("a2_qk"), 1 + 2 * i + e + 1)
                if g >= 2:
                    pe.wait_ge(sem("a2_ms"), 4 * i + g - 1)
                nc.tensor.matmul(BANK[g % 2][:, 0:nk], v["QS"][e][:, P * qt:P * (qt + 1)], v["KS"][e][:, 0:nk],
                                 start=True, stop=True).then_inc(sem("a2_sc"), 1)

            scores2(0)
            scores2(1)
            for g in range(4):
                e, (qt, nk) = g // 2, JOBS2[g % 2]
                pe.wait_ge(sem("a2_comb"), 4 * i + g + 1)
                for c in range(nk // P):
                    last = nc.tensor.transpose(BANK[2][:, P * c:P * (c + 1)], v["PP"][g % 2][:, P * c:P * (c + 1)], IDENT)
                last.then_inc(sem("a2_tr"), 1)
                if g + 2 < 4:
                    scores2(g + 2)
                pe.wait_ge(sem("a2_at"), 4 * i + g + 1)
                if g % 2 == 0:
                    pe.wait_ge(sem("a2_yl"), 1 + 2 * i + e)
                for c in range(nk // P):
                    last = nc.tensor.matmul(BANK[3][:, P * qt:P * (qt + 1)], v["VT"][e][:, P * c:P * (c + 1)],
                                            v["AT"][g % 2][:, P * c:P * (c + 1)], start=c == 0, stop=c == nk // P - 1)
                last.then_inc(sem("a2_pv"), 1)

        def pair_tiles(u0, t0_, units, hi, lo):
            with pe.Fori(0, units // 2) as i:
                for r in range(2):
                    pe.wait_ge(split_ready, u0 + 2 * i + r + 1)
                    for b in range(2):
                        s = 2 * r + b
                        pe.wait_ge(bank_free[s], 1 + t0_ // 4 + i)
                        last = product(L[s], r, range(8 * b, 8 * b + 8), 0, hi, lo, 0, T, True, True)
                    last.then_inc(units_done, 1)

        pe.wait_ge(sem("gelu_lo"), 1)
        pe.wait_ge(sem("a2_yl"), 1 + 8)
        pair_tiles(U_GLU, T_GLU, 4, GSH, GSL)
        pair_tiles(U_ABR, T_ABR, 8, YAH, YAL)
        pe.wait_ge(sem("ys_lo"), 4)
        pair_tiles(U_SBR, T_SBR, 8, YSH, YSL)
        pe.wait_ge(sem("m_lo"), 16)
        tiles(U_OUT2, T_OUT2, 16, MH, ML, 0, T)

        norm("b2", T)
        pe.wait_ge(sem("n_hl"), 16 * S_AT["b2"] + 2 + KT)
        tiles(U_UP, T_UP, 2 * FFN, H2H, H2L, 0, T)
        pe.wait_ge(sem("ffn_lo"), FFN)
        with pe.Fori(0, 8) as i:
            for r in range(6):
                s, third = r // 3, r % 3
                pe.wait_ge(split_ready, U_DOWN + 6 * i + r + 1)
                if third == 0:
                    pe.wait_ge(bank_free[s], 1 + T_DOWN // 4 + i)
                product(L[s], r % 2, range(16 if third < 2 else FFN - 32), 16 * third, FH, FL, 0, T,
                        third == 0, third == 2).then_inc(units_done, 1)


    @block.scalar
    def _(act):
        own = Steps(act, sem("act_own"))

        def run(out, in_, func, bias=None, scale=None, accum=None):
            kw = {}
            if bias is not None:
                kw["bias"] = bias
            if scale is not None:
                kw["scale"] = scale
            if accum is not None:
                kw["accum_out"] = accum
            return nc.scalar.activation(out, in_, func, **kw)

        def high(u, slot, i=0, per=0):
            act.wait_ge(raw_in[slot], 16 * (u // 2 + 1) + 8 * per * i)
            run(WH[slot][:], RAW[slot][:], ACT.Copy).then_inc(high_ready, 1)

        def done(u, i=0, per=0):
            act.wait_ge(units_done, u + 1 + per * i)

        def norm(name, src, n, halves, final=None):
            with act.Fori(0, KT // 2) as i:
                for s in range(2):
                    act.wait_ge(sem("n_squsd"), 16 * N_AT[name] + 2 * i + s + 1)
                    run(as_src(NT_[:, s, 0:n], src), src(2 * i + s), ACT.Square).then_inc(sem("n_sq"), 1)
            act.wait_ge(sem("n_squsd"), 16 * N_AT[name] + 2 + KT)
            run(NT_[:, 6, 0:n], AUX[0][:, 0:n], ACT.Sqrt, bias=vec("eps"), scale=1.0 / D).then_inc(sem("n_std"), 1)
            act.wait_ge(sem("n_gain"), N_AT[name] + 1)
            with act.Fori(0, KT // 2) as i:
                for s in range(2):
                    k = 2 * i + s
                    act.wait_ge(sem("n_tt"), 16 * N_AT[name] + k + 1)
                    if final:
                        run(src(k), NT_[:, 2 + s, 0:n], ACT.Copy, scale=vec_at(final, k)) \
                            .then_inc(sem("n_hf"), 1)
                        continue
                    act.wait_ge(sem("n_hl"), 16 * S_AT[name] + k + 1)
                    for j, (t0, shift, col) in enumerate(halves):
                        last = run(NT_[:, 4 + s, t0:t0 + T], NT_[:, 2 + s, t0:t0 + T], ACT.Identity,
                                   bias=MODF[:, ds(3 * k + 3 * shift + col, 1)], scale=GAIN[:, ds(2 * k + j, 1)])
                    last.then_inc(sem("n_hf"), 1)
                    act.wait_ge(sem("n_hf"), 16 * N_AT[name] + k + 3)
                    hi = HH if n == T2 else H2H
                    run(tile(hi, k), NT_[:, 4 + s, 0:n], ACT.Copy).then_inc(sem("n_hh"), 1)

        def evac(u0, tiles_, w, func, dst, d0, lead=2):
            with act.Fori(0, tiles_ // 4) as i:
                for s in range(4):
                    done(u0 + s, i, 4)
                    run(tile(dst, 4 * i + s + d0)[:, 0:w], L[s][:, 0:w], func).then_inc(bank_free[s], 1)
                    high(u0 + s + 2, s % 2, i, 4)

        def highs(u0, n):
            with act.Fori(0, n // 2) as i:
                for s in range(2):
                    done(u0 + s, i, 2)
                    high(u0 + s + 2, s, i, 2)

        def attention(l):
            w, q, k, v, up, uc, y = views(l)
            nm, jobs = f"at{l}", JOBS[l]
            J = len(jobs)
            QS, KS, VS, VT, PP, AA, AT, OC, TR, SD = att_views(l)
            with act.Fori(0, 4) as i:
                for e in range(2):
                    h = 2 * i + e
                    act.wait_ge(sem(nm + "_pv"), 1 + 2 * J * i)
                    if l == 0:
                        run(QS[e][:, 0:T], tile(q, h)[:, 0:T], ACT.Copy)
                    run(KS[e][:, 0:T], tile(k, h)[:, 0:T], ACT.Copy)
                    run(VS[e], tile(v, h), ACT.Copy).then_inc(sem(nm + "_vs"), 1)
                for e in range(2):
                    act.wait_ge(sem(nm + "_vtr"), 2 * i + e + 1)
                    run(VT[e], BANK[5][:, 0:T2], ACT.Copy).then_inc(sem(nm + "_vt"), 1)

                def exps(g):
                    nk = jobs[g % J][1]
                    act.wait_ge(sem(nm + "_nb"), 2 * J * i + g + 1)
                    b = g % 2
                    for c in range(2):
                        last = run(PP[b][c][:, 0:nk], BANK[2 * b + c][:, 0:nk], ACT.Exp, bias=NB[:, 2 * b + c:2 * b + c + 1],
                                   scale=0.125, accum=SM[:, 2 * b + c:2 * b + c + 1])
                    last.then_inc(sem(nm + "_exp"), 1)

                def head(e):
                    ob = BANK[7] if e == 0 else BANK[4]
                    act.wait_ge(sem(nm + "_pv"), 1 + 2 * J * i + J * (e + 1))
                    act.wait_ge(sem(nm + "_on"), 1 + 2 * i + e)
                    for jj in range(J):
                        last = run(SD[:, P * jj:P * (jj + 1)], ob[:, P * jj:P * (jj + 1)], ACT.Square, accum=SS[:, jj:jj + 1])
                    own.mark(last)
                    act.wait_ge(sem(nm + "_ot"), 1 + 2 * i + e)
                    run(OC[:, 0:P * J], ob[:, 0:P * J], ACT.Copy).then_inc(sem(nm + "_oc"), 1)
                    own.wait()
                    own.mark(run(SS[:, 4:4 + J], SS[:, 0:J], ACT.Ln, bias=vec("eps"), scale=1.0 / P))
                    own.wait()
                    run(RR[:, 0:J], SS[:, 4:4 + J], ACT.Exp, scale=-0.5).then_inc(sem(nm + "_rr"), 1)

                own.loop(i, 4)
                exps(0)
                exps(1)
                for g in range(2 * J):
                    nk = jobs[g % J][1]
                    act.wait_ge(sem(nm + "_tr"), 2 * J * i + g + 1)
                    run(AT[g % 2][:, 0:nk], BANK[6][:, 0:nk], ACT.Copy).then_inc(sem(nm + "_at"), 1)
                    if g + 2 < 2 * J:
                        exps(g + 2)
                    if g == J:
                        head(0)
                head(1)
            own.end(4)

        def small(l):
            w, q, k, v, up, uc, y = views(l)
            name = f"cv{l}"
            act.wait_ge(sem("cv_cen"), l + 1)
            run(uc[:, :, 0:w], y[:, 4:8, 0:w], ACT.Square).then_inc(sem("cv_sq"), 1)
            act.wait_ge(sem("cv_var"), l + 1)
            run(up[:, 0, :], AUX[1][:, 0:w], ACT.Sqrt, bias=vec("eps"), scale=1.0 / 512).then_inc(sem("cv_std"), 1)
            act.wait_ge(sem("cv_nrm"), l + 1)
            for c in range(4):
                last = run(uc[:, c, :], y[:, 4 + c, :], ACT.Silu, bias=vec("ln_b", 4 * l + c), scale=vec("ln_g", 4 * l + c))
            last.then_inc(sem("cv_z"), 1)
            for r in range(2):
                done(U_SMALL[l] + r)
                high(U_SMALL[l] + r + 2, r)

        for b in range(4):
            act.sem_inc(bank_free[b], 1)
        for n in [f"at{l}_{m}" for l in range(2) for m in ("oc", "at")] + ["tables"]:
            act.sem_inc(sem(n), 1)
        act.sem_inc(sem("n_hf"), 2)
        act.wait_ge(sem("vec_in"), 16)
        run(vec("cvec", 0, 48), vec("cvec", 0, 48), ACT.Silu).then_inc(sem("s_ready"), 1)
        high(0, 0)
        high(1, 1)
        act.wait_ge(sem("x_in"), 16)
        for l in range(2):
            w, q, k, v, up, uc, y = views(l)
            if l == 0:
                act.wait_ge(sem("mod_out"), 8 + 192)
                norm("in0", src_in0, T2, [(0, 0, 1), (T, 0, 0)])
                act.wait_ge(sem("lam_sum"), 1)
                run(LAM[:, 4:8], AUX[1][:, 0:4], ACT.Exp).then_inc(sem("lam_exp"), 1)
            else:
                act.wait_ge(sem("res1"), 16)
                norm("in1", src_in1, T2, [(0, 48, 1), (T, 48, 0)])
            u = U_IN[l]
            evac(u + A0_, 4, w, ACT.Copy, uc, 0)
            evac(u + B0_, 4, w, ACT.Sigmoid, y, 0)
            evac(u + UP_, 4, w, ACT.Copy, up, 0)
            evac(u + GP_, 4, w, ACT.Silu, y, 8)
            evac(u + GC_, 4, w, ACT.Silu, y, 12)
            evac(u + Q_, 8, w, ACT.Copy, q, 0)
            evac(u + K_, 8, T2, ACT.Copy, k, 0)
            small(l)
            evac(U_INB[l], 8, T2, ACT.Copy, v, 0)
            act.wait_ge(sem("cv_pw"), 4 * l + 4)
            evac(U_INB[l] + 8, 8, w, ACT.Silu, y, 0)
            attention(l)
            act.wait_ge(sem(f"at{l}_y"), 1 + 8)
            if l == 0:
                act.dma_start(R2[:, 0:8192], dram["xin"]).then_inc(sem("x_in"), 16)
            for c in range(4):
                run(HH[:, 4 * c:4 * c + 4, T2 - w:T2], y[:, 4 * c:4 * c + 4, :], ACT.Copy).then_inc(sem(f"ys{l}_hi"), 1)
            highs(U_OUT[l], 16)

        act.wait_ge(sem("res2"), 16)
        norm("fin", src_res, T, [], final="final_g")
        act.wait_ge(sem("n_hf"), 16 * N_AT["fin"] + 2 + KT)
        norm("b1", src_res, T, [(0, 96, 2)])

        act.wait_ge(sem("n_hl"), 16 * S_AT["b1"] + 2 + KT)
        act.dma_start(POSI, dram["positions"].broadcast_to([P, T])).then_inc(sem("pos_in"), 16)
        act.dma_start(STEPS, dram["steps"].broadcast_to([P, T])).then_inc(sem("steps_in"), 16)
        act.dma_start(BST, dram["ssm_b"][0]).then_inc(sem("b_in"), 16)
        act.dma_start(CST, dram["ssm_c"][0]).then_inc(sem("c_in"), 16)

        act.wait_ge(sem("ang"), 1)
        run(SIN, NT_[:, 0, 0:T], ACT.Sin).then_inc(sem("rope_sin"), 1)
        own.mark(run(NT_[:, 1, 0:T], NT_[:, 0, 0:T], ACT.Abs))
        own.wait()
        run(COS, NT_[:, 1, 0:T], ACT.Sin, bias=vec("half_pi"), scale=-1.0).then_inc(sem("rope_cos"), 1)
        act.wait_ge(sem("th"), 1)
        par = CTAB.rearrange("p (n g) -> p n g", g=64)
        own.mark(run(par[:, 4, :], par[:, 0, :], ACT.Abs))
        run(par[:, 1, :], par[:, 0, :], ACT.Sin)
        run(par[:, 3, :], par[:, 0, :], ACT.Sin, scale=0.5)
        own.wait()
        run(par[:, 2, :], par[:, 4, :], ACT.Sin, bias=vec("half_pi"), scale=-1.0).then_inc(sem("trig"), 1)

        evac(U_IN2, 8, T, ACT.Copy, U2, 0)

        def tables(q, slot, i=None):
            sl = slice(512 * slot, 512 * slot + 512)
            act.wait_ge(sem("phase"), q + 1)
            run(STAB[:, sl], PH, ACT.Sin, scale=vec("sign2pi"))
            own.mark(run(RN, PH, ACT.Abs))
            own.wait()
            run(CTAB[:, sl], RN, ACT.Sin, bias=vec("half_pi"), scale=-2 * math.pi).then_inc(sem("tables"), 1)

        def stage_u(j):
            act.wait_ge(sem("ssm_b"), 1 + 4 * j)
            run(US, tile(U2, j), ACT.Copy).then_inc(sem("us_ready"), 1)


        evacuated(act, T_IN2 + 8)
        for j0, j1, func, dst in ((0, 3, ACT.Copy, QKV2), (3, 5, ACT.Sigmoid, GATE_A), (5, 7, ACT.Sigmoid, GATE_S)):
            with act.Fori(j0, j1) as j:
                own.loop(j, 4, j0)
                stage_u(j)
                for a in range(4):
                    tables(4 * j + a, a % 2)
                    for r in range(2):
                        t = 2 * a + r
                        done(U_IN2 + 8 + t, j, 8)
                        run(tile(dst, 8 * (j - j0) + t), L[t % 4][:, 0:T], func).then_inc(bank_free[t % 4], 1)
                        high(U_IN2 + 10 + t, r, j, 8)
            own.end(j1 - j0)
        stage_u(7)
        for a in range(4):
            tables(28 + a, a % 2)
        act.wait_ge(sem("gelu_in"), 1)
        run(US8, US8, ACT.Sigmoid, scale=2 * math.sqrt(2 / math.pi)).then_inc(sem("gelu_sig"), 1)

        v = att2_views()
        act.wait_ge(sem("gelu_g"), 1)
        with act.Fori(0, 4) as i:
            own.loop(i, 2)
            for e in range(2):
                h = 2 * i + e
                act.wait_ge(sem("a2_ssum"), 1 + h)
                run(v["SQ"][:, 0:T], tile(Q2, h), ACT.Square)
                run(v["SQ"][:, T:T2], tile(K2, h), ACT.Square).then_inc(sem("a2_sq"), 1)
                act.wait_ge(sem("a2_pv"), 1 + 4 * i)
                run(v["VS"][e], tile(V2, h), ACT.Copy).then_inc(sem("a2_vs"), 1)
                act.wait_ge(sem("a2_vv"), 1 + h + 1)
                own.mark(run(v["SQ2"], v["VV"], ACT.Ln))
                own.wait()
                run(v["R0"], v["SQ2"], ACT.Exp, scale=-0.5).then_inc(sem("a2_r0"), 1)
                act.wait_ge(sem("a2_vtr"), h + 1)
                run(v["VT"][e], BANK[6][:, 0:T], ACT.Copy).then_inc(sem("a2_vt"), 1)

            def exps2(g):
                nk = JOBS2[g % 2][1]
                act.wait_ge(sem("a2_nb"), 4 * i + g + 1)
                run(v["PP"][g % 2][:, 0:nk], v["SS_"][g % 2][:, 0:nk], ACT.Exp, bias=NB[:, g % 2:g % 2 + 1],
                    accum=SM[:, g % 2:g % 2 + 1]).then_inc(sem("a2_exp"), 1)

            exps2(0)
            exps2(1)
            for g in range(4):
                nk = JOBS2[g % 2][1]
                act.wait_ge(sem("a2_tr"), 4 * i + g + 1)
                run(v["AT"][g % 2][:, 0:nk], BANK[2][:, 0:nk], ACT.Copy).then_inc(sem("a2_at"), 1)
                if g + 2 < 4:
                    exps2(g + 2)
                if g % 2 == 1:
                    act.wait_ge(sem("a2_pv"), 1 + 4 * i + g + 1)
                    run(tile(YAH, 2 * i + g // 2), BANK[3][:, 0:T], ACT.Copy).then_inc(sem("a2_yh"), 1)

        own.end(4)

        run(GSH[:], U2, ACT.Copy).then_inc(sem("gelu_hi"), 1)
        with act.Fori(0, 2) as i:
            for r in range(2):
                done(U_GLU + r, i, 2)
                for b in range(2):
                    n = 4 * i + 2 * r + b
                    run(tile(V2, n), L[2 * r + b][:, 0:T], ACT.Sigmoid, bias=vec_at("b_glu", n)) \
                        .then_inc(bank_free[2 * r + b], 1)
                high(U_GLU + r + 2, r, i, 2)
        for c in range(4):
            act.wait_ge(sem("ys_mul"), c + 1)
            run(YSH[:, 2 * c:2 * c + 2, :], V2[:, 2 * c:2 * c + 2, :], ACT.Copy).then_inc(sem("ys_hi"), 1)
        highs(U_ABR, 16)
        with act.Fori(0, KT) as k:
            act.wait_ge(sem("m_sum"), k + 1)
            run(tile(MH, k), tile(GATE_A, k), ACT.Copy).then_inc(sem("m_hi"), 1)
        highs(U_OUT2, 16)

        act.wait_ge(sem("res3"), 16)
        norm("b2", src_res, T, [(0, 144, 2)])
        with act.Fori(0, FFN // 2) as i:
            for r in range(4):
                m, half = r // 2, r % 2
                done(U_UP + r, i, 4)
                n = 4 * i + r
                run(FT[:, 2 * m + half, :], L[r][:, 0:T], ACT.Identity, bias=vec_at("conv_b", n),
                    scale=vec_at("conv_w", 3 * n + 2)).then_inc(sem("ffn_mid"), 1)
                high(U_UP + r + 2, r % 2, i, 4)
                if half == 1:
                    act.wait_ge(sem("ffn_conv"), 2 * (2 * i + m) + 2)
                    run(FT[:, 2 * m + 1, :], FT[:, 2 * m + 1, :], ACT.Silu).then_inc(sem("ffn_silu"), 1)
                    act.wait_ge(sem("ffn_prod"), 2 * i + m + 1)
                    run(tile(FH, 2 * i + m), FT[:, 4 + m, :], ACT.Copy).then_inc(sem("ffn_hi"), 1)
        with act.Fori(0, 7) as i:
            for r in range(6):
                done(U_DOWN + r, i, 6)
                high(U_DOWN + r + 2, r % 2, i, 6)
        for r in range(4):
            done(U_DOWN + 42 + r)
            high(U_DOWN + 44 + r, r % 2)

    @block.vector
    def _(dve):
        V = nc.vector
        own = Steps(dve, sem("dve_own"))

        def mul(o_, a, b):
            return V.tensor_tensor(o_, a, b, ALU.mult)

        def sub(o_, a, b):
            return V.tensor_tensor(o_, a, b, ALU.subtract)

        def add(o_, a, b):
            return V.tensor_tensor(o_, a, b, ALU.add)

        def seq(ins):
            own.mark(ins)
            own.wait()

        def norm(name, src, n, halves=(), gname=None, g0=0, final=False):
            hi, lo = (HH, HL) if n == T2 else (H2H, H2L)
            for j, (scale, col) in enumerate(halves):
                gain = GAIN[:].rearrange("p (k j) -> p k j", j=2)[:, :, j]
                last = V.scalar_tensor_tensor(gain, MOD[:, scale:scale + KT, col], 1.0, vec(gname, g0, KT), ALU.add, ALU.mult)
            if halves:
                last.then_inc(sem("n_gain"), 1)
            else:
                dve.sem_inc(sem("n_gain"), 1)
            dve.wait_ge(sem("n_std"), N_AT[name] + 1)
            seq(V.reciprocal(NT_[:, 7, 0:n], NT_[:, 6, 0:n]))
            with dve.Fori(0, KT // 2) as i:
                for s in range(2):
                    k = 2 * i + s
                    dve.wait_ge(sem("n_hf"), 16 * N_AT[name] + k + 1)
                    mul(as_src(NT_[:, 2 + s, 0:n], src), src(k), as_src(NT_[:, 7, 0:n], src)).then_inc(sem("n_tt"), 1)
                if not final:
                    for s in range(2):
                        k = 2 * i + s
                        dve.wait_ge(sem("n_hh"), 16 * S_AT[name] + k + 1)
                        sub(tile(lo, k), NT_[:, 4 + s, 0:n], tile(hi, k)).then_inc(sem("n_hl"), 1)

        def small(l):
            w, q, k, v, up, uc, y = views(l)
            S = w // T
            name, tiles_ = f"cv{l}", T_IN[l]
            st = lambda ap: ap.rearrange("p (s t) -> p s t", s=S)
            evacuated(dve, tiles_ + 8)
            seq(mul(uc, uc, y[:, 0:4, :]))
            wdw, bdw = VEC["w_dw"][0] + l * 124, VEC["b_dw"][0] + 4 * l
            for c in range(4):
                own.mark(V.tensor_scalar(y[:, 4 + c, :], uc[:, c, :], VE[:, wdw + 31 * c + 15:wdw + 31 * c + 16],
                                         VE[:, bdw + c:bdw + c + 1], ALU.mult, ALU.add))
            for tap in [j for j in range(31) if j != 15]:
                off = tap - 15
                a, b = max(0, -off), min(T, T - off)
                for c in range(4):
                    acc = st(y[:, 4 + c, :])[:, :, a:b]
                    own.wait(3)
                    own.mark(V.scalar_tensor_tensor(acc, st(uc[:, c, :])[:, :, a + off:b + off],
                                                    VE[:, wdw + 31 * c + tap:wdw + 31 * c + tap + 1], acc,
                                                    ALU.mult, ALU.add))
            own.wait()
            dve.sem_inc(sem("cv_conv"), 1)
            dve.wait_ge(sem("rcount_in"), 16)
            evacuated(dve, tiles_ + 12)
            for g in range(4):
                own.mark(V.tensor_copy(y[:, g, :], up[:, g, :]))
            for off in [o_ for h in range(8) for o_ in (-1 - h, h + 1)][:15]:
                groups = [g for g in range(4) if -(1 << g) <= off < (1 << g)]
                for g in groups:
                    a, b = max(0, -off), min(T, T - off)
                    acc = st(y[:, g, :])[:, :, a:b]
                    own.wait(len(groups) - 1)
                    own.mark(add(acc, acc, st(up[:, g, :])[:, :, a + off:b + off]))
            own.wait()
            rc = RCNT[:].rearrange("p (g t) -> p g t", g=4)
            for g in range(4):
                for s in range(S):
                    own.mark(mul(st(y[:, g, :])[:, s, :], st(y[:, g, :])[:, s, :], rc[:, g, :]))
            own.wait()
            sub(y[:, 0:4, :], y[:, 0:4, :], up).then_inc(sem("cv_pool"), 1)
            dve.wait_ge(sem("cv_sum"), l + 1)
            for c in range(4):
                last = V.scalar_tensor_tensor(y[:, 4 + c, :], AUX[0][:, 0:w], -1.0 / 512, y[:, 4 + c, :], ALU.mult, ALU.add)
            last.then_inc(sem("cv_cen"), 1)
            evacuated(dve, tiles_ + 20)
            for g in range(4):
                dve.wait_ge(sem("cv_poolmm") if g < 3 else units_done, 3 * l + g + 1 if g < 3 else U_SMALL[l] + 1)
                V.scalar_tensor_tensor(y[:, 8 + g, :], AUX[2 + g % 2][:, 0:w], vec("pool_scale", 4 * l + g), y[:, 8 + g, :],
                                       ALU.mult, ALU.mult).then_inc(sem("cv_pooled"), 1)
            dve.wait_ge(sem("cv_std"), l + 1)
            seq(V.reciprocal(up[:, 1, :], up[:, 0, :]))
            for c in range(4):
                last = mul(y[:, 4 + c, :], y[:, 4 + c, :], up[:, 1, :])
            last.then_inc(sem("cv_nrm"), 1)
            for n in range(4):
                dve.wait_ge(sem("cv_pwmm") if n < 3 else units_done, 3 * l + n + 1 if n < 3 else U_SMALL[l] + 2)
                mul(y[:, 12 + n, :], AUX[n % 2][:, 0:w], y[:, 12 + n, :]).then_inc(sem("cv_pw"), 1)

        def attention(l):
            w, q, k, v, up, uc, y = views(l)
            nm, jobs = f"at{l}", JOBS[l]
            J = len(jobs)
            QS, KS, VS, VT, PP, AA, AT, OC, TR, SD = att_views(l)
            evacuated(dve, T_IN[l] + 52)
            cos, sin = COS, SIN
            with dve.Fori(0, 4) as i:
                own.loop(i, 2 * 4 + 2 * J * 3 + 2 * 4)
                for e in range(2):
                    h = 2 * i + e
                    dve.wait_ge(sem(nm + "_pv"), 1 + 2 * J * i)
                    qx, kx = QS[e][:, w - T:w], KS[e][:, T:T2]
                    own.mark(mul(qx, tile(q, h)[:, w - T:w], cos))
                    own.mark(mul(kx, tile(k, h)[:, T:T2], cos))
                    dve.wait_ge(sem(nm + "_rot"), h + 1)
                    for r in range(2):
                        own.mark(mul(TR[:, T * r:T * (r + 1)], BANK[4][:, T * r:T * (r + 1)], sin))
                    own.wait()
                    add(qx, qx, TR[:, 0:T])
                    add(kx, kx, TR[:, T:T2]).then_inc(sem(nm + "_qk"), 1)
                    dve.wait_ge(sem(nm + "_qk"), h + 1)

                def maxima(g):
                    b, nk = g % 2, jobs[g % J][1]
                    dve.wait_ge(sem(nm + "_sc"), 2 * J * i + g + 1)
                    for c in range(2):
                        last = V.reduce_max(MX[:, 2 * b + c:2 * b + c + 1], BANK[2 * b + c][:, 0:nk], AX)
                    seq(last)
                    V.tensor_scalar(NB[:, 2 * b:2 * b + 2], MX[:, 2 * b:2 * b + 2], -0.125, None, ALU.mult) \
                        .then_inc(sem(nm + "_nb"), 1)

                def head(e):
                    dve.wait_ge(sem(nm + "_rr"), 2 * i + e + 1)
                    ms, r0 = SS[:, 0:J], RR[:, 0:J]
                    seq(V.tensor_scalar(ms, ms, 1.0 / P, EPS, ALU.mult, ALU.add))
                    seq(mul(RR[:, 4:4 + J], r0, r0))
                    seq(mul(RR[:, 4:4 + J], RR[:, 4:4 + J], ms))
                    own.mark(V.tensor_scalar(RR[:, 4:4 + J], RR[:, 4:4 + J], -0.5, 1.5, ALU.mult, ALU.add))
                    own.wait()
                    mul(r0, r0, RR[:, 4:4 + J]).then_inc(sem(nm + "_r1"), 1)
                    dve.wait_ge(sem(nm + "_r1"), 2 * i + e + 1)
                    dve.wait_ge(sem(nm + "_oc"), 1 + 2 * i + e + 1)
                    oc = OC[:, 0:P * J].rearrange("p (j t) -> p j t", j=J)
                    mul(oc, oc, r0.unsqueeze(2).broadcast_to([P, J, P])).then_inc(sem(nm + "_on"), 1)

                def gated(e):
                    dve.wait_ge(sem(nm + "_ot"), 1 + 2 * i + e + 1)
                    yt = tile(y, 2 * i + e)
                    V.scalar_tensor_tensor(yt, BANK[5][:, 0:P * J], SG[:, l:l + 1], yt, ALU.mult, ALU.mult) \
                        .then_inc(sem(nm + "_y"), 1)

                maxima(0)
                maxima(1)
                for g in range(2 * J):
                    b, nk = g % 2, jobs[g % J][1]
                    dve.wait_ge(sem(nm + "_exp"), 2 * J * i + g + 1)
                    seq(V.reciprocal(RC[:, 2 * b:2 * b + 2], SM[:, 2 * b:2 * b + 2]))
                    p0, p1 = PP[b][0][:, 0:nk], PP[b][1][:, 0:nk]
                    seq(V.tensor_scalar(p1, p1, RC[:, 2 * b + 1:2 * b + 2], LAM[:, l:l + 1], ALU.mult, ALU.mult))
                    V.scalar_tensor_tensor(AA[b][:, 0:nk], p0, RC[:, 2 * b:2 * b + 1], p1, ALU.mult, ALU.add) \
                        .then_inc(sem(nm + "_comb"), 1)
                    if g + 2 < 2 * J:
                        dve.wait_ge(sem(nm + "_comb"), 2 * J * i + g + 1)
                        maxima(g + 2)
                    if g == J + 1:
                        head(0)
                        gated(0)
                head(1)
                gated(1)
            own.end(4)

        dve.wait_ge(sem("vec_in"), 16)
        for n in [f"at{l}_{m}" for l in range(2) for m in ("y", "on")] + ["ssm_read", "ssm_y", "a2_vv", "a2_qk", "a2_yl"]:
            dve.sem_inc(sem(n), 1)
        dve.sem_inc(sem("mod_out"), 8)
        dve.sem_inc(sem("n_hl"), 2)
        lamv = vec("lam", 0, 8)[0:64, :].rearrange("p (n c) -> p n c", c=2)
        mul(LAM[0:64, 0:4], lamv[:, :, 0], lamv[:, :, 1]).then_inc(sem("lam_prod"), 1)
        for l in range(2):
            last = V.tensor_scalar(SG[:, l:l + 1], vec("subln_g", l), 1.0 - LAM_INIT[l], None, ALU.mult)
        own.mark(last)
        with dve.Fori(0, 24) as i:
            for s in range(8):
                n = 8 * i + s
                dve.wait_ge(sem("mod_used"), n + 1)
                V.tensor_scalar(MODF[:, ds(24 * i + 3 * s, 3)], BANK[s][:, 0:3], vec_at("b_mod", n), None, ALU.add) \
                    .then_inc(sem("mod_out"), 1)
        dve.wait_ge(sem("mod_out"), 8 + 192)
        dve.wait_ge(sem("x_in"), 16)
        norm("in0", src_in0, T2, [(16, 1), (16, 0)], "norm_g", 0)
        dve.wait_ge(sem("lam_exp"), 1)
        for l in range(2):
            own.mark(V.scalar_tensor_tensor(LAM[:, l:l + 1], LAM[:, 5 + 2 * l:6 + 2 * l], -LAM_INIT[l],
                                            LAM[:, 4 + 2 * l:5 + 2 * l], ALU.add, ALU.subtract))
        dve.wait_ge(sem("const_in"), 16)
        for l in range(2):
            w, q, k, v, up, uc, y = views(l)
            if l == 1:
                norm("in1", src_in1, T2, [(64, 1), (64, 0)], "norm_g", KT)
            small(l)
            attention(l)
            for c in range(4):
                dve.wait_ge(sem(f"ys{l}_hi"), c + 1)
                r = (slice(None), slice(4 * c, 4 * c + 4), slice(T2 - w, T2))
                sub(HL[r], y[:, 4 * c:4 * c + 4, :], HH[r]).then_inc(sem(f"ys{l}_lo"), 1)
            if l == 0:
                dve.wait_ge(sem("x_in"), 32)
            with dve.Fori(0, 4) as i:
                for s in range(4):
                    n = 4 * i + s
                    dve.wait_ge(units_done, U_OUT[l] + n + 1)
                    if l == 0:
                        V.scalar_tensor_tensor(tile(CT0, n), L[s][:, 0:T], MODF[:, ds(3 * n + 3 * 32 + 1, 1)],
                                               tile(XIN, n)[:, 0:T], ALU.mult, ALU.add)
                        V.scalar_tensor_tensor(tile(RES, n), L[s][:, T:T2], MODF[:, ds(3 * n + 3 * 32, 1)],
                                               tile(XIN, n)[:, T:T2], ALU.mult, ALU.add).then_inc(bank_free[s], 1)
                    else:
                        V.scalar_tensor_tensor(tile(RES, n), L[s][:, 0:T], MODF[:, ds(3 * n + 3 * 80, 1)],
                                               tile(RES, n), ALU.mult, ALU.add).then_inc(bank_free[s], 1)
            evacuated(dve, T_OUT[l] + 16)
            dve.sem_inc(sem(f"res{l + 1}"), 16)
        norm("fin", src_res, T, final=True)
        dve.wait_ge(sem("n_hf"), 16 * N_AT["fin"] + 2 + KT)
        norm("b1", src_res, T, [(112, 2)], "norm1_g", 0)

        C1, C2, C3 = 6.28125, 1.93500518798828125e-3, 3.0199159819567e-07
        MAGIC = 12582912.0

        def reduce_angle(a, r):
            seq(V.tensor_scalar(r, a, 1 / (2 * math.pi), MAGIC, ALU.mult, ALU.add))
            seq(V.tensor_scalar(r, r, -MAGIC, None, ALU.add))
            for c in (C1, C2, C3):
                seq(V.scalar_tensor_tensor(a, r, -c, a, ALU.mult, ALU.add))
            seq(V.tensor_scalar(a, a, 3.1415925, -3.1415925, ALU.min, ALU.max))

        ang, tmp = NT_[:, 0, 0:T], NT_[:, 2, 0:T]
        dve.wait_ge(sem("pos_in"), 16)
        seq(V.tensor_copy(ang, POSI))
        seq(V.tensor_scalar(ang, ang, vec("inv_freq"), None, ALU.mult))
        reduce_angle(ang, tmp)
        own.mark(V.tensor_copy(tmp, ang))
        own.wait()
        dve.sem_inc(sem("ang"), 1)

        par = CTAB.rearrange("p (n g) -> p n g", g=64)
        stab = STAB.rearrange("p (n g) -> p n g", g=64)
        th, sn, cs, sh, _, dt, x, e1 = (par[:, n, :] for n in range(8))
        ta, tb, tc, den, nr, ni, cr, ci = (stab[:, n, :] for n in range(8))
        bits = par[:, 8, :].bitcast(i32)
        coef = COEF.rearrange("p (n g) -> p n g", g=64)
        CA, CB, CE, CF, TURN, MAG = (coef[:, n, :] for n in range(6))
        seq(V.tensor_scalar(dt, vec("log_dt", 0, 64), 88.0, -89.0, ALU.min, ALU.max))
        seq(V.tensor_scalar(ta, dt, 1 / math.log(2), MAGIC, ALU.mult, ALU.add))
        seq(V.tensor_scalar(ta, ta, -MAGIC, -127.0, ALU.add, ALU.max))
        seq(V.scalar_tensor_tensor(dt, ta, -0.693359375, dt, ALU.mult, ALU.add))
        seq(V.scalar_tensor_tensor(dt, ta, 2.12194440e-4, dt, ALU.mult, ALU.add))
        seq(V.tensor_scalar(bits, ta, 127.0, 8388608.0, ALU.add, ALU.mult))
        seq(V.tensor_scalar(tb, dt, 1 / 5040, 1 / 720, ALU.mult, ALU.add))
        for c in (1 / 120, 1 / 24, 1 / 6, 0.5, 1.0, 1.0):
            seq(mul(tb, tb, dt))
            seq(V.tensor_scalar(tb, tb, c, None, ALU.add))
        seq(mul(dt, tb, par[:, 8, :]))
        seq(mul(x, vec("lam_re", 0, 64), dt))
        seq(V.tensor_scalar(x, x, 40.0, -40.0, ALU.min, ALU.max))
        seq(V.tensor_scalar(x, x, 1 / 64, None, ALU.mult))
        seq(V.tensor_scalar(e1, x, 1 / 40320, 1 / 5040, ALU.mult, ALU.add))
        for c in (1 / 720, 1 / 120, 1 / 24, 1 / 6, 0.5, 1.0):
            seq(mul(e1, e1, x))
            seq(V.tensor_scalar(e1, e1, c, None, ALU.add))
        seq(mul(e1, e1, x))
        for _ in range(6):
            seq(V.scalar_tensor_tensor(e1, e1, 2.0, e1, ALU.add, ALU.mult))
        seq(V.tensor_scalar(MAG, e1, 1.0, None, ALU.add))
        seq(mul(th, vec("lam_im", 0, 64), dt))
        reduce_angle(th, ta)
        seq(V.tensor_scalar(TURN, th, 1 / (2 * math.pi), None, ALU.mult))
        dve.sem_inc(sem("th"), 1)
        dve.wait_ge(sem("trig"), 1)
        seq(mul(nr, e1, cs))
        seq(mul(ta, sh, sh))
        seq(V.scalar_tensor_tensor(nr, ta, -2.0, nr, ALU.mult, ALU.add))
        seq(mul(ni, MAG, sn))
        lr, li = vec("lam_re", 0, 64), vec("lam_im", 0, 64)
        seq(mul(den, lr, lr))
        seq(mul(ta, li, li))
        seq(add(den, den, ta))
        seq(V.reciprocal(den, den))
        seq(mul(cr, nr, lr))
        seq(mul(ta, ni, li))
        seq(add(cr, cr, ta))
        seq(mul(cr, cr, den))
        seq(mul(ci, ni, lr))
        seq(mul(ta, nr, li))
        seq(sub(ci, ci, ta))
        seq(mul(ci, ci, den))
        m0, m1 = vec("half0"), vec("half1")
        seq(V.tensor_scalar(ta, ci, m1, None, ALU.mult))
        seq(V.scalar_tensor_tensor(CA, cr, m0, ta, ALU.mult, ALU.subtract))
        seq(V.tensor_scalar(CF, cr, m0, -1.0, ALU.mult, ALU.mult))
        seq(sub(CF, CF, ta))
        seq(V.tensor_scalar(tb, cr, m1, None, ALU.mult))
        seq(V.tensor_scalar(tc, ci, m0, -1.0, ALU.mult, ALU.mult))
        seq(sub(CB, tc, tb))
        seq(add(CE, tc, tb))
        seq(V.memset(WPAD, 0.0))

        wpad = [WPAD[:, 1024 * n:1024 * n + 1152].rearrange("p (g x) -> p g x", x=144)[:, :, 0:16] for n in range(2)]
        cst = CST.rearrange("p (c g h) -> p c g h", c=2, h=16)
        t12 = [T12[:, P * n:P * (n + 1)].rearrange("p (g h) -> p g h", h=16) for n in range(2)]

        def lay_c(j):
            dve.wait_ge(sem("c_in"), 16 * j + 16)
            dve.wait_ge(sem("ssm_c"), 1 + 4 * j)
            for n, (c0, c1) in enumerate(((CA, CB), (CE, CF))):
                for m, c in enumerate((c0, c1)):
                    own.mark(mul(t12[m], cst[:, m], c[:, ds(8 * j, 8)].unsqueeze(2).broadcast_to([P, 8, 16])))
                own.wait()
                last = add(wpad[n], t12[0], t12[1])
                if n == 0:
                    seq(last)
            last.then_inc(sem("ssm_w"), 1)

        ph3, rn3 = (r.rearrange("p (g t) -> p g t", g=2) for r in (PH, RN))
        steps3 = STEPS.unsqueeze(1).broadcast_to([P, 2, T])

        def phase(q, g):
            dve.wait_ge(sem("tables"), 1 + q)
            seq(mul(ph3, TURN[:, ds(g, 2)].unsqueeze(2).broadcast_to([P, 2, T]), steps3))
            seq(V.tensor_scalar(RN, PH, MAGIC, -MAGIC, ALU.add, ALU.add))
            sub(PH, PH, RN).then_inc(sem("phase"), 1)
            dve.wait_ge(sem("phase"), q + 1)

        def scan(j, a):
            q = 4 * j + a
            sl = slice(512 * (a % 2), 512 * (a % 2) + 512)
            dve.wait_ge(sem("ssm_b"), 1 + q + 1)
            dve.wait_ge(sem("tables"), 1 + q + 1)
            dve.wait_ge(sem("ssm_c"), 1 + q)
            own.mark(mul(SW, AUX[0][:, 0:T2], CTAB[:, sl]))
            mul(STM, AUX[1][:, 0:T2], STAB[:, sl]).then_inc(sem("ssm_read"), 1)
            dve.wait_ge(sem("ssm_read"), 1 + q + 1)
            own.wait()
            seq(add(SW, SW, STM))
            for r in range(2):
                part = SW[:, T * r:T * (r + 1)]
                own.mark(V.tensor_tensor_scan(part, MAG[:, ds(8 * j + 2 * a + r, 1)].broadcast_to([P, T]), part, 0.0,
                                              ALU.mult, ALU.add))
            own.wait()
            seq(mul(STM, SW, CTAB[:, sl]))
            mul(SW, SW, STAB[:, sl]).then_inc(sem("ssm_x"), 1)

        def finish(j):
            dve.wait_ge(sem("ssm_c"), 1 + 4 * j + 4)
            V.scalar_tensor_tensor(tile(U2, j), tile(U2, j), vec_at("d_skip", j), AUX[2][:, 0:T], ALU.mult, ALU.add) \
                .then_inc(sem("ssm_y"), 1)

        dve.wait_ge(sem("steps_in"), 16)
        evacuated(dve, T_IN2 + 8)
        phase(0, 0)
        with dve.Fori(0, 7) as j:
            own.loop(j, 5 + 4 * 7)
            lay_c(j)
            for a in range(4):
                phase(4 * j + a + 1, 8 * j + 2 * a + 2)
                scan(j, a)
            finish(j)
        own.end(7)
        lay_c(7)
        for a in range(4):
            if a < 3:
                phase(28 + a + 1, 56 + 2 * a + 2)
            scan(7, a)
        finish(7)

        dve.wait_ge(sem("ssm_y"), 1 + 8)
        G = R2[:, 0:2048]
        seq(mul(US8, G, G))
        seq(V.tensor_scalar(US8, US8, 0.044715, 1.0, ALU.mult, ALU.add))
        mul(US8, US8, G).then_inc(sem("gelu_in"), 1)
        dve.wait_ge(sem("gelu_sig"), 1)
        mul(G, G, US8).then_inc(sem("gelu_g"), 1)

        v = att2_views()
        dve.wait_ge(sem("rope_cos"), 1)
        evacuated(dve, T_IN2 + 64)
        with dve.Fori(0, 4) as i:
            own.loop(i, 2 * 7 + 4)
            for e in range(2):
                h = 2 * i + e
                dve.wait_ge(sem("a2_ssum"), 1 + h + 1)
                V.tensor_scalar(v["VV"], BANK[5][:, 0:T2], 1.0 / P, EPS, ALU.mult, ALU.add).then_inc(sem("a2_vv"), 1)
                dve.wait_ge(sem("a2_r0"), h + 1)
                dve.wait_ge(sem("a2_vv"), 1 + h + 1)
                r0, tt = v["R0"], v["TT"]
                seq(mul(tt, r0, r0))
                seq(mul(tt, tt, v["VV"]))
                seq(V.tensor_scalar(tt, tt, -0.5, 1.5, ALU.mult, ALU.add))
                seq(mul(tt, tt, r0))
                V.scalar_tensor_tensor(v["QN"][:, 0:T], tile(Q2, h), vec("q_g"), tt[:, 0:T], ALU.mult, ALU.mult)
                V.scalar_tensor_tensor(v["QN"][:, T:T2], tile(K2, h), vec("k_g"), tt[:, T:T2], ALU.mult, ALU.mult) \
                    .then_inc(sem("a2_qn"), 1)
                dve.wait_ge(sem("a2_qn"), h + 1)
                dve.wait_ge(sem("a2_pv"), 1 + 4 * i)
                own.mark(mul(v["QS"][e], v["QN"][:, 0:T], COS))
                own.mark(mul(v["KS"][e], v["QN"][:, T:T2], COS))
                dve.wait_ge(sem("a2_rot"), h + 1)
                mul(tt[:, 0:T], BANK[4][:, 0:T], SIN)
                own.mark(mul(tt[:, T:T2], BANK[4][:, T:T2], SIN))
                own.wait()
                add(v["QS"][e], v["QS"][e], tt[:, 0:T])
                add(v["KS"][e], v["KS"][e], tt[:, T:T2]).then_inc(sem("a2_qk"), 1)
                dve.wait_ge(sem("a2_qk"), 1 + h + 1)

            def scores2(g):
                b, nk = g % 2, JOBS2[g % 2][1]
                dve.wait_ge(sem("a2_sc"), 4 * i + g + 1)
                ss, sc = v["SS_"][b], BANK[b]
                if nk > P:
                    V.tensor_scalar(ss[:, 0:nk - P], sc[:, 0:nk - P], P ** -0.5, None, ALU.mult)
                V.scalar_tensor_tensor(ss[:, nk - P:nk], sc[:, nk - P:nk], P ** -0.5, MASK, ALU.mult, ALU.add) \
                    .then_inc(sem("a2_ms"), 1)
                dve.wait_ge(sem("a2_ms"), 4 * i + g + 1)
                seq(V.reduce_max(MX[:, b:b + 1], ss[:, 0:nk], AX))
                V.tensor_scalar(NB[:, b:b + 1], MX[:, b:b + 1], -1.0, None, ALU.mult).then_inc(sem("a2_nb"), 1)

            scores2(0)
            scores2(1)
            for g in range(4):
                b, nk = g % 2, JOBS2[g % 2][1]
                dve.wait_ge(sem("a2_exp"), 4 * i + g + 1)
                V.reciprocal(RC[:, b:b + 1], SM[:, b:b + 1]).then_inc(sem("a2_rc"), 1)
                dve.wait_ge(sem("a2_rc"), 4 * i + g + 1)
                V.tensor_scalar(v["PP"][b][:, 0:nk], v["PP"][b][:, 0:nk], RC[:, b:b + 1], None, ALU.mult) \
                    .then_inc(sem("a2_comb"), 1)
                if g + 2 < 4:
                    scores2(g + 2)
                if g % 2 == 1:
                    n = 2 * i + g // 2
                    dve.wait_ge(sem("a2_yh"), n + 1)
                    sub(tile(YAL, n), BANK[3][:, 0:T], tile(YAH, n)).then_inc(sem("a2_yl"), 1)
        own.end(4)

        dve.wait_ge(sem("gelu_hi"), 1)
        sub(GSL[:], U2, GSH[:]).then_inc(sem("gelu_lo"), 1)
        evacuated(dve, T_GLU + 8)
        for c in range(4):
            r = (slice(None), slice(2 * c, 2 * c + 2), slice(None))
            mul(V2[r], V2[r], U2[r]).then_inc(sem("ys_mul"), 1)
        for c in range(4):
            r = (slice(None), slice(2 * c, 2 * c + 2), slice(None))
            dve.wait_ge(sem("ys_hi"), c + 1)
            sub(YSL[r], V2[r], YSH[r]).then_inc(sem("ys_lo"), 1)
        with dve.Fori(0, 4) as i:
            for s in range(4):
                dve.wait_ge(units_done, U_ABR + 2 * i + s // 2 + 1)
                mul(tile(GATE_A, 4 * i + s), L[s][:, 0:T], tile(GATE_A, 4 * i + s)).then_inc(bank_free[s], 1)
        evacuated(dve, T_ABR + 16)
        with dve.Fori(0, 4) as i:
            for s in range(4):
                n = 4 * i + s
                dve.wait_ge(units_done, U_SBR + 2 * i + s // 2 + 1)
                mul(tile(GATE_S, n), L[s][:, 0:T], tile(GATE_S, n)).then_inc(bank_free[s], 1)
                dve.wait_ge(bank_free[s], 1 + T_SBR // 4 + i + 1)
                add(tile(GATE_A, n), tile(GATE_A, n), tile(GATE_S, n)).then_inc(sem("m_sum"), 1)
        with dve.Fori(0, KT) as k:
            dve.wait_ge(sem("m_hi"), k + 1)
            sub(tile(ML, k), tile(GATE_A, k), tile(MH, k)).then_inc(sem("m_lo"), 1)
        with dve.Fori(0, 4) as i:
            for s in range(4):
                n = 4 * i + s
                dve.wait_ge(units_done, U_OUT2 + n + 1)
                V.scalar_tensor_tensor(tile(RES, n), L[s][:, 0:T], MODF[:, ds(3 * n + 3 * 128 + 2, 1)], tile(RES, n),
                                       ALU.mult, ALU.add).then_inc(bank_free[s], 1)
        evacuated(dve, T_OUT2 + 16)
        dve.sem_inc(sem("res3"), 16)

        norm("b2", src_res, T, [(160, 2)], "norm2_g", 0)
        with dve.Fori(0, FFN // 2) as i:
            own.loop(i, 4)
            for r in range(4):
                m, half = r // 2, r % 2
                n = 4 * i + r
                acc = FT[:, 2 * m + half, :]
                dve.wait_ge(sem("ffn_mid"), n + 1)
                seq(V.scalar_tensor_tensor(acc[:, 1:T], L[r][:, 0:T - 1], vec_at("conv_w", 3 * n + 1), acc[:, 1:T],
                                           ALU.mult, ALU.add))
                V.scalar_tensor_tensor(acc[:, 2:T], L[r][:, 0:T - 2], vec_at("conv_w", 3 * n), acc[:, 2:T],
                                       ALU.mult, ALU.add).then_inc(bank_free[r], 1)
                if half == 1:
                    for b in (r - 1, r):
                        dve.wait_ge(bank_free[b], 1 + T_UP // 4 + i + 1)
                    dve.sem_inc(sem("ffn_conv"), 2)
                    dve.wait_ge(sem("ffn_silu"), 2 * i + m + 1)
                    mul(FT[:, 4 + m, :], FT[:, 2 * m, :], FT[:, 2 * m + 1, :]).then_inc(sem("ffn_prod"), 1)
                    dve.wait_ge(sem("ffn_hi"), 2 * i + m + 1)
                    sub(tile(FL, 2 * i + m), FT[:, 4 + m, :], tile(FH, 2 * i + m)).then_inc(sem("ffn_lo"), 1)
        own.end(FFN // 2)
        with dve.Fori(0, 8) as i:
            for s in range(2):
                n = 2 * i + s
                dve.wait_ge(units_done, U_DOWN + 3 * n + 3)
                V.scalar_tensor_tensor(tile(RES, n), L[s][:, 0:T], MODF[:, ds(3 * n + 3 * 176 + 2, 1)], tile(RES, n),
                                       ALU.mult, ALU.add).then_inc(bank_free[s], 1)
    ctx.close()


def kernel(**inputs):
    import concourse.bacc as bacc
    from concourse.bass_utils import run_bass_kernel_spmd

    a = {name: np.asarray(v) for name, v in inputs.items()}
    laid = lay_out(a)
    nc = bacc.Bacc("TRN2", target_bir_lowering=False, num_devices=1)
    arrays, dram = {}, {}
    for name in ARRAYS:
        v = np.ascontiguousarray(laid[name])
        arrays[f"in_{name}"] = v
        dram[name] = nc.dram_tensor(f"in_{name}", v.shape, mybir.dt.from_np(v.dtype), kind="ExternalInput").ap()
    out = nc.dram_tensor("out_y", (P, KT, T), mybir.dt.float32, kind="ExternalOutput").ap()
    build(nc, dram, out)
    r = run_bass_kernel_spmd(nc, [arrays], core_ids=[0])
    y = r.results[0]["out_y"]
    return y.transpose(1, 0, 2).reshape(D, T).T.reshape(1, T, D)
```

```python
import math
from contextlib import ExitStack

import numpy as np
import concourse.bass as bass
from concourse import mybir

P = 128
D = 2048
KT = D // P
T = 256
T2 = 2 * T
EPS = 1e-6
KB = 256
HALF = 8 * P
UNIT = 16 * P

A0_, B0_, UP_, GP_, GC_, Q_, K_, V_, GA_ = 0, 4, 8, 12, 16, 20, 28, 36, 44
IN_TILES = 52
SPECIAL = 2
FFN = 44

VEC = {}
_at = 0
for _name, _cols in [
    ("b_mod", 192), ("norm_g", 32), ("subln_g", 2), ("pool_scale", 8), ("b_dw", 8), ("ln_g", 8),
    ("ln_b", 8), ("w_dw", 2 * 4 * 31), ("lam", 8), ("final_g", 16), ("norm1_g", 16), ("q_g", 1), ("k_g", 1),
    ("b_glu", 8), ("norm2_g", 16), ("d_skip", 8), ("conv_b", 88), ("conv_w", 88 * 3),
    ("lam_re", 64), ("lam_im", 64), ("log_dt", 64), ("inv_freq", 1), ("half0", 1), ("half1", 1), ("sign2pi", 1),
    ("eps", 1), ("half_pi", 1),
]:
    VEC[_name] = (_at, _cols)
    _at += _cols
NVEC = _at


def feature_columns(v):
    return v.reshape(-1, P).T


def tiles_of(w):
    kt, nt = w.shape[0] // P, w.shape[1] // P
    return w.reshape(kt, P, nt, P).transpose(2, 1, 0, 3).reshape(nt, P, kt * P)


def pairs_of(w):
    kt, nt = w.shape[0] // P, w.shape[1] // P
    return w.reshape(kt, P, nt // 2, 2, P).transpose(2, 1, 3, 0, 4).reshape(nt // 2, P, 2 * kt * P)


def lay_out(a):
    out = {}
    f = np.float32
    out["xin"] = np.stack([a["ctx"][0].T.reshape(KT, P, T), a["x"][0].T.reshape(KT, P, T)], 2) \
        .transpose(1, 0, 2, 3).reshape(P, KT * T2)
    order = [range(40, 44), range(44, 48), range(32, 36), range(36, 40), range(48, 52),
             range(0, 8), range(8, 16), range(16, 24), range(24, 32)]
    order = [n for r in order for n in r]
    for l in range(2):
        out[f"w_in{l}"] = tiles_of(a["w_in"][l])[order]
        out[f"w_out{l}"] = tiles_of(a["w_out"][l])
        small = np.zeros((SPECIAL, P, UNIT), f)
        small[0, :, :4 * P] = a["w_pool"][l].transpose(1, 0, 2).reshape(P, 4 * P)
        small[1] = a["w_pw2"][l].reshape(4, P, 4, P).transpose(1, 2, 0, 3).reshape(P, UNIT)
        out[f"w_small{l}"] = small
    out["w_mods"] = np.concatenate([w.T.reshape(-1, P, D) for w in (a["w_mod"][0], a["w_mod"][1], a["w_mod_2"][0])])
    out["cond"] = np.concatenate([a["c"][0], a["c_ctx"], a["c_2"][0]])[None]
    order2 = list(range(24, 32)) + list(range(24)) + list(range(32, 64))
    out["w_in2"] = tiles_of(a["w_in_2"][0])[order2]
    out["w_glu"] = pairs_of(a["w_glu_2"][0])
    out["w_abr"] = pairs_of(a["w_attn_br_2"][0])
    out["w_sbr"] = pairs_of(a["w_ssm_br_2"][0])
    out["w_out2"] = tiles_of(a["w_out_2"][0])
    up = tiles_of(a["w_up_2"][0])
    out["w_up"] = np.stack([up[:FFN], up[FFN:]], 1).reshape(2 * FFN, P, UNIT)
    down = a["w_down_2"][0].reshape(FFN, P, KT, P).transpose(2, 1, 0, 3)
    down = np.concatenate([down, np.zeros((KT, P, 48 - FFN, P), f)], 2)
    out["w_down"] = down.reshape(KT, P, 3, UNIT).transpose(0, 2, 1, 3).reshape(3 * KT, P, UNIT)

    vec = np.zeros((P, NVEC), f)

    def put(name, v):
        at, n = VEC[name]
        vec[:v.shape[0], at:at + n] = v

    put("b_mod", np.concatenate([feature_columns(v) for v in (a["b_mod"][0], a["b_mod"][1], a["b_mod_2"][0])], 1))
    for name, key in [("norm_g", "norm_g"), ("subln_g", "subln_g"), ("pool_scale", "pool_scale"), ("b_dw", "b_dw"),
                      ("ln_g", "conv_ln_g"), ("ln_b", "conv_ln_b"), ("final_g", "final_g"), ("norm1_g", "norm1_g_2"),
                      ("q_g", "q_norm_g_2"), ("k_g", "k_norm_g_2"), ("b_glu", "b_glu_2"), ("norm2_g", "norm2_g_2"),
                      ("d_skip", "ssm_d_2")]:
        put(name, feature_columns(a[key]))
    put("w_dw", a["w_dw"].reshape(2, 31, 4, P).transpose(3, 0, 2, 1).reshape(P, -1))
    put("lam", np.stack([a["lambda_q1"], a["lambda_k1"], a["lambda_q2"], a["lambda_k2"]], 1).reshape(8, 64).T)
    pair = lambda v: feature_columns(v).reshape(P, 2, FFN).transpose(0, 2, 1)
    put("conv_b", pair(a["conv_b_2"][0]).reshape(P, -1))
    put("conv_w", np.stack([pair(a["conv_w_2"][0][i]) for i in range(3)], 3).reshape(P, -1))
    twice = lambda v: np.concatenate([v, v], 0)
    put("lam_re", twice(a["ssm_lambda_re_2"][0].T))
    put("lam_im", twice(a["ssm_lambda_im_2"][0].T))
    put("log_dt", np.broadcast_to(a["ssm_log_dt_2"], (P, 64)))
    half = np.arange(64, dtype=f)
    put("inv_freq", twice((f(10000.0) ** (-half / f(64))).astype(f)[:, None]))
    low = (np.arange(P) < 64)[:, None]
    put("half0", low.astype(f))
    put("half1", (~low).astype(f))
    put("sign2pi", np.where(low, 2 * math.pi, -2 * math.pi).astype(f))
    put("eps", np.full((P, 1), EPS, f))
    put("half_pi", np.full((P, 1), math.pi / 2, f))
    out["vec"] = vec
    out["positions"] = a["positions_2"]
    bre, bim = (a[k][0].transpose(0, 2, 1) for k in ("ssm_b_re_2", "ssm_b_im_2"))
    b = np.stack([np.concatenate([bre, bim], 2), np.concatenate([bim, bre], 2)], 2)
    bp = np.zeros((8, 4, 2, 16, 2, 2, P), f)
    b = b.reshape(8, 4, 2, 16, 2, P)
    for par in range(2):
        bp[:, :, par, :, par] = b[:, :, par]
    out["ssm_b"] = bp.reshape(8, P, 4 * P)
    c = np.stack([twice(a[k][0].transpose(2, 0, 1)) for k in ("ssm_c_re_2", "ssm_c_im_2")], 1)
    out["ssm_c"] = c.reshape(P, 2, 8, 8, 16).transpose(2, 0, 1, 3, 4).reshape(8, P, 256)

    eye = np.eye(P, dtype=f)
    rot1 = np.zeros((P, P), f)
    rot2 = np.zeros((P, P), f)
    for m in range(P):
        if m % 32 < 16:
            rot1[m + 16, m] = -1
        else:
            rot1[m - 16, m] = 1
        if m < 64:
            rot2[m + 64, m] = -1
        else:
            rot2[m - 64, m] = 1
    mask = np.where(np.arange(P)[None, :] <= np.arange(P)[:, None], 0.0, -1e30).astype(f)
    t = np.arange(T)
    freq = (f(10000.0) ** (-np.arange(16, dtype=f) / f(16))).astype(f)
    m = np.arange(P)
    pos = np.where(((m % 64) < 32)[:, None], (t // 64)[None, :], (t % 64)[None, :]).astype(f)
    ang = (pos * freq[m % 16][:, None]).astype(f)
    out["const"] = np.concatenate([eye, np.ones((P, P), f), rot1, rot2, mask, np.cos(ang), np.sin(ang)], 1).astype(f)
    cnt = np.stack([np.minimum(t + h, T) - np.maximum(t - h, 0) for h in (1, 2, 4, 8)])
    out["rcount"] = (f(1) / cnt.astype(f)).reshape(1, 4 * T)
    out["steps"] = t.astype(f).reshape(1, T)
    return out


ARRAYS = ["xin", "cond", "w_mods", "vec", "const", "rcount", "steps", "positions", "ssm_b", "ssm_c",
          "w_in0", "w_small0", "w_out0", "w_in1", "w_small1", "w_out1", "w_in2", "w_glu", "w_abr", "w_sbr",
          "w_out2", "w_up", "w_down"]
LAM_INIT = [0.8 - 0.6 * math.exp(-0.3 * l) for l in range(2)]


class Steps:

    def __init__(self, eng, sem):
        self.eng, self.sem, self.at, self.turn = eng, sem, 0, 0

    def mark(self, ins):
        ins.then_inc(self.sem, 1)
        self.at += 1

    def wait(self, back=0):
        self.eng.wait_ge(self.sem, self.at - back + self.turn)

    def loop(self, i, per_turn, start=0):
        self.turn, self.first, self.per_turn = (i - start) * per_turn, self.at, per_turn

    def end(self, turns):
        assert self.at - self.first == self.per_turn, (self.at - self.first, self.per_turn)
        self.at, self.turn = self.first + turns * self.per_turn, 0


def build(nc, dram, out):
    f32, f32r, i32 = mybir.dt.float32, mybir.dt.float32r, mybir.dt.int32
    ACT, ALU = mybir.ActivationFunctionType, mybir.AluOpType
    AX = mybir.AxisListType.X
    ctx = ExitStack()
    ds = bass.ds

    def at(kib, name, shape, dt=f32):
        if kib:
            with nc.sbuf_tensor(f"skip_{name}", [P, int(kib * KB)], f32):
                with nc.sbuf_tensor(name, shape, dt) as t:
                    return t
        with nc.sbuf_tensor(name, shape, dt) as t:
            return t

    MODW = at(0, "mod_weights", [P, 8, UNIT])
    MOD_POOL = [1, 2, 4, 5, 7]
    HH = at(0, "h_high", [P, KT, T2], f32r)
    HL = at(32, "h_low", [P, KT, T2], f32r)
    WS = at(0, "attention_space", [P, 16384])
    H2H = at(0, "h2_high", [P, KT, T], f32r)
    H2L = at(16, "h2_low", [P, KT, T], f32r)
    WS2 = at(32, "second_space", [P, 8192])
    YAH = at(72, "y_attn_high", [P, 8, T], f32r)
    YAL = at(80, "y_attn_low", [P, 8, T], f32r)
    YSH = at(16, "y_ssm_high", [P, 8, T], f32r)
    YSL = at(24, "y_ssm_low", [P, 8, T], f32r)
    MH = at(32, "merged_high", [P, KT, T], f32r)
    ML = at(48, "merged_low", [P, KT, T], f32r)
    FH = at(32, "ffn_high", [P, FFN, T], f32r)
    FL = at(76, "ffn_low", [P, FFN, T], f32r)
    FT = at(120, "ffn_space", [P, 8, T])
    R2 = at(64, "region2", [P, 12288])
    GSH = at(0, "gelu_high", [P, 8, T], f32r)
    GSL = at(8, "gelu_low", [P, 8, T], f32r)
    R3 = at(112, "region3", [P, 8192])
    RAW = [at(144 + 8 * s, f"raw{s}", [P, UNIT]) for s in range(2)]
    WH = [at(160 + 8 * s, f"w_high{s}", [P, UNIT], f32r) for s in range(2)]
    WL = [at(176 + 8 * s, f"w_low{s}", [P, UNIT], f32r) for s in range(2)]
    o = 192 * KB
    small = {}
    for name, n in [("vec", NVEC), ("const", 9 * P), ("mod", 576), ("rcount", 4 * T), ("gain", 32), ("lam", 8),
                    ("mx", 4), ("nb", 4), ("sums", 4), ("rc", 4), ("ss", 8), ("rr", 8), ("sg", 2)]:
        small[name] = at(o / KB, name + "_sb", [P, n])
        o += -(-n // 8) * 8
    VE, CO, MODF, RCNT, GAIN, LAM = (small[n] for n in ("vec", "const", "mod", "rcount", "gain", "lam"))
    MX, NB, SM, RC, SS, RR, SG = (small[n] for n in ("mx", "nb", "sums", "rc", "ss", "rr", "sg"))
    MOD = MODF[:].rearrange("p (n c) -> p n c", c=3)
    IDENT, ONES, ROT1, ROT2, MASK = (CO[:, P * i:P * (i + 1)] for i in range(5))
    COS, SIN = CO[:, 5 * P:7 * P], CO[:, 7 * P:9 * P]
    XIN = R2[:, 0:8192].rearrange("p (k t) -> p k t", t=T2)
    NT_ = R2[:, 8192:12288].rearrange("p (n t) -> p n t", t=T2)
    COND, JUNK = R3[:, 0:2 * D], R3[:, 3 * D:4 * D]
    PROD = [R3[:, 2 * D:3 * D], at(184, "products", [P, UNIT])[:]]
    CT0 = R3[:, 0:4096].rearrange("p (k t) -> p k t", t=T)
    RES = R3[:, 4096:8192].rearrange("p (k t) -> p k t", t=T)

    def vec(name, n=0, cols=1):
        return VE[:, VEC[name][0] + n:VEC[name][0] + n + cols]

    def vec_at(name, n):
        return VE[:, ds(VEC[name][0] + n, 1)]

    def tile(view, n):
        return view[:, ds(n, 1), :].rearrange("p a t -> p (a t)")

    BANK = [ctx.enter_context(nc.psum_tensor(f"bank{i}", [P, T2], f32)) for i in range(8)]
    L, AUX = BANK[:4], BANK[4:]

    _w, _at = {}, 0
    for _n, _c in [("BST", 512), ("CST", 256), ("WPAD", 2176), ("COEF", 384), ("STEPS", 256), ("PH", 512),
                   ("RN", 512), ("CT", 1024), ("ST", 1024), ("W", 512), ("TM", 512), ("US", 256), ("T12", 256)]:
        _w[_n] = WS2[:, _at:_at + _c]
        _at += _c
    assert _at <= 8192
    BST, CST, WPAD, COEF, STEPS, PH, RN, CTAB, STAB, SW, STM, US, T12 = _w.values()
    POSI = R3[:, 0:T].bitcast(i32)
    bst = BST.rearrange("p (r s n) -> p r s n", r=2, s=2)
    GATE_A = R2[:, 8192:12288].rearrange("p (n t) -> p n t", t=T)
    GATE_S = R3[:, 0:4096].rearrange("p (n t) -> p n t", t=T)
    U2, Q2, K2, V2 = (R2[:, 2048 * i:2048 * (i + 1)].rearrange("p (n t) -> p n t", t=T) for i in range(4))
    JOBS = [[(0, T), (1, T), (2, T2), (3, T2)], [(0, T2), (1, T2)]]
    JOBS2 = [(0, P), (1, T)]

    def att_views(l):
        f = lambda a, n: WS[:, a:a + n]
        two = lambda a: [f(a, T2), f(a + T2, T2)]
        QS, KS, VS, VT = two(0), two(1024), two(2048), two(3072)
        PP = [[f(4096 + 512 * (2 * b + c), T2) for c in range(2)] for b in range(2)]
        AA, AT = two(6144), two(7168)
        return QS, KS, VS, VT, PP, AA, AT, f(8192, T2), f(8704, T2), f(9216, T2)

    M2, M2_TURN = [0, 48, 72, 96], [6, 3, 3]
    COND2 = R2[:, 0:D]
    MODW2 = [[R2[:, a:a + UNIT] for a in starts] for starts in
             ((2048, 4096, 6144), (2048, 6144, 10240), (2048, 4096, 6144))]
    USED1 = 1 + 96

    QKV2 = R2[:, 2048:8192].rearrange("p (n t) -> p n t", t=T)
    US8 = WS2[:, 3584:5632]

    def src_in0(k):
        return tile(XIN, k)

    def src_in1(k):
        v4 = R3[:].rearrange("p (s k t) -> p s k t", s=2, k=KT)
        return v4[:, :, ds(k, 1), :].rearrange("p s a t -> p s (a t)")

    def src_res(k):
        return tile(RES, k)

    def as_src(ap, src):
        return ap.rearrange("p (s t) -> p s t", s=2) if src is src_in1 else ap

    def att2_views():
        f = lambda a, n: WS2[:, a:a + n]
        two = lambda a, n: [f(a, n), f(a + n, n)]
        return dict(QS=two(0, T), KS=two(512, T), VS=two(1024, T), VT=two(1536, T), PP=two(2048, T), AT=two(2560, T),
                    SQ=f(3072, T2), VV=f(3584, T2), R0=f(4096, T2), TT=f(4608, T2), QN=f(5120, T2), SS_=two(5632, T),
                    SQ2=f(6144, T2))

    SC2 = [BANK[5], BANK[7]]
    TR2 = BANK[6]

    sems = {}

    def sem(name):
        if name not in sems:
            sems[name] = ctx.enter_context(nc.semaphore(name))
        return sems[name]

    raw_in = [sem("raw_in0"), sem("raw_in1")]
    high_ready = sem("high_ready")
    split_ready = sem("split_ready")
    halves_done = sem("halves_done")
    bank_free = [sem(f"bank_free{b}") for b in range(4)]

    STREAM = [("w_in0", 0, 36), ("w_small0", 0, 2), ("w_in0", 36, 16), ("w_out0", 0, 16),
              ("w_in1", 0, 36), ("w_small1", 0, 2), ("w_in1", 36, 16), ("w_out1", 0, 16),
              ("w_in2", 0, 64), ("w_glu", 0, 4), ("w_abr", 0, 8), ("w_sbr", 0, 8), ("w_out2", 0, 16),
              ("w_up", 0, 88), ("w_down", 0, 48)]
    UNITS = sum(n for _, _, n in STREAM)
    U_IN, U_SMALL, U_INB, U_OUT = [0, 70], [36, 106], [38, 108], [54, 124]
    U_IN2, U_GLU, U_ABR, U_SBR, U_OUT2, U_UP, U_DOWN = 140, 204, 208, 216, 224, 240, 328
    T_IN, T_OUT, T_IN2, T_GLU, T_ABR, T_SBR, T_OUT2, T_UP, T_DOWN = \
        [0, 68], [52, 120], 136, 200, 208, 224, 240, 256, 344
    assert UNITS == U_DOWN + 48

    def evacuated(eng, tiles):
        for b in range(4):
            eng.wait_ge(bank_free[b], 1 + tiles // 4)

    N_AT = {"in0": 0, "in1": 1, "fin": 2, "b1": 3, "b2": 4}
    S_AT = {"in0": 0, "in1": 1, "b1": 2, "b2": 3}

    def views(l):
        w = T2 if l == 0 else T
        split = lambda r, a, n, t: r[:, a:a + n * t].rearrange("p (n t) -> p n t", t=t)
        if l == 0:
            q, k, v = split(R2, 0, 8, T2), split(R2, 4096, 8, T2), split(R2, 8192, 8, T2)
            up, uc = split(R2, 8192, 4, T2), split(R2, 8192 + 4 * T2, 4, T2)
        else:
            k, v, q = split(R2, 0, 8, T2), split(R2, 4096, 8, T2), split(R2, 8192, 8, T)
            up, uc = split(R2, 4096, 4, T), split(R2, 4096 + 4 * T, 4, T)
        y = split(R3, 0, 16, w)
        return w, q, k, v, up, uc, y

    block = ctx.enter_context(nc.Block())

    @block.sync
    def _(sp):
        sp.dma_start(VE[:], dram["vec"]).then_inc(sem("vec_in"), 16)
        sp.dma_start(CO[:], dram["const"]).then_inc(sem("const_in"), 16)
        sp.dma_start(R2[:, 0:8192], dram["xin"]).then_inc(sem("x_in"), 16)
        sp.dma_start(RCNT[:], dram["rcount"].broadcast_to([P, 4 * T])).then_inc(sem("rcount_in"), 16)

        sp.dma_start(COND, dram["cond"][:, 0:2 * D].broadcast_to([P, 2 * D])).then_inc(sem("cond_in"), 16)
        mods = dram["w_mods"].rearrange("(i s) p n -> i s p n", s=8)
        for s in range(8):
            sp.dma_start(MODW[:, s, :], mods[0, s]).then_inc(sem(f"mod_in{s}"), 16)
        with sp.Fori(1, 12) as i:
            for s in range(8):
                if s in MOD_POOL:
                    sp.wait_ge(sem("mod_sum"), 2 + 5 * i - 4 + MOD_POOL.index(s))
                else:
                    sp.wait_ge(sem("mod_used"), 1 + 8 * i + s - 7)
                sp.dma_start(MODW[:, s, :], mods[ds(i, 1), s].rearrange("a p n -> (a p) n")) \
                    .then_inc(sem(f"mod_in{s}"), 16)

        def modulation2(p, i):
            n = M2_TURN[p]
            mods2 = dram["w_mods"].rearrange("(i q) p n -> i q p n", q=n)
            for q in range(n):
                sp.wait_ge(sem("mod_used"), USED1 + M2[p] + q - 2 + n * i)
                sp.dma_start(MODW2[p][q % 3], mods2[ds((96 + M2[p]) // n + i, 1), q].rearrange("a p n -> (a p) n")) \
                    .then_inc(sem(f"mod_in{q % 3}"), 16)

        def stream(name, first, n, u0):
            w = dram[name].rearrange("(i s) p n -> i s p n", s=2)
            start = 0
            if u0 == 0:
                for s in range(2):
                    sp.dma_start(RAW[s][:], w[0, s]).then_inc(raw_in[s], 16)
                start = 1

            def two(i):
                for s in range(2):
                    sp.wait_ge(split_ready, 2 * (u0 - 1) + 4 * i + 2 * s)
                    sp.dma_start(RAW[s][:], w[ds(first // 2 + i, 1), s].rearrange("a p n -> (a p) n")) \
                        .then_inc(raw_in[s], 16)
            places = ["w_in0", "w_in1", "w_out1"]
            if name in places and first == 0:
                p = places.index(name)
                if start == 0:
                    two(0)
                if name == "w_out1":
                    sp.wait_ge(sem("at1_y"), 1 + 8)
                else:
                    sp.wait_ge(sem("n_hl"), 16 * S_AT[["in0", "in1"][p]] + 2 + KT)
                sp.dma_start(COND2, dram["cond"][:, 2 * D:3 * D].broadcast_to([P, D])).then_inc(sem("cond_in"), 16)
                with sp.Fori(0, 7) as i:
                    two(i + 1)
                    modulation2(p, i)
                start = 8
                if start < n // 2:
                    two(start)
                    start = 9
                modulation2(p, 7)
                if start >= n // 2:
                    return
            with sp.Fori(start, n // 2) as i:
                two(i)

        u = 0
        for name, first, n in STREAM:
            if name == "w_in2":
                stream(name, 0, 10, u)
                w = dram["w_in2"].rearrange("(i s) p n -> i s p n", s=2)
                with sp.Fori(0, 7) as j:
                    for k in range(4):
                        s = k % 2
                        sp.wait_ge(split_ready, 2 * (u + 9 + k) + 8 * j)
                        sp.dma_start(RAW[s][:], w[ds(2 * j + 5 + k // 2, 1), s].rearrange("a p n -> (a p) n")) \
                            .then_inc(raw_in[s], 16)
                    sp.wait_ge(sem("ssm_b"), 1 + 4 * j + 4)
                    sp.dma_start(BST, dram["ssm_b"][ds(j + 1, 1)].rearrange("a p n -> (a p) n")).then_inc(sem("b_in"), 16)
                    sp.wait_ge(sem("ssm_w"), j + 1)
                    sp.dma_start(CST, dram["ssm_c"][ds(j + 1, 1)].rearrange("a p n -> (a p) n")).then_inc(sem("c_in"), 16)
                with sp.Fori(19, 32) as i:
                    for s in range(2):
                        sp.wait_ge(split_ready, 2 * (u - 1) + 4 * i + 2 * s)
                        sp.dma_start(RAW[s][:], w[ds(i, 1), s].rearrange("a p n -> (a p) n")).then_inc(raw_in[s], 16)
            else:
                stream(name, first, n, u)
            u += n
        for c in range(4):
            for s in range(2):
                sp.wait_ge(bank_free[s], 1 + T_DOWN // 4 + 2 * (c + 1))
            sp.dma_start(out[:, 4 * c:4 * c + 4, :], RES[:, 4 * c:4 * c + 4, :]).then_inc(sem("stored"), 16)
        sp.wait_ge(sem("stored"), 64)

    @block.gpsimd
    def _(pool):
        pool.wait_ge(sem("s_ready"), 1)
        with pool.Fori(0, 12) as i:
            for q, s in enumerate(MOD_POOL):
                pool.wait_ge(sem(f"mod_in{s}"), 16 * i + 16)
                pool.wait_ge(sem("mod_sum"), 5 * i + (q + 1 if q else 2))
                nc.gpsimd.tensor_tensor(PROD[q % 2], MODW[:, s, :], COND[:, D:2 * D], ALU.mult) \
                    .then_inc(sem("mod_prod"), 1)
        with pool.Fori(0, UNITS // 2) as i:
            for s in range(2):
                for half in range(2):
                    part = slice(HALF * half, HALF * (half + 1))
                    pool.wait_ge(high_ready, 4 * i + 2 * s + half + 1)
                    nc.gpsimd.tensor_tensor(WL[s][:, part], RAW[s][:, part], WH[s][:, part], ALU.subtract) \
                        .then_inc(split_ready, 1)

    @block.tensor
    def _(pe):
        pe.wait_ge(sem("const_in"), 16)
        for n in [f"at{l}_{m}" for l in range(2) for m in ("pv", "ot")] + ["ssm_b", "ssm_c", "a2_ssum", "a2_pv"]:
            pe.sem_inc(sem(n), 1)
        pe.sem_inc(sem("n_squsd"), 2)

        def norm(name, n):
            for k in range(KT):
                add_squares(name, n, k, k % 2, k == 0, k == KT - 1)

        def add_squares(name, n, k, slot, first, last):
            pe.wait_ge(sem("n_sq"), 16 * N_AT[name] + 1 + k)
            nc.tensor.matmul(AUX[0][:, 0:n], ONES, NT_[:, slot, 0:n], start=first, stop=last) \
                .then_inc(sem("n_squsd"), 1)

        def product(bank, slot, blocks, k0, hi, lo, t0, n, first, last):
            for j, b in enumerate(blocks):
                h, l = (r[:, k0 + j, t0:t0 + n] for r in (hi, lo))
                w = slice(P * b, P * (b + 1))
                nc.tensor.matmul(bank[:, 0:n], WH[slot][:, w], h, start=first and j == 0, stop=False)
                nc.tensor.matmul(bank[:, 0:n], WH[slot][:, w], l, start=False, stop=False)
                end = nc.tensor.matmul(bank[:, 0:n], WL[slot][:, w], h, start=False,
                                       stop=last and j == len(blocks) - 1)
            end.then_inc(halves_done, 1)

        def whole(u, i, per, bank, slot, hi, lo, t0, n):
            for half in range(2):
                pe.wait_ge(split_ready, 2 * u + half + 1 + 2 * per * i)
                product(bank, slot, range(8 * half, 8 * half + 8), 8 * half, hi, lo, t0, n, half == 0, half == 1)

        def tiles(u0, t0_, n_tiles, hi, lo, t0, n):
            with pe.Fori(0, n_tiles // 4) as i:
                for s in range(4):
                    pe.wait_ge(bank_free[s], 1 + t0_ // 4 + i)
                    whole(u0 + s, i, 4, L[s], s % 2, hi, lo, t0, n)

        def residual_tiles(u0, t0_, hi, lo, t0, n, name, width):
            for first, end in ((0, 1), (1, 4)):
                with pe.Fori(first, end) as i:
                    for s in range(4):
                        pe.wait_ge(bank_free[s], 1 + t0_ // 4 + i)
                        whole(u0 + s, i, 4, L[s], s % 2, hi, lo, t0, n)
                        if end == 4 or s >= 2:
                            add_squares(name, width, 4 * i + (s - 2), s % 2, end == 1 and s == 2, False)
            for k in (14, 15):
                add_squares(name, width, k, k % 2, False, k == 15)

        def small(l):
            w, q, k, v, up, uc, y = views(l)
            name = f"cv{l}"
            pe.wait_ge(sem("cv_conv"), l + 1)
            for c in range(4):
                last = nc.tensor.matmul(AUX[0][:, 0:w], ONES, y[:, 4 + c, :], start=c == 0, stop=c == 3)
            last.then_inc(sem("cv_sum"), 1)
            u = U_SMALL[l]
            pe.wait_ge(split_ready, 2 * u + 2)
            pe.wait_ge(sem("cv_pool"), l + 1)
            for g in range(4):
                if g >= 2:
                    pe.wait_ge(sem("cv_pooled"), 4 * l + g - 1)
                for half, wt in enumerate((WH[0], WL[0])):
                    last = nc.tensor.matmul(AUX[2 + g % 2][:, 0:w], wt[:, P * g:P * (g + 1)].bitcast(f32),
                                            y[:, g, :], start=half == 0, stop=half == 1)
                last.then_inc(*((sem("cv_poolmm"), 1) if g < 3 else (halves_done, 2)))
            pe.wait_ge(sem("cv_sq"), l + 1)
            for c in range(4):
                last = nc.tensor.matmul(AUX[1][:, 0:w], ONES, uc[:, c, :], start=c == 0, stop=c == 3)
            last.then_inc(sem("cv_var"), 1)
            pe.wait_ge(split_ready, 2 * u + 4)
            pe.wait_ge(sem("cv_z"), l + 1)
            for n in range(4):
                if n >= 2:
                    pe.wait_ge(sem("cv_pw"), 4 * l + n - 1)
                for c in range(4):
                    for half, wt in enumerate((WH[1], WL[1])):
                        b = 4 * n + c
                        last = nc.tensor.matmul(AUX[n % 2][:, 0:w], wt[:, P * b:P * (b + 1)].bitcast(f32),
                                                uc[:, c, :], start=c == 0 and half == 0, stop=c == 3 and half == 1)
                last.then_inc(*((sem("cv_pwmm"), 1) if n < 3 else (halves_done, 2)))

        def attention(l):
            w, q, k, v, up, uc, y = views(l)
            nm = f"at{l}"
            jobs = JOBS[l]
            J = len(jobs)
            QS, KS, VS, VT, PP, AA, AT, OC, TR, SD = att_views(l)
            with pe.Fori(0, 4) as i:
                for e in range(2):
                    h = 2 * i + e
                    if e == 0:
                        pe.wait_ge(sem(nm + "_oc"), 1 + 2 * i)
                    else:
                        pe.wait_ge(sem(nm + "_qk"), h)
                    nc.tensor.matmul(BANK[4][:, 0:T], ROT1, tile(q, h)[:, w - T:w], start=True, stop=True)
                    nc.tensor.matmul(BANK[4][:, T:T2], ROT1, tile(k, h)[:, T:T2], start=True, stop=True) \
                        .then_inc(sem(nm + "_rot"), 1)
                    pe.wait_ge(sem(nm + "_vs"), h + 1)
                    if e == 0:
                        pe.wait_ge(sem(nm + "_y"), 1 + 2 * i)
                    else:
                        pe.wait_ge(sem(nm + "_vt"), h)
                    for c in range(4):
                        last = nc.tensor.transpose(BANK[5][:, P * c:P * (c + 1)], VS[e][:, P * c:P * (c + 1)], IDENT)
                    last.then_inc(sem(nm + "_vtr"), 1)

                def scores(g):
                    e, (qt, nk) = g // J, jobs[g % J]
                    if g == 0:
                        pe.wait_ge(sem(nm + "_qk"), 2 * i + 1)
                    if g == J:
                        pe.wait_ge(sem(nm + "_qk"), 2 * i + 2)
                    if g >= 2:
                        pe.wait_ge(sem(nm + "_exp"), 2 * J * i + g - 1)
                    for c in range(2):
                        r = slice(64 * c, 64 * c + 64)
                        last = nc.tensor.matmul(BANK[2 * (g % 2) + c][:, 0:nk], QS[e][r, P * qt:P * (qt + 1)],
                                                KS[e][r, 0:nk], start=True, stop=True)
                    last.then_inc(sem(nm + "_sc"), 1)

                def out_back(e):
                    pe.wait_ge(sem(nm + "_on"), 1 + 2 * i + e + 1)
                    if e == 1:
                        pe.wait_ge(sem(nm + "_y"), 1 + 2 * i + 1)
                    for jj in range(J):
                        last = nc.tensor.transpose(BANK[5][:, P * jj:P * (jj + 1)], OC[:, P * jj:P * (jj + 1)], IDENT)
                    last.then_inc(sem(nm + "_ot"), 1)

                scores(0)
                scores(1)
                for g in range(2 * J):
                    e, (qt, nk) = g // J, jobs[g % J]
                    pe.wait_ge(sem(nm + "_comb"), 2 * J * i + g + 1)
                    pe.wait_ge(sem(nm + "_at"), 1 + 2 * J * i + g)
                    for c in range(nk // P):
                        last = nc.tensor.transpose(BANK[6][:, P * c:P * (c + 1)], AA[g % 2][:, P * c:P * (c + 1)], IDENT)
                    last.then_inc(sem(nm + "_tr"), 1)
                    if g + 2 < 2 * J:
                        scores(g + 2)
                    pe.wait_ge(sem(nm + "_at"), 1 + 2 * J * i + g + 1)
                    if g % J == 0:
                        pe.wait_ge(sem(nm + "_vt"), 2 * i + e + 1)
                    if g == 0:
                        pe.wait_ge(sem(nm + "_oc"), 1 + 2 * i)
                    ob = BANK[7] if e == 0 else BANK[4]
                    for c in range(nk // P):
                        last = nc.tensor.matmul(ob[:, P * (g % J):P * (g % J + 1)], AT[g % 2][:, P * c:P * (c + 1)],
                                                VT[e][:, P * c:P * (c + 1)], start=c == 0, stop=c == nk // P - 1)
                    last.then_inc(sem(nm + "_pv"), 1)
                    if g == J + 1:
                        out_back(0)
                out_back(1)

        norm("in0", T2)
        pe.wait_ge(sem("lam_prod"), 1)
        nc.tensor.matmul(AUX[1][:, 0:4], ONES[0:64, :], LAM[0:64, 0:4], start=True, stop=True) \
            .then_inc(sem("lam_sum"), 1)
        for l in range(2):
            w = T2 if l == 0 else T
            t0 = T2 - w
            pe.wait_ge(sem("n_hl"), 16 * S_AT[f"in{l}"] + 2 + KT)
            n_in = T_IN[l]
            if l == 0:
                tiles(0, 0, 36, HH, HL, 0, T2)
            else:
                tiles(U_IN[1], n_in, 28, HH, HL, T, T)
                tiles(U_IN[1] + 28, n_in + 28, 8, HH, HL, 0, T2)
            small(l)
            tiles(U_INB[l], n_in + 36, 8, HH, HL, 0, T2)
            tiles(U_INB[l] + 8, n_in + 44, 8, HH, HL, t0, w)
            evacuated(pe, n_in + 52)
            pe.wait_ge(sem("cv_pw"), 4 * l + 4)
            pe.wait_ge(sem("cv_pooled"), 4 * l + 4)
            attention(l)
            pe.wait_ge(sem(f"ys{l}_lo"), 16 // 4)
            pe.wait_ge(sem(f"at{l}_exp"), 8 * len(JOBS[l]))
            residual_tiles(U_OUT[l], T_OUT[l], HH, HL, t0, w, ("in1", "fin")[l], (T2, T)[l])

        norm("b1", T)
        pe.wait_ge(sem("n_hl"), 16 * S_AT["b1"] + 2 + KT)
        tiles(U_IN2, T_IN2, 8, H2H, H2L, 0, T)

        def inputs(j, a):
            pe.wait_ge(sem("ssm_read"), 1 + 4 * j + a)
            for s in range(2):
                for r in range(2):
                    last = nc.tensor.matmul(AUX[s][:, T * r:T * (r + 1)], bst[32 * a:32 * a + 32, r, s, :],
                                            US[32 * a:32 * a + 32, :], start=True, stop=True)
            last.then_inc(sem("ssm_b"), 1)

        def outputs(j, a):
            pe.wait_ge(sem("ssm_x"), 4 * j + a + 1)
            for ver, x in enumerate((STM, SW)):
                for r in range(2):
                    g = 2 * a + r
                    last = nc.tensor.matmul(AUX[2][:, 0:T], WPAD[:, 1024 * ver + P * g:1024 * ver + P * (g + 1)],
                                            x[:, T * r:T * (r + 1)], start=a == 0 and ver == 0 and r == 0,
                                            stop=a == 3 and ver == 1 and r == 1)
            last.then_inc(sem("ssm_c"), 1)

        def step_start(j):
            pe.wait_ge(sem("b_in"), 16 * j + 16)
            pe.wait_ge(sem("us_ready"), j + 1)
            pe.wait_ge(sem("ssm_y"), 1 + j)
            pe.wait_ge(sem("ssm_w"), j + 1)

        with pe.Fori(0, 8) as j:
            step_start(j)
            inputs(j, 0)
            for a in range(4):
                pe.wait_ge(bank_free[a], 1 + (T_IN2 + 8) // 4 + j)
                whole(U_IN2 + 8 + a, j, 4, L[a], a % 2, H2H, H2L, 0, T)
                if a < 3:
                    inputs(j, a + 1)
                outputs(j, a)

        v = att2_views()
        pe.wait_ge(sem("ssm_y"), 1 + 8)

        def heads2(i, gates):
            def gate_tile(t):
                if gates:
                    pe.wait_ge(bank_free[t % 4], 1 + (T_IN2 + 40) // 4 + t // 4 + 2 * i)
                    whole(U_IN2 + 40 + t, i, 8, L[t % 4], t % 2, H2H, H2L, 0, T)

            for e in range(2):
                h = 2 * i + e
                pe.wait_ge(sem("a2_sq"), h + 1)
                pe.wait_ge(sem("a2_vv"), 1 + h)
                nc.tensor.matmul(BANK[5][:, 0:T2], ONES, v["SQ"], start=True, stop=True).then_inc(sem("a2_ssum"), 1)
                pe.wait_ge(sem("a2_vs"), h + 1)
                for c in range(2):
                    last = nc.tensor.transpose(BANK[6][:, P * c:P * (c + 1)], v["VS"][e][:, P * c:P * (c + 1)], IDENT)
                last.then_inc(sem("a2_vtr"), 1)
                gate_tile(e)
                pe.wait_ge(sem("a2_qn"), h + 1)
                pe.wait_ge(sem("a2_qk"), 1 + h)
                if e == 0:
                    pe.wait_ge(sem("a2_yl"), 1 + 2 * i)
                nc.tensor.matmul(BANK[4][:, 0:T2], ROT2, v["QN"], start=True, stop=True).then_inc(sem("a2_rot"), 1)
                pe.wait_ge(sem("a2_vt"), h + 1)
            gate_tile(2)

            def scores2(g):
                e, (qt, nk) = g // 2, JOBS2[g % 2]
                pe.wait_ge(sem("a2_qk"), 1 + 2 * i + e + 1)
                if g >= 2:
                    pe.wait_ge(sem("a2_ms"), 4 * i + g - 1)
                nc.tensor.matmul(SC2[g % 2][:, 0:nk], v["QS"][e][:, P * qt:P * (qt + 1)], v["KS"][e][:, 0:nk],
                                 start=True, stop=True).then_inc(sem("a2_sc"), 1)

            scores2(0)
            scores2(1)
            for g in range(4):
                e, (qt, nk) = g // 2, JOBS2[g % 2]
                pe.wait_ge(sem("a2_comb"), 4 * i + g + 1)
                for c in range(nk // P):
                    last = nc.tensor.transpose(TR2[:, P * c:P * (c + 1)], v["PP"][g % 2][:, P * c:P * (c + 1)], IDENT)
                last.then_inc(sem("a2_tr"), 1)
                if g + 2 < 4:
                    scores2(g + 2)
                gate_tile(3 + g)
                pe.wait_ge(sem("a2_at"), 4 * i + g + 1)
                if g % 2 == 0:
                    pe.wait_ge(sem("a2_yl"), 1 + 2 * i + e)
                for c in range(nk // P):
                    last = nc.tensor.matmul(BANK[4][:, P * qt:P * (qt + 1)], v["VT"][e][:, P * c:P * (c + 1)],
                                            v["AT"][g % 2][:, P * c:P * (c + 1)], start=c == 0, stop=c == nk // P - 1)
                last.then_inc(sem("a2_pv"), 1)
            gate_tile(7)

        for first, end in ((0, 3), (3, 4)):
            with pe.Fori(first, end) as i:
                heads2(i, end == 3)

        def pair_tiles(u0, t0_, units, hi, lo):
            with pe.Fori(0, units // 2) as i:
                for r in range(2):
                    for b in range(2):
                        s = 2 * r + b
                        pe.wait_ge(bank_free[s], 1 + t0_ // 4 + i)
                        pe.wait_ge(split_ready, 2 * (u0 + r) + b + 1 + 4 * i)
                        product(L[s], r, range(8 * b, 8 * b + 8), 0, hi, lo, 0, T, True, True)

        pe.wait_ge(sem("gelu_lo"), 1)
        pe.wait_ge(sem("a2_yl"), 1 + 8)
        pair_tiles(U_GLU, T_GLU, 4, GSH, GSL)
        pair_tiles(U_ABR, T_ABR, 8, YAH, YAL)
        pe.wait_ge(sem("ys_lo"), 4)
        pair_tiles(U_SBR, T_SBR, 8, YSH, YSL)
        pe.wait_ge(sem("m_lo"), 16)
        residual_tiles(U_OUT2, T_OUT2, MH, ML, 0, T, "b2", T)

        pe.wait_ge(sem("n_hl"), 16 * S_AT["b2"] + 2 + KT)
        tiles(U_UP, T_UP, 2 * FFN, H2H, H2L, 0, T)
        pe.wait_ge(sem("ffn_lo"), FFN)
        with pe.Fori(0, 8) as i:
            for r in range(6):
                s, third = r // 3, r % 3
                if third == 0:
                    pe.wait_ge(bank_free[s], 1 + T_DOWN // 4 + i)
                for half in range(2):
                    pe.wait_ge(split_ready, 2 * (U_DOWN + r) + half + 1 + 12 * i)
                    k0 = 16 * third + 8 * half
                    product(L[s], r % 2, range(8 * half, 8 * half + min(8, FFN - k0)), k0, FH, FL, 0, T,
                            k0 == 0, k0 + 8 >= FFN)

    @block.scalar
    def _(act):
        own = Steps(act, sem("act_own"))

        def run(out, in_, func, bias=None, scale=None, accum=None):
            kw = {}
            if bias is not None:
                kw["bias"] = bias
            if scale is not None:
                kw["scale"] = scale
            if accum is not None:
                kw["accum_out"] = accum
            return nc.scalar.activation(out, in_, func, **kw)

        def high(u, slot, half, i=0, per=0):
            part = slice(HALF * half, HALF * (half + 1))
            act.wait_ge(raw_in[slot], 16 * (u // 2 + 1) + 8 * per * i)
            run(WH[slot][:, part], RAW[slot][:, part], ACT.Copy).then_inc(high_ready, 1)

        def ahead(u, slot, i=0, per=0, between=None):
            act.wait_ge(halves_done, 2 * u + 1 + 2 * per * i)
            high(u + 2, slot, 0, i, per)
            act.wait_ge(halves_done, 2 * u + 2 + 2 * per * i)
            if between:
                between()
            high(u + 2, slot, 1, i, per)

        def squares(name, src, n, i):
            for s in range(2):
                act.wait_ge(sem("n_squsd"), 16 * N_AT[name] + 2 * i + s + 1)
                run(as_src(NT_[:, s, 0:n], src), src(2 * i + s), ACT.Square).then_inc(sem("n_sq"), 1)

        def root(name, n):
            act.wait_ge(sem("n_squsd"), 16 * N_AT[name] + 2 + KT)
            run(NT_[:, 6, 0:n], AUX[0][:, 0:n], ACT.Sqrt, bias=vec("eps"), scale=1.0 / D).then_inc(sem("n_std"), 1)

        def norm(name, src, n, halves, final=None):
            if name == "b1":
                with act.Fori(0, KT // 2) as i:
                    squares(name, src, n, i)
                root(name, n)
            act.wait_ge(sem("n_gain"), N_AT[name] + 1)
            with act.Fori(0, KT // 2) as i:
                for s in range(2):
                    k = 2 * i + s
                    act.wait_ge(sem("n_tt"), 16 * N_AT[name] + k + 1)
                    if final:
                        run(src(k), NT_[:, 2 + s, 0:n], ACT.Copy, scale=vec_at(final, k)) \
                            .then_inc(sem("n_hf"), 1)
                        continue
                    act.wait_ge(sem("n_hl"), 16 * S_AT[name] + k + 1)
                    for j, (t0, shift, col) in enumerate(halves):
                        last = run(NT_[:, 4 + s, t0:t0 + T], NT_[:, 2 + s, t0:t0 + T], ACT.Identity,
                                   bias=MODF[:, ds(3 * k + 3 * shift + col, 1)], scale=GAIN[:, ds(2 * k + j, 1)])
                    last.then_inc(sem("n_hf"), 1)
                    act.wait_ge(sem("n_hf"), 16 * N_AT[name] + k + 3)
                    hi = HH if n == T2 else H2H
                    run(tile(hi, k), NT_[:, 4 + s, 0:n], ACT.Copy).then_inc(sem("n_hh"), 1)

        def evac(u0, tiles_, w, func, dst, d0):
            with act.Fori(0, tiles_ // 4) as i:
                for s in range(4):
                    ahead(u0 + s, s % 2, i, 4, lambda: run(tile(dst, 4 * i + s + d0)[:, 0:w], L[s][:, 0:w], func)
                          .then_inc(bank_free[s], 1))

        def silu_cond2(p):
            act.wait_ge(sem("cond_in"), 16 * (p + 2))
            run(COND2, COND2, ACT.Silu).then_inc(sem("s_ready"), 1)

        def highs(u0, n):
            with act.Fori(0, n // 2) as i:
                for s in range(2):
                    ahead(u0 + s, s, i, 2)

        def residual_highs(u0, t0_, name, src, n):
            def square(i, s):
                act.wait_ge(bank_free[s % 4], 1 + t0_ // 4 + i + (1 if s >= 0 else 0))
                act.wait_ge(sem("n_squsd"), 16 * N_AT[name] + 1 + s + 4 * i)
                run(as_src(NT_[:, s % 2, 0:n], src), src(4 * i + s), ACT.Square).then_inc(sem("n_sq"), 1)

            for first, end in ((0, 1), (1, 4)):
                with act.Fori(first, end) as i:
                    for s in range(4):
                        ahead(u0 + s, s % 2, i, 4)
                        if s or first:
                            square(i, s - 1)
            square(3, 3)
            root(name, n)

        def attention(l):
            w, q, k, v, up, uc, y = views(l)
            nm, jobs = f"at{l}", JOBS[l]
            J = len(jobs)
            QS, KS, VS, VT, PP, AA, AT, OC, TR, SD = att_views(l)
            with act.Fori(0, 4) as i:
                for e in range(2):
                    h = 2 * i + e
                    act.wait_ge(sem(nm + "_pv"), 1 + 2 * J * i)
                    if l == 0:
                        run(QS[e][:, 0:T], tile(q, h)[:, 0:T], ACT.Copy)
                    run(KS[e][:, 0:T], tile(k, h)[:, 0:T], ACT.Copy)
                    run(VS[e], tile(v, h), ACT.Copy).then_inc(sem(nm + "_vs"), 1)
                for e in range(2):
                    act.wait_ge(sem(nm + "_vtr"), 2 * i + e + 1)
                    run(VT[e], BANK[5][:, 0:T2], ACT.Copy).then_inc(sem(nm + "_vt"), 1)

                def exps(g):
                    nk = jobs[g % J][1]
                    act.wait_ge(sem(nm + "_nb"), 2 * J * i + g + 1)
                    b = g % 2
                    for c in range(2):
                        last = run(PP[b][c][:, 0:nk], BANK[2 * b + c][:, 0:nk], ACT.Exp, bias=NB[:, 2 * b + c:2 * b + c + 1],
                                   scale=0.125, accum=SM[:, 2 * b + c:2 * b + c + 1])
                    last.then_inc(sem(nm + "_exp"), 1)

                def head(e):
                    ob = BANK[7] if e == 0 else BANK[4]
                    act.wait_ge(sem(nm + "_pv"), 1 + 2 * J * i + J * (e + 1))
                    act.wait_ge(sem(nm + "_on"), 1 + 2 * i + e)
                    for jj in range(J):
                        last = run(SD[:, P * jj:P * (jj + 1)], ob[:, P * jj:P * (jj + 1)], ACT.Square, accum=SS[:, jj:jj + 1])
                    own.mark(last)
                    act.wait_ge(sem(nm + "_ot"), 1 + 2 * i + e)
                    run(OC[:, 0:P * J], ob[:, 0:P * J], ACT.Copy).then_inc(sem(nm + "_oc"), 1)
                    own.wait()
                    own.mark(run(SS[:, 4:4 + J], SS[:, 0:J], ACT.Ln, bias=vec("eps"), scale=1.0 / P))
                    own.wait()
                    run(RR[:, 0:J], SS[:, 4:4 + J], ACT.Exp, scale=-0.5).then_inc(sem(nm + "_rr"), 1)

                own.loop(i, 4)
                exps(0)
                exps(1)
                for g in range(2 * J):
                    nk = jobs[g % J][1]
                    act.wait_ge(sem(nm + "_tr"), 2 * J * i + g + 1)
                    run(AT[g % 2][:, 0:nk], BANK[6][:, 0:nk], ACT.Copy).then_inc(sem(nm + "_at"), 1)
                    if g + 2 < 2 * J:
                        exps(g + 2)
                    if g == J:
                        head(0)
                head(1)
            own.end(4)

        def small(l):
            w, q, k, v, up, uc, y = views(l)
            name = f"cv{l}"
            act.wait_ge(sem("cv_cen"), l + 1)
            run(uc[:, :, 0:w], y[:, 4:8, 0:w], ACT.Square).then_inc(sem("cv_sq"), 1)
            act.wait_ge(sem("cv_var"), l + 1)
            run(up[:, 0, :], AUX[1][:, 0:w], ACT.Sqrt, bias=vec("eps"), scale=1.0 / 512).then_inc(sem("cv_std"), 1)
            act.wait_ge(sem("cv_nrm"), l + 1)
            for c in range(4):
                last = run(uc[:, c, :], y[:, 4 + c, :], ACT.Silu, bias=vec("ln_b", 4 * l + c), scale=vec("ln_g", 4 * l + c))
            last.then_inc(sem("cv_z"), 1)
            for r in range(2):
                ahead(U_SMALL[l] + r, r)

        for b in range(4):
            act.sem_inc(bank_free[b], 1)
        for n in [f"at{l}_{m}" for l in range(2) for m in ("oc", "at")] + ["tables"]:
            act.sem_inc(sem(n), 1)
        act.sem_inc(sem("n_hf"), 2)
        act.wait_ge(sem("vec_in"), 16)
        act.wait_ge(sem("cond_in"), 16)
        run(COND, COND, ACT.Silu).then_inc(sem("s_ready"), 1)
        act.sem_inc(sem("mod_sum"), 2)
        act.wait_ge(sem("mod_zero"), 1)
        act.wait_ge(sem("x_in"), 16)
        for first, end in ((0, KT // 2), (KT // 2, 12)):
            with act.Fori(first, end) as i:
                for q, s in enumerate(MOD_POOL):
                    act.wait_ge(sem("mod_used"), 1 + 8 * i + s + 1)
                    act.wait_ge(sem("mod_prod"), 5 * i + q + 1)
                    run(PROD[q % 2], PROD[q % 2], ACT.Copy, accum=MODF[:, ds(24 * i + 3 * s + 1, 1)]).then_inc(sem("mod_sum"), 1)
                if first == 0:
                    squares("in0", src_in0, T2, i)
            if first == 0:
                root("in0", T2)
        for u in range(2):
            for half in range(2):
                high(u, u, half)
        for l in range(2):
            w, q, k, v, up, uc, y = views(l)
            if l == 0:
                act.wait_ge(sem("mod_out"), 1)
                norm("in0", src_in0, T2, [(0, 0, 1), (T, 0, 0)])
                act.wait_ge(sem("lam_sum"), 1)
                run(LAM[:, 4:8], AUX[1][:, 0:4], ACT.Exp).then_inc(sem("lam_exp"), 1)
            else:
                act.wait_ge(sem("res1"), 16)
                norm("in1", src_in1, T2, [(0, 48, 1), (T, 48, 0)])
            u = U_IN[l]
            silu_cond2(l)
            evac(u + A0_, 4, w, ACT.Copy, uc, 0)
            evac(u + B0_, 4, w, ACT.Sigmoid, y, 0)
            evac(u + UP_, 4, w, ACT.Copy, up, 0)
            evac(u + GP_, 4, w, ACT.Silu, y, 8)
            evac(u + GC_, 4, w, ACT.Silu, y, 12)
            act.wait_ge(sem("mod_used"), USED1 + M2[l + 1])
            evac(u + Q_, 8, w, ACT.Copy, q, 0)
            evac(u + K_, 8, T2, ACT.Copy, k, 0)
            small(l)
            evac(U_INB[l], 8, T2, ACT.Copy, v, 0)
            act.wait_ge(sem("cv_pw"), 4 * l + 4)
            evac(U_INB[l] + 8, 8, w, ACT.Silu, y, 0)
            attention(l)
            act.wait_ge(sem(f"at{l}_y"), 1 + 8)
            if l == 0:
                act.dma_start(R2[:, 0:8192], dram["xin"]).then_inc(sem("x_in"), 16)
            for c in range(4):
                run(HH[:, 4 * c:4 * c + 4, T2 - w:T2], y[:, 4 * c:4 * c + 4, :], ACT.Copy).then_inc(sem(f"ys{l}_hi"), 1)
            if l == 1:
                silu_cond2(2)
            residual_highs(U_OUT[l], T_OUT[l], *(("in1", src_in1, T2), ("fin", src_res, T))[l])

        act.wait_ge(sem("res2"), 16)
        norm("fin", src_res, T, [], final="final_g")
        act.wait_ge(sem("n_hf"), 16 * N_AT["fin"] + 2 + KT)
        act.wait_ge(sem("mod_out"), 2)
        norm("b1", src_res, T, [(0, 96, 2)])

        act.wait_ge(sem("n_hl"), 16 * S_AT["b1"] + 2 + KT)
        act.dma_start(POSI, dram["positions"].broadcast_to([P, T])).then_inc(sem("pos_in"), 16)
        act.dma_start(STEPS, dram["steps"].broadcast_to([P, T])).then_inc(sem("steps_in"), 16)
        act.dma_start(BST, dram["ssm_b"][0]).then_inc(sem("b_in"), 16)
        act.dma_start(CST, dram["ssm_c"][0]).then_inc(sem("c_in"), 16)

        act.wait_ge(sem("ang"), 1)
        run(SIN, NT_[:, 0, 0:T], ACT.Sin).then_inc(sem("rope_sin"), 1)
        own.mark(run(NT_[:, 1, 0:T], NT_[:, 0, 0:T], ACT.Abs))
        own.wait()
        run(COS, NT_[:, 1, 0:T], ACT.Sin, bias=vec("half_pi"), scale=-1.0).then_inc(sem("rope_cos"), 1)
        act.wait_ge(sem("th"), 1)
        par = CTAB.rearrange("p (n g) -> p n g", g=64)
        own.mark(run(par[:, 4, :], par[:, 0, :], ACT.Abs))
        run(par[:, 1, :], par[:, 0, :], ACT.Sin)
        run(par[:, 3, :], par[:, 0, :], ACT.Sin, scale=0.5)
        own.wait()
        run(par[:, 2, :], par[:, 4, :], ACT.Sin, bias=vec("half_pi"), scale=-1.0).then_inc(sem("trig"), 1)

        evac(U_IN2, 8, T, ACT.Copy, U2, 0)

        def tables(q, slot, i=None):
            sl = slice(512 * slot, 512 * slot + 512)
            act.wait_ge(sem("phase"), q + 1)
            run(STAB[:, sl], PH, ACT.Sin, scale=vec("sign2pi"))
            own.mark(run(RN, PH, ACT.Abs))
            own.wait()
            run(CTAB[:, sl], RN, ACT.Sin, bias=vec("half_pi"), scale=-2 * math.pi).then_inc(sem("tables"), 1)

        def stage_u(j):
            act.wait_ge(sem("ssm_b"), 1 + 4 * j)
            run(US, tile(U2, j), ACT.Copy).then_inc(sem("us_ready"), 1)

        evacuated(act, T_IN2 + 8)
        stage_u(0)
        tables(0, 0)
        for j0, j1, func, dst, d0 in ((0, 6, ACT.Copy, QKV2, 0), (6, 7, ACT.Sigmoid, GATE_A, 0),
                                      (7, 8, ACT.Sigmoid, GATE_A, 4)):
            with act.Fori(j0, j1) as j:
                own.loop(j, 3 if j1 == 8 else 4, j0)
                for a in range(4):
                    if a < 3 or j1 < 8:
                        tables(4 * j + a + 1, (a + 1) % 2)
                    if a == 3 and j1 < 8:
                        stage_u(j + 1)
                    ahead(U_IN2 + 8 + a, a % 2, j, 4, lambda: run(tile(dst, d0 + a + 4 * (j - j0)), L[a][:, 0:T], func)
                          .then_inc(bank_free[a], 1))
            own.end(j1 - j0)
        act.wait_ge(sem("gelu_in"), 1)
        run(US8, US8, ACT.Sigmoid, scale=2 * math.sqrt(2 / math.pi)).then_inc(sem("gelu_sig"), 1)

        v = att2_views()
        act.wait_ge(sem("gelu_g"), 1)

        def heads2(i, i0, dst, d0):
            own.loop(i, 2, i0)

            def gate_tile(t):
                if dst is not None:
                    ahead(U_IN2 + 40 + t, t % 2, i, 8, lambda: run(tile(dst, d0 + t + 8 * (i - i0)), L[t % 4][:, 0:T],
                                                                   ACT.Sigmoid).then_inc(bank_free[t % 4], 1))

            def squares(e):
                h = 2 * i + e
                act.wait_ge(sem("a2_ssum"), 1 + h)
                run(v["SQ"][:, 0:T], tile(Q2, h), ACT.Square)
                run(v["SQ"][:, T:T2], tile(K2, h), ACT.Square).then_inc(sem("a2_sq"), 1)
                act.wait_ge(sem("a2_pv"), 1 + 4 * i)
                run(v["VS"][e], tile(V2, h), ACT.Copy).then_inc(sem("a2_vs"), 1)

            squares(0)
            for e in range(2):
                h = 2 * i + e
                act.wait_ge(sem("a2_vv"), 1 + h + 1)
                own.mark(run(v["SQ2"], v["VV"], ACT.Ln))
                own.wait()
                run(v["R0"], v["SQ2"], ACT.Exp, scale=-0.5).then_inc(sem("a2_r0"), 1)
                act.wait_ge(sem("a2_vtr"), h + 1)
                run(v["VT"][e], BANK[6][:, 0:T], ACT.Copy).then_inc(sem("a2_vt"), 1)
                if e == 0:
                    squares(1)
                gate_tile(e)
            gate_tile(2)

            def exps2(g):
                nk = JOBS2[g % 2][1]
                act.wait_ge(sem("a2_nb"), 4 * i + g + 1)
                run(v["PP"][g % 2][:, 0:nk], v["SS_"][g % 2][:, 0:nk], ACT.Exp, bias=NB[:, g % 2:g % 2 + 1],
                    accum=SM[:, g % 2:g % 2 + 1]).then_inc(sem("a2_exp"), 1)

            exps2(0)
            exps2(1)
            for g in range(4):
                nk = JOBS2[g % 2][1]
                act.wait_ge(sem("a2_tr"), 4 * i + g + 1)
                run(v["AT"][g % 2][:, 0:nk], TR2[:, 0:nk], ACT.Copy).then_inc(sem("a2_at"), 1)
                if g + 2 < 4:
                    exps2(g + 2)
                gate_tile(3 + g)
                if g % 2 == 1:
                    act.wait_ge(sem("a2_pv"), 1 + 4 * i + g + 1)
                    run(tile(YAH, 2 * i + g // 2), BANK[4][:, 0:T], ACT.Copy).then_inc(sem("a2_yh"), 1)
            gate_tile(7)

        for first, end, dst, d0 in ((0, 1, GATE_A, 8), (1, 3, GATE_S, 0), (3, 4, None, 0)):
            with act.Fori(first, end) as i:
                heads2(i, first, dst, d0)
            own.end(end - first)

        run(GSH[:], U2, ACT.Copy).then_inc(sem("gelu_hi"), 1)
        with act.Fori(0, 2) as i:
            for r in range(2):
                def gates():
                    for b in range(2):
                        n = 4 * i + 2 * r + b
                        run(tile(V2, n), L[2 * r + b][:, 0:T], ACT.Sigmoid, bias=vec_at("b_glu", n)) \
                            .then_inc(bank_free[2 * r + b], 1)
                ahead(U_GLU + r, r, i, 2, gates)
        for c in range(4):
            act.wait_ge(sem("ys_mul"), c + 1)
            run(YSH[:, 2 * c:2 * c + 2, :], V2[:, 2 * c:2 * c + 2, :], ACT.Copy).then_inc(sem("ys_hi"), 1)
        highs(U_ABR, 16)
        with act.Fori(0, KT) as k:
            act.wait_ge(sem("m_sum"), k + 1)
            run(tile(MH, k), tile(GATE_A, k), ACT.Copy).then_inc(sem("m_hi"), 1)
        residual_highs(U_OUT2, T_OUT2, "b2", src_res, T)

        act.wait_ge(sem("res3"), 16)
        norm("b2", src_res, T, [(0, 144, 2)])
        with act.Fori(0, FFN // 2) as i:
            for r in range(4):
                m, half = r // 2, r % 2
                n = 4 * i + r
                ahead(U_UP + r, r % 2, i, 4, lambda: run(
                    FT[:, 2 * m + half, :], L[r][:, 0:T], ACT.Identity, bias=vec_at("conv_b", n),
                    scale=vec_at("conv_w", 3 * n + 2)).then_inc(sem("ffn_mid"), 1))
                if half == 1:
                    act.wait_ge(sem("ffn_conv"), 2 * (2 * i + m) + 2)
                    run(FT[:, 2 * m + 1, :], FT[:, 2 * m + 1, :], ACT.Silu).then_inc(sem("ffn_silu"), 1)
                    act.wait_ge(sem("ffn_prod"), 2 * i + m + 1)
                    run(tile(FH, 2 * i + m), FT[:, 4 + m, :], ACT.Copy).then_inc(sem("ffn_hi"), 1)
        with act.Fori(0, 7) as i:
            for r in range(6):
                ahead(U_DOWN + r, r % 2, i, 6)
        for r in range(4):
            ahead(U_DOWN + 42 + r, r % 2)

    @block.vector
    def _(dve):
        V = nc.vector
        own = Steps(dve, sem("dve_own"))

        def mul(o_, a, b):
            return V.tensor_tensor(o_, a, b, ALU.mult)

        def sub(o_, a, b):
            return V.tensor_tensor(o_, a, b, ALU.subtract)

        def add(o_, a, b):
            return V.tensor_tensor(o_, a, b, ALU.add)

        def seq(ins):
            own.mark(ins)
            own.wait()

        def norm(name, src, n, halves=(), gname=None, g0=0, final=False):
            hi, lo = (HH, HL) if n == T2 else (H2H, H2L)
            for j, (scale, col) in enumerate(halves):
                gain = GAIN[:].rearrange("p (k j) -> p k j", j=2)[:, :, j]
                last = V.scalar_tensor_tensor(gain, MOD[:, scale:scale + KT, col], 1.0, vec(gname, g0, KT), ALU.add, ALU.mult)
            if halves:
                last.then_inc(sem("n_gain"), 1)
            else:
                dve.sem_inc(sem("n_gain"), 1)
            dve.wait_ge(sem("n_std"), N_AT[name] + 1)
            seq(V.reciprocal(NT_[:, 7, 0:n], NT_[:, 6, 0:n]))

            def scaled(k, s):
                dve.wait_ge(sem("n_hf"), 16 * N_AT[name] + 1 + k)
                mul(as_src(NT_[:, 2 + s, 0:n], src), src(k), as_src(NT_[:, 7, 0:n], src)).then_inc(sem("n_tt"), 1)

            def low(k, s):
                if not final:
                    dve.wait_ge(sem("n_hh"), 16 * S_AT[name] + 1 + k)
                    sub(tile(lo, k), NT_[:, 4 + s, 0:n], tile(hi, k)).then_inc(sem("n_hl"), 1)

            for s in range(2):
                scaled(s, s)
            with dve.Fori(0, KT // 2 - 1) as i:
                for s in range(2):
                    scaled(2 * i + (s + 2), s)
                    low(2 * i + s, s)
            for s in range(2):
                low(KT - 2 + s, s)

        def small(l):
            w, q, k, v, up, uc, y = views(l)
            S = w // T
            name, tiles_ = f"cv{l}", T_IN[l]
            st = lambda ap: ap.rearrange("p (s t) -> p s t", s=S)
            evacuated(dve, tiles_ + 8)
            seq(mul(uc, uc, y[:, 0:4, :]))
            wdw, bdw = VEC["w_dw"][0] + l * 124, VEC["b_dw"][0] + 4 * l
            for c in range(4):
                own.mark(V.tensor_scalar(y[:, 4 + c, :], uc[:, c, :], VE[:, wdw + 31 * c + 15:wdw + 31 * c + 16],
                                         VE[:, bdw + c:bdw + c + 1], ALU.mult, ALU.add))
            for tap in [j for j in range(31) if j != 15]:
                off = tap - 15
                a, b = max(0, -off), min(T, T - off)
                for c in range(4):
                    acc = st(y[:, 4 + c, :])[:, :, a:b]
                    own.wait(3)
                    own.mark(V.scalar_tensor_tensor(acc, st(uc[:, c, :])[:, :, a + off:b + off],
                                                    VE[:, wdw + 31 * c + tap:wdw + 31 * c + tap + 1], acc,
                                                    ALU.mult, ALU.add))
            own.wait()
            dve.sem_inc(sem("cv_conv"), 1)
            dve.wait_ge(sem("rcount_in"), 16)
            evacuated(dve, tiles_ + 12)
            for g in range(4):
                own.mark(V.tensor_copy(y[:, g, :], up[:, g, :]))
            for off in [o_ for h in range(8) for o_ in (-1 - h, h + 1)][:15]:
                groups = [g for g in range(4) if -(1 << g) <= off < (1 << g)]
                for g in groups:
                    a, b = max(0, -off), min(T, T - off)
                    acc = st(y[:, g, :])[:, :, a:b]
                    own.wait(len(groups) - 1)
                    own.mark(add(acc, acc, st(up[:, g, :])[:, :, a + off:b + off]))
            own.wait()
            rc = RCNT[:].rearrange("p (g t) -> p g t", g=4)
            for g in range(4):
                for s in range(S):
                    own.mark(mul(st(y[:, g, :])[:, s, :], st(y[:, g, :])[:, s, :], rc[:, g, :]))
            own.wait()
            sub(y[:, 0:4, :], y[:, 0:4, :], up).then_inc(sem("cv_pool"), 1)
            dve.wait_ge(sem("cv_sum"), l + 1)
            for c in range(4):
                last = V.scalar_tensor_tensor(y[:, 4 + c, :], AUX[0][:, 0:w], -1.0 / 512, y[:, 4 + c, :], ALU.mult, ALU.add)
            last.then_inc(sem("cv_cen"), 1)
            evacuated(dve, tiles_ + 20)
            for g in range(4):
                dve.wait_ge(sem("cv_poolmm") if g < 3 else halves_done, 3 * l + g + 1 if g < 3 else 2 * U_SMALL[l] + 2)
                V.scalar_tensor_tensor(y[:, 8 + g, :], AUX[2 + g % 2][:, 0:w], vec("pool_scale", 4 * l + g), y[:, 8 + g, :],
                                       ALU.mult, ALU.mult).then_inc(sem("cv_pooled"), 1)
            dve.wait_ge(sem("cv_std"), l + 1)
            seq(V.reciprocal(up[:, 1, :], up[:, 0, :]))
            for c in range(4):
                last = mul(y[:, 4 + c, :], y[:, 4 + c, :], up[:, 1, :])
            last.then_inc(sem("cv_nrm"), 1)
            for n in range(4):
                dve.wait_ge(sem("cv_pwmm") if n < 3 else halves_done, 3 * l + n + 1 if n < 3 else 2 * U_SMALL[l] + 4)
                mul(y[:, 12 + n, :], AUX[n % 2][:, 0:w], y[:, 12 + n, :]).then_inc(sem("cv_pw"), 1)

        def modulate2(p, i, first, end):
            for q in range(first, end):
                n = M2_TURN[p]
                dve.wait_ge(sem(f"mod_in{q % 3}"), 16 * (12 + M2[p] // 3 + q // 3 + 1) + 16 * n // 3 * i)
                w = MODW2[p][q % 3]
                V.scalar_tensor_tensor(w, w, 1.0, COND2, ALU.mult, ALU.mult,
                                       accum_out=MODF[:, ds(3 * (96 + M2[p] + q) + 2 + 3 * n * i, 1)]) \
                    .then_inc(sem("mod_used"), 1)

        def attention(l):
            w, q, k, v, up, uc, y = views(l)
            nm, jobs = f"at{l}", JOBS[l]
            J = len(jobs)
            QS, KS, VS, VT, PP, AA, AT, OC, TR, SD = att_views(l)
            evacuated(dve, T_IN[l] + 52)
            cos, sin = COS, SIN
            with dve.Fori(0, 4) as i:
                own.loop(i, 2 * 4 + 2 * J * 3 + 2 * 4)
                for e in range(2):
                    h = 2 * i + e
                    dve.wait_ge(sem(nm + "_pv"), 1 + 2 * J * i)
                    qx, kx = QS[e][:, w - T:w], KS[e][:, T:T2]
                    own.mark(mul(qx, tile(q, h)[:, w - T:w], cos))
                    own.mark(mul(kx, tile(k, h)[:, T:T2], cos))
                    dve.wait_ge(sem(nm + "_rot"), h + 1)
                    for r in range(2):
                        own.mark(mul(TR[:, T * r:T * (r + 1)], BANK[4][:, T * r:T * (r + 1)], sin))
                    own.wait()
                    add(qx, qx, TR[:, 0:T])
                    add(kx, kx, TR[:, T:T2]).then_inc(sem(nm + "_qk"), 1)
                    dve.wait_ge(sem(nm + "_qk"), h + 1)

                def maxima(g):
                    b, nk = g % 2, jobs[g % J][1]
                    dve.wait_ge(sem(nm + "_sc"), 2 * J * i + g + 1)
                    for c in range(2):
                        last = V.reduce_max(MX[:, 2 * b + c:2 * b + c + 1], BANK[2 * b + c][:, 0:nk], AX)
                    seq(last)
                    V.tensor_scalar(NB[:, 2 * b:2 * b + 2], MX[:, 2 * b:2 * b + 2], -0.125, None, ALU.mult) \
                        .then_inc(sem(nm + "_nb"), 1)

                def head(e):
                    dve.wait_ge(sem(nm + "_rr"), 2 * i + e + 1)
                    ms, r0 = SS[:, 0:J], RR[:, 0:J]
                    seq(V.tensor_scalar(ms, ms, 1.0 / P, EPS, ALU.mult, ALU.add))
                    seq(mul(RR[:, 4:4 + J], r0, r0))
                    seq(mul(RR[:, 4:4 + J], RR[:, 4:4 + J], ms))
                    own.mark(V.tensor_scalar(RR[:, 4:4 + J], RR[:, 4:4 + J], -0.5, 1.5, ALU.mult, ALU.add))
                    own.wait()
                    mul(r0, r0, RR[:, 4:4 + J]).then_inc(sem(nm + "_r1"), 1)
                    dve.wait_ge(sem(nm + "_r1"), 2 * i + e + 1)
                    dve.wait_ge(sem(nm + "_oc"), 1 + 2 * i + e + 1)
                    oc = OC[:, 0:P * J].rearrange("p (j t) -> p j t", j=J)
                    mul(oc, oc, r0.unsqueeze(2).broadcast_to([P, J, P])).then_inc(sem(nm + "_on"), 1)

                def gated(e):
                    dve.wait_ge(sem(nm + "_ot"), 1 + 2 * i + e + 1)
                    yt = tile(y, 2 * i + e)
                    V.scalar_tensor_tensor(yt, BANK[5][:, 0:P * J], SG[:, l:l + 1], yt, ALU.mult, ALU.mult) \
                        .then_inc(sem(nm + "_y"), 1)

                maxima(0)
                maxima(1)
                for g in range(2 * J):
                    b, nk = g % 2, jobs[g % J][1]
                    dve.wait_ge(sem(nm + "_exp"), 2 * J * i + g + 1)
                    seq(V.reciprocal(RC[:, 2 * b:2 * b + 2], SM[:, 2 * b:2 * b + 2]))
                    p0, p1 = PP[b][0][:, 0:nk], PP[b][1][:, 0:nk]
                    seq(V.tensor_scalar(p1, p1, RC[:, 2 * b + 1:2 * b + 2], LAM[:, l:l + 1], ALU.mult, ALU.mult))
                    V.scalar_tensor_tensor(AA[b][:, 0:nk], p0, RC[:, 2 * b:2 * b + 1], p1, ALU.mult, ALU.add) \
                        .then_inc(sem(nm + "_comb"), 1)
                    if g + 2 < 2 * J:
                        dve.wait_ge(sem(nm + "_comb"), 2 * J * i + g + 1)
                        maxima(g + 2)
                    if g == J + 1:
                        head(0)
                        gated(0)
                head(1)
                gated(1)
            own.end(4)

        dve.wait_ge(sem("vec_in"), 16)
        for n in [f"at{l}_{m}" for l in range(2) for m in ("y", "on")] + ["ssm_read", "ssm_y", "a2_vv", "a2_qk", "a2_yl"]:
            dve.sem_inc(sem(n), 1)
        V.memset(MODF[:], 0.0).then_inc(sem("mod_zero"), 1)
        dve.sem_inc(sem("n_hl"), 2)
        lamv = vec("lam", 0, 8)[0:64, :].rearrange("p (n c) -> p n c", c=2)
        mul(LAM[0:64, 0:4], lamv[:, :, 0], lamv[:, :, 1]).then_inc(sem("lam_prod"), 1)
        for l in range(2):
            last = V.tensor_scalar(SG[:, l:l + 1], vec("subln_g", l), 1.0 - LAM_INIT[l], None, ALU.mult)
        own.mark(last)
        own.wait()
        dve.wait_ge(sem("mod_zero"), 1)
        dve.wait_ge(sem("s_ready"), 1)
        dve.sem_inc(sem("mod_used"), 1)

        with dve.Fori(0, 12) as i:
            for s in range(8):
                dve.wait_ge(sem(f"mod_in{s}"), 16 * i + 16)
                for c in (1, 0) if s not in MOD_POOL else (0,):
                    over = c == 0 and s not in MOD_POOL
                    if not over:
                        dve.wait_ge(sem("mod_used"), 1 + 8 * i + s)
                    last = V.scalar_tensor_tensor(MODW[:, s, :] if over else JUNK, MODW[:, s, :], 1.0,
                                                  COND[:, D * c:D * (c + 1)], ALU.mult, ALU.mult,
                                                  accum_out=MODF[:, ds(24 * i + 3 * s + c, 1)])
                last.then_inc(sem("mod_used"), 1)
        dve.wait_ge(sem("mod_used"), USED1)
        dve.wait_ge(sem("mod_sum"), 2 + 12 * len(MOD_POOL))
        own.wait()
        V.tensor_tensor(MOD[:, 0:96, :], MOD[:, 0:96, :], vec("b_mod", 0, 96).unsqueeze(2).broadcast_to([P, 96, 3]),
                        ALU.add).then_inc(sem("mod_out"), 1)
        dve.wait_ge(sem("mod_out"), 1)
        dve.wait_ge(sem("x_in"), 16)
        norm("in0", src_in0, T2, [(16, 1), (16, 0)], "norm_g", 0)
        dve.wait_ge(sem("lam_exp"), 1)
        for l in range(2):
            own.mark(V.scalar_tensor_tensor(LAM[:, l:l + 1], LAM[:, 5 + 2 * l:6 + 2 * l], -LAM_INIT[l],
                                            LAM[:, 4 + 2 * l:5 + 2 * l], ALU.add, ALU.subtract))
        dve.wait_ge(sem("const_in"), 16)
        for l in range(2):
            w, q, k, v, up, uc, y = views(l)
            if l == 1:
                norm("in1", src_in1, T2, [(64, 1), (64, 0)], "norm_g", KT)
            dve.wait_ge(sem("s_ready"), l + 2)
            with dve.Fori(0, 8) as i:
                modulate2(l, i, 0, M2_TURN[l])
            small(l)
            attention(l)
            for c in range(4):
                dve.wait_ge(sem(f"ys{l}_hi"), c + 1)
                r = (slice(None), slice(4 * c, 4 * c + 4), slice(T2 - w, T2))
                sub(HL[r], y[:, 4 * c:4 * c + 4, :], HH[r]).then_inc(sem(f"ys{l}_lo"), 1)
            if l == 0:
                dve.wait_ge(sem("x_in"), 32)
            with dve.Fori(0, 4) as i:
                for s in range(4):
                    n = 4 * i + s
                    dve.wait_ge(halves_done, 2 * U_OUT[l] + 2 * n + 2)
                    if l == 0:
                        V.scalar_tensor_tensor(tile(CT0, n), L[s][:, 0:T], MODF[:, ds(3 * n + 3 * 32 + 1, 1)],
                                               tile(XIN, n)[:, 0:T], ALU.mult, ALU.add)
                        V.scalar_tensor_tensor(tile(RES, n), L[s][:, T:T2], MODF[:, ds(3 * n + 3 * 32, 1)],
                                               tile(XIN, n)[:, T:T2], ALU.mult, ALU.add).then_inc(bank_free[s], 1)
                    else:
                        V.scalar_tensor_tensor(tile(RES, n), L[s][:, 0:T], MODF[:, ds(3 * n + 3 * 80, 1)],
                                               tile(RES, n), ALU.mult, ALU.add).then_inc(bank_free[s], 1)
                        if s == 0:
                            dve.wait_ge(sem("s_ready"), 4)
                        modulate2(2, 2 * i + s // 2, *((0, 2) if s % 2 == 0 else (2, 3)))
            if l == 1:
                dve.wait_ge(sem("mod_used"), USED1 + M2[3])
                V.tensor_tensor(MOD[:, 96:192, 2], MOD[:, 96:192, 2], vec("b_mod", 96, 96), ALU.add) \
                    .then_inc(sem("mod_out"), 1)
            evacuated(dve, T_OUT[l] + 16)
            dve.sem_inc(sem(f"res{l + 1}"), 16)
        norm("fin", src_res, T, final=True)
        dve.wait_ge(sem("mod_out"), 2)
        dve.wait_ge(sem("n_hf"), 16 * N_AT["fin"] + 2 + KT)
        norm("b1", src_res, T, [(112, 2)], "norm1_g", 0)

        C1, C2, C3 = 6.28125, 1.93500518798828125e-3, 3.0199159819567e-07
        MAGIC = 12582912.0

        def reduce_angle(a, r):
            seq(V.tensor_scalar(r, a, 1 / (2 * math.pi), MAGIC, ALU.mult, ALU.add))
            seq(V.tensor_scalar(r, r, -MAGIC, None, ALU.add))
            for c in (C1, C2, C3):
                seq(V.scalar_tensor_tensor(a, r, -c, a, ALU.mult, ALU.add))
            seq(V.tensor_scalar(a, a, 3.1415925, -3.1415925, ALU.min, ALU.max))

        ang, tmp = NT_[:, 0, 0:T], NT_[:, 2, 0:T]
        dve.wait_ge(sem("pos_in"), 16)
        seq(V.tensor_copy(ang, POSI))
        seq(V.tensor_scalar(ang, ang, vec("inv_freq"), None, ALU.mult))
        reduce_angle(ang, tmp)
        own.mark(V.tensor_copy(tmp, ang))
        own.wait()
        dve.sem_inc(sem("ang"), 1)

        par = CTAB.rearrange("p (n g) -> p n g", g=64)
        stab = STAB.rearrange("p (n g) -> p n g", g=64)
        th, sn, cs, sh, _, dt, x, e1 = (par[:, n, :] for n in range(8))
        ta, tb, tc, den, nr, ni, cr, ci = (stab[:, n, :] for n in range(8))
        bits = par[:, 8, :].bitcast(i32)
        coef = COEF.rearrange("p (n g) -> p n g", g=64)
        CA, CB, CE, CF, TURN, MAG = (coef[:, n, :] for n in range(6))
        seq(V.tensor_scalar(dt, vec("log_dt", 0, 64), 88.0, -89.0, ALU.min, ALU.max))
        seq(V.tensor_scalar(ta, dt, 1 / math.log(2), MAGIC, ALU.mult, ALU.add))
        seq(V.tensor_scalar(ta, ta, -MAGIC, -127.0, ALU.add, ALU.max))
        seq(V.scalar_tensor_tensor(dt, ta, -0.693359375, dt, ALU.mult, ALU.add))
        seq(V.scalar_tensor_tensor(dt, ta, 2.12194440e-4, dt, ALU.mult, ALU.add))
        seq(V.tensor_scalar(bits, ta, 127.0, 8388608.0, ALU.add, ALU.mult))
        seq(V.tensor_scalar(tb, dt, 1 / 5040, 1 / 720, ALU.mult, ALU.add))
        for c in (1 / 120, 1 / 24, 1 / 6, 0.5, 1.0, 1.0):
            seq(mul(tb, tb, dt))
            seq(V.tensor_scalar(tb, tb, c, None, ALU.add))
        seq(mul(dt, tb, par[:, 8, :]))
        seq(mul(x, vec("lam_re", 0, 64), dt))
        seq(V.tensor_scalar(x, x, 40.0, -40.0, ALU.min, ALU.max))
        seq(V.tensor_scalar(x, x, 1 / 64, None, ALU.mult))
        seq(V.tensor_scalar(e1, x, 1 / 40320, 1 / 5040, ALU.mult, ALU.add))
        for c in (1 / 720, 1 / 120, 1 / 24, 1 / 6, 0.5, 1.0):
            seq(mul(e1, e1, x))
            seq(V.tensor_scalar(e1, e1, c, None, ALU.add))
        seq(mul(e1, e1, x))
        for _ in range(6):
            seq(V.scalar_tensor_tensor(e1, e1, 2.0, e1, ALU.add, ALU.mult))
        seq(V.tensor_scalar(MAG, e1, 1.0, None, ALU.add))
        seq(mul(th, vec("lam_im", 0, 64), dt))
        reduce_angle(th, ta)
        seq(V.tensor_scalar(TURN, th, 1 / (2 * math.pi), None, ALU.mult))
        dve.sem_inc(sem("th"), 1)
        dve.wait_ge(sem("trig"), 1)
        seq(mul(nr, e1, cs))
        seq(mul(ta, sh, sh))
        seq(V.scalar_tensor_tensor(nr, ta, -2.0, nr, ALU.mult, ALU.add))
        seq(mul(ni, MAG, sn))
        lr, li = vec("lam_re", 0, 64), vec("lam_im", 0, 64)
        seq(mul(den, lr, lr))
        seq(mul(ta, li, li))
        seq(add(den, den, ta))
        seq(V.reciprocal(den, den))
        seq(mul(cr, nr, lr))
        seq(mul(ta, ni, li))
        seq(add(cr, cr, ta))
        seq(mul(cr, cr, den))
        seq(mul(ci, ni, lr))
        seq(mul(ta, nr, li))
        seq(sub(ci, ci, ta))
        seq(mul(ci, ci, den))
        m0, m1 = vec("half0"), vec("half1")
        seq(V.tensor_scalar(ta, ci, m1, None, ALU.mult))
        seq(V.scalar_tensor_tensor(CA, cr, m0, ta, ALU.mult, ALU.subtract))
        seq(V.tensor_scalar(CF, cr, m0, -1.0, ALU.mult, ALU.mult))
        seq(sub(CF, CF, ta))
        seq(V.tensor_scalar(tb, cr, m1, None, ALU.mult))
        seq(V.tensor_scalar(tc, ci, m0, -1.0, ALU.mult, ALU.mult))
        seq(sub(CB, tc, tb))
        seq(add(CE, tc, tb))
        seq(V.memset(WPAD, 0.0))

        wpad = [WPAD[:, 1024 * n:1024 * n + 1152].rearrange("p (g x) -> p g x", x=144)[:, :, 0:16] for n in range(2)]
        cst = CST.rearrange("p (c g h) -> p c g h", c=2, h=16)
        t12 = [T12[:, P * n:P * (n + 1)].rearrange("p (g h) -> p g h", h=16) for n in range(2)]

        def lay_c(j):
            dve.wait_ge(sem("c_in"), 16 * j + 16)
            dve.wait_ge(sem("ssm_c"), 1 + 4 * j)
            for n, (c0, c1) in enumerate(((CA, CB), (CE, CF))):
                for m, c in enumerate((c0, c1)):
                    own.mark(mul(t12[m], cst[:, m], c[:, ds(8 * j, 8)].unsqueeze(2).broadcast_to([P, 8, 16])))
                own.wait()
                last = add(wpad[n], t12[0], t12[1])
                if n == 0:
                    seq(last)
            last.then_inc(sem("ssm_w"), 1)

        ph3, rn3 = (r.rearrange("p (g t) -> p g t", g=2) for r in (PH, RN))
        steps3 = STEPS.unsqueeze(1).broadcast_to([P, 2, T])

        def phase(q, g):
            dve.wait_ge(sem("tables"), 1 + q)
            seq(mul(ph3, TURN[:, ds(g, 2)].unsqueeze(2).broadcast_to([P, 2, T]), steps3))
            seq(V.tensor_scalar(RN, PH, MAGIC, -MAGIC, ALU.add, ALU.add))
            sub(PH, PH, RN).then_inc(sem("phase"), 1)
            dve.wait_ge(sem("phase"), q + 1)

        def scan(j, a):
            q = 4 * j + a
            sl = slice(512 * (a % 2), 512 * (a % 2) + 512)
            dve.wait_ge(sem("ssm_b"), 1 + q + 1)
            dve.wait_ge(sem("tables"), 1 + q + 1)
            dve.wait_ge(sem("ssm_c"), 1 + q)
            own.mark(mul(SW, AUX[0][:, 0:T2], CTAB[:, sl]))
            mul(STM, AUX[1][:, 0:T2], STAB[:, sl]).then_inc(sem("ssm_read"), 1)
            dve.wait_ge(sem("ssm_read"), 1 + q + 1)
            own.wait()
            seq(add(SW, SW, STM))
            for r in range(2):
                part = SW[:, T * r:T * (r + 1)]
                own.mark(V.tensor_tensor_scan(part, MAG[:, ds(8 * j + 2 * a + r, 1)].broadcast_to([P, T]), part, 0.0,
                                              ALU.mult, ALU.add))
            own.wait()
            seq(mul(STM, SW, CTAB[:, sl]))
            mul(SW, SW, STAB[:, sl]).then_inc(sem("ssm_x"), 1)

        def finish(j):
            dve.wait_ge(sem("ssm_c"), 1 + 4 * j + 4)
            V.scalar_tensor_tensor(tile(U2, j), tile(U2, j), vec_at("d_skip", j), AUX[2][:, 0:T], ALU.mult, ALU.add) \
                .then_inc(sem("ssm_y"), 1)

        dve.wait_ge(sem("steps_in"), 16)
        evacuated(dve, T_IN2 + 8)
        phase(0, 0)
        with dve.Fori(0, 7) as j:
            own.loop(j, 5 + 4 * 7)
            lay_c(j)
            for a in range(4):
                phase(4 * j + a + 1, 8 * j + 2 * a + 2)
                scan(j, a)
            finish(j)
        own.end(7)
        lay_c(7)
        for a in range(4):
            if a < 3:
                phase(28 + a + 1, 56 + 2 * a + 2)
            scan(7, a)
        finish(7)

        dve.wait_ge(sem("ssm_y"), 1 + 8)
        G = R2[:, 0:2048]
        seq(mul(US8, G, G))
        seq(V.tensor_scalar(US8, US8, 0.044715, 1.0, ALU.mult, ALU.add))
        mul(US8, US8, G).then_inc(sem("gelu_in"), 1)
        dve.wait_ge(sem("gelu_sig"), 1)
        mul(G, G, US8).then_inc(sem("gelu_g"), 1)

        v = att2_views()
        dve.wait_ge(sem("rope_cos"), 1)
        evacuated(dve, T_IN2 + 32)
        with dve.Fori(0, 4) as i:
            own.loop(i, 2 * 7 + 4)
            for e in range(2):
                h = 2 * i + e
                dve.wait_ge(sem("a2_ssum"), 1 + h + 1)
                V.tensor_scalar(v["VV"], BANK[5][:, 0:T2], 1.0 / P, EPS, ALU.mult, ALU.add).then_inc(sem("a2_vv"), 1)
                dve.wait_ge(sem("a2_r0"), h + 1)
                dve.wait_ge(sem("a2_vv"), 1 + h + 1)
                r0, tt = v["R0"], v["TT"]
                seq(mul(tt, r0, r0))
                seq(mul(tt, tt, v["VV"]))
                seq(V.tensor_scalar(tt, tt, -0.5, 1.5, ALU.mult, ALU.add))
                seq(mul(tt, tt, r0))
                V.scalar_tensor_tensor(v["QN"][:, 0:T], tile(Q2, h), vec("q_g"), tt[:, 0:T], ALU.mult, ALU.mult)
                V.scalar_tensor_tensor(v["QN"][:, T:T2], tile(K2, h), vec("k_g"), tt[:, T:T2], ALU.mult, ALU.mult) \
                    .then_inc(sem("a2_qn"), 1)
                dve.wait_ge(sem("a2_qn"), h + 1)
                dve.wait_ge(sem("a2_pv"), 1 + 4 * i)
                own.mark(mul(v["QS"][e], v["QN"][:, 0:T], COS))
                own.mark(mul(v["KS"][e], v["QN"][:, T:T2], COS))
                dve.wait_ge(sem("a2_rot"), h + 1)
                mul(tt[:, 0:T], BANK[4][:, 0:T], SIN)
                own.mark(mul(tt[:, T:T2], BANK[4][:, T:T2], SIN))
                own.wait()
                add(v["QS"][e], v["QS"][e], tt[:, 0:T])
                add(v["KS"][e], v["KS"][e], tt[:, T:T2]).then_inc(sem("a2_qk"), 1)
                dve.wait_ge(sem("a2_qk"), 1 + h + 1)

            def scores2(g):
                b, nk = g % 2, JOBS2[g % 2][1]
                dve.wait_ge(sem("a2_sc"), 4 * i + g + 1)
                ss, sc = v["SS_"][b], SC2[b]
                if nk > P:
                    V.tensor_scalar(ss[:, 0:nk - P], sc[:, 0:nk - P], P ** -0.5, None, ALU.mult)
                V.scalar_tensor_tensor(ss[:, nk - P:nk], sc[:, nk - P:nk], P ** -0.5, MASK, ALU.mult, ALU.add) \
                    .then_inc(sem("a2_ms"), 1)
                dve.wait_ge(sem("a2_ms"), 4 * i + g + 1)
                seq(V.reduce_max(MX[:, b:b + 1], ss[:, 0:nk], AX))
                V.tensor_scalar(NB[:, b:b + 1], MX[:, b:b + 1], -1.0, None, ALU.mult).then_inc(sem("a2_nb"), 1)

            scores2(0)
            scores2(1)
            for g in range(4):
                b, nk = g % 2, JOBS2[g % 2][1]
                dve.wait_ge(sem("a2_exp"), 4 * i + g + 1)
                V.reciprocal(RC[:, b:b + 1], SM[:, b:b + 1]).then_inc(sem("a2_rc"), 1)
                dve.wait_ge(sem("a2_rc"), 4 * i + g + 1)
                V.tensor_scalar(v["PP"][b][:, 0:nk], v["PP"][b][:, 0:nk], RC[:, b:b + 1], None, ALU.mult) \
                    .then_inc(sem("a2_comb"), 1)
                if g + 2 < 4:
                    scores2(g + 2)
                if g % 2 == 1:
                    n = 2 * i + g // 2
                    dve.wait_ge(sem("a2_yh"), n + 1)
                    sub(tile(YAL, n), BANK[4][:, 0:T], tile(YAH, n)).then_inc(sem("a2_yl"), 1)
        own.end(4)

        dve.wait_ge(sem("gelu_hi"), 1)
        sub(GSL[:], U2, GSH[:]).then_inc(sem("gelu_lo"), 1)
        evacuated(dve, T_GLU + 8)
        for c in range(4):
            r = (slice(None), slice(2 * c, 2 * c + 2), slice(None))
            mul(V2[r], V2[r], U2[r]).then_inc(sem("ys_mul"), 1)
        for c in range(4):
            r = (slice(None), slice(2 * c, 2 * c + 2), slice(None))
            dve.wait_ge(sem("ys_hi"), c + 1)
            sub(YSL[r], V2[r], YSH[r]).then_inc(sem("ys_lo"), 1)
        with dve.Fori(0, 4) as i:
            for s in range(4):
                n = 4 * i + s
                dve.wait_ge(halves_done, 2 * U_ABR + n + 1)
                mul(tile(GATE_A, n), L[s][:, 0:T], tile(GATE_A, n)).then_inc(bank_free[s], 1)
        evacuated(dve, T_ABR + 16)
        with dve.Fori(0, 4) as i:
            for s in range(4):
                n = 4 * i + s
                dve.wait_ge(halves_done, 2 * U_SBR + n + 1)
                mul(tile(GATE_S, n), L[s][:, 0:T], tile(GATE_S, n)).then_inc(bank_free[s], 1)
                dve.wait_ge(bank_free[s], 1 + T_SBR // 4 + i + 1)
                add(tile(GATE_A, n), tile(GATE_A, n), tile(GATE_S, n)).then_inc(sem("m_sum"), 1)
        with dve.Fori(0, KT) as k:
            dve.wait_ge(sem("m_hi"), k + 1)
            sub(tile(ML, k), tile(GATE_A, k), tile(MH, k)).then_inc(sem("m_lo"), 1)
        with dve.Fori(0, 4) as i:
            for s in range(4):
                n = 4 * i + s
                dve.wait_ge(halves_done, 2 * U_OUT2 + 2 * n + 2)
                V.scalar_tensor_tensor(tile(RES, n), L[s][:, 0:T], MODF[:, ds(3 * n + 3 * 128 + 2, 1)], tile(RES, n),
                                       ALU.mult, ALU.add).then_inc(bank_free[s], 1)
        evacuated(dve, T_OUT2 + 16)
        dve.sem_inc(sem("res3"), 16)

        norm("b2", src_res, T, [(160, 2)], "norm2_g", 0)
        with dve.Fori(0, FFN // 2) as i:
            own.loop(i, 4)
            for r in range(4):
                m, half = r // 2, r % 2
                n = 4 * i + r
                acc = FT[:, 2 * m + half, :]
                dve.wait_ge(sem("ffn_mid"), n + 1)
                seq(V.scalar_tensor_tensor(acc[:, 1:T], L[r][:, 0:T - 1], vec_at("conv_w", 3 * n + 1), acc[:, 1:T],
                                           ALU.mult, ALU.add))
                V.scalar_tensor_tensor(acc[:, 2:T], L[r][:, 0:T - 2], vec_at("conv_w", 3 * n), acc[:, 2:T],
                                       ALU.mult, ALU.add).then_inc(bank_free[r], 1)
                if half == 1:
                    for b in (r - 1, r):
                        dve.wait_ge(bank_free[b], 1 + T_UP // 4 + i + 1)
                    dve.sem_inc(sem("ffn_conv"), 2)
                    dve.wait_ge(sem("ffn_silu"), 2 * i + m + 1)
                    mul(FT[:, 4 + m, :], FT[:, 2 * m, :], FT[:, 2 * m + 1, :]).then_inc(sem("ffn_prod"), 1)
                    dve.wait_ge(sem("ffn_hi"), 2 * i + m + 1)
                    sub(tile(FL, 2 * i + m), FT[:, 4 + m, :], tile(FH, 2 * i + m)).then_inc(sem("ffn_lo"), 1)
        own.end(FFN // 2)
        with dve.Fori(0, 8) as i:
            for s in range(2):
                n = 2 * i + s
                dve.wait_ge(halves_done, 2 * U_DOWN + 6 * n + 6)
                V.scalar_tensor_tensor(tile(RES, n), L[s][:, 0:T], MODF[:, ds(3 * n + 3 * 176 + 2, 1)], tile(RES, n),
                                       ALU.mult, ALU.add).then_inc(bank_free[s], 1)
    ctx.close()


def kernel(**inputs):
    import concourse.bacc as bacc
    from concourse.bass_utils import run_bass_kernel_spmd

    a = {name: np.asarray(v) for name, v in inputs.items()}
    laid = lay_out(a)
    nc = bacc.Bacc("TRN2", target_bir_lowering=False, num_devices=1)
    arrays, dram = {}, {}
    for name in ARRAYS:
        v = np.ascontiguousarray(laid[name])
        arrays[f"in_{name}"] = v
        dram[name] = nc.dram_tensor(f"in_{name}", v.shape, mybir.dt.from_np(v.dtype), kind="ExternalInput").ap()
    out = nc.dram_tensor("out_y", (P, KT, T), mybir.dt.float32, kind="ExternalOutput").ap()
    build(nc, dram, out)
    r = run_bass_kernel_spmd(nc, [arrays], core_ids=[0])
    y = r.results[0]["out_y"]
    return y.transpose(1, 0, 2).reshape(D, T).T.reshape(1, T, D)
```
